# Optimizing a Trainium2 kernel written in Bass

```python
import math
import jax, jax.numpy as jnp
from jax import lax
import numpy as np

D_MODEL = 1024
BATCH = 1
SEQ = 128
DEPTH = 4
DEC_BATCH = 1
DEC_SEQ = 256
PAST_LEN = 128

GRID_W = 64
N_MIXERS = 4
N_LAYERS_POOL = (DEPTH + 3) // 4
N_LAYERS_SSD = (DEPTH + 2) // 4
N_LAYERS_CONV = (DEPTH + 1) // 4
N_LAYERS_ATTN = DEPTH // 4
N_MOD = 6
EPS = 1e-6

POOL_WINDOWS = (2, 4, 8, 16)
POOL_GROUP = D_MODEL // len(POOL_WINDOWS)

SSD_D_INNER = 2 * D_MODEL
SSD_HEAD_DIM = 64
SSD_HEADS = SSD_D_INNER // SSD_HEAD_DIM
SSD_GROUPS = 8
SSD_STATE = 128
SSD_CONV = 3
SSD_CHUNK = 128
SSD_GN = SSD_GROUPS * SSD_STATE
SSD_CONV_DIM = SSD_D_INNER + 2 * SSD_GN
SSD_IN_DIM = SSD_D_INNER + SSD_CONV_DIM + 2 * SSD_HEADS

CONF_KERNEL = 31

ATTN_HEADS = 8
ATTN_KV_HEADS = 2
ATTN_HEAD_DIM = 128
ROPE_THETA = 10000.0
Q_BLOCK = 128

FFN_DIM = 2816
FFN_CONV = 3

kernel_name = 'hybrid_diffusion_prefix_trunk_step'

def rms_norm(x, g):
    xf = x.astype(jnp.float32)
    y = xf * lax.rsqrt(jnp.mean(xf * xf, axis=-1, keepdims=True) + EPS)
    return (y * g.astype(jnp.float32)).astype(x.dtype)

def layer_norm(x, g, b):
    xf = x.astype(jnp.float32)
    mu = jnp.mean(xf, axis=-1, keepdims=True)
    var = jnp.mean(jnp.square(xf - mu), axis=-1, keepdims=True)
    y = (xf - mu) * lax.rsqrt(var + EPS)
    return (y * g.astype(jnp.float32) + b.astype(jnp.float32)).astype(x.dtype)

def depthwise_conv(x, w, b):
    k = w.shape[0]
    left = (k - 1) // 2
    y = lax.conv_general_dilated(
        x, w.astype(x.dtype)[:, None, :], window_strides=(1,),
        padding=[(left, k - 1 - left)],
        dimension_numbers=('NWC', 'WIO', 'NWC'),
        feature_group_count=x.shape[-1])
    return y + b.astype(x.dtype)

def modulation(cond, w, b):
    m = jax.nn.silu(cond) @ w + b
    return m.reshape(m.shape[:-1] + (N_MOD, D_MODEL))

def modulate_in(x, mod, k, g):
    return rms_norm(x, g) * (1.0 + mod[:, None, 3 * k + 1]) + mod[:, None, 3 * k]

def gated_residual(x, out, mod, k, g):
    return x + mod[:, None, 3 * k + 2] * rms_norm(out, g)

def pool_mixer(h, w, scale):
    seq_len = h.shape[1]
    hf = h.astype(jnp.float32)
    cs = jnp.concatenate([jnp.zeros_like(hf[:, :1]), jnp.cumsum(hf, axis=1)], axis=1)
    t = jnp.arange(seq_len)
    outs = []
    for gi, win in enumerate(POOL_WINDOWS):
        sl = slice(gi * POOL_GROUP, (gi + 1) * POOL_GROUP)
        lo = jnp.clip(t - win // 2, 0, seq_len)
        hi = jnp.clip(t + win - win // 2, 0, seq_len)
        csg = cs[..., sl]
        mean = (csg[:, hi] - csg[:, lo]) / (hi - lo).astype(jnp.float32)[None, :, None]
        outs.append(mean - hf[..., sl])
    p = jnp.stack(outs, axis=2).astype(h.dtype)
    y = jnp.einsum('blgc,gcd->blgd', p, w).reshape(h.shape)
    return y * scale

def ssd_scan(x, dt, a, bm, cm, h0):
    bsz, seq_len = x.shape[:2]
    nc = seq_len // SSD_CHUNK
    r = SSD_HEADS // SSD_GROUPS
    xc = x.reshape(bsz, nc, SSD_CHUNK, SSD_GROUPS, r, SSD_HEAD_DIM)
    dtc = dt.reshape(bsz, nc, SSD_CHUNK, SSD_GROUPS, r)
    bc = bm.reshape(bsz, nc, SSD_CHUNK, SSD_GROUPS, SSD_STATE)
    cc = cm.reshape(bsz, nc, SSD_CHUNK, SSD_GROUPS, SSD_STATE)
    acs = jnp.cumsum(dtc * a.reshape(SSD_GROUPS, r), axis=2)
    pos = jnp.arange(SSD_CHUNK)
    lower = (pos[:, None] >= pos[None, :])[None, None, :, :, None, None]
    seg = acs[:, :, :, None] - acs[:, :, None, :]
    decay = jnp.exp(jnp.where(lower, seg, -jnp.inf))
    cb = jnp.einsum('bcign,bcjgn->bcijg', cc, bc)
    wts = cb[..., None] * decay * dtc[:, :, None]
    y_diag = jnp.einsum('bcijgr,bcjgrp->bcigrp', wts, xc)
    to_end = jnp.exp(acs[:, :, -1:] - acs) * dtc
    chunk_states = jnp.einsum('bcjgn,bcjgr,bcjgrp->bcgrpn', bc, to_end, xc)
    chunk_decay = jnp.exp(acs[:, :, -1])

    def step(hs, inp):
        s, dcy = inp
        return hs * dcy[..., None, None] + s, hs

    h_init = h0.astype(jnp.float32).reshape(bsz, SSD_GROUPS, r, SSD_HEAD_DIM, SSD_STATE)
    h_last, h_prev = lax.scan(step, h_init, (jnp.moveaxis(chunk_states, 1, 0),
                                             jnp.moveaxis(chunk_decay, 1, 0)))
    h_prev = jnp.moveaxis(h_prev, 0, 1)
    y_off = jnp.einsum('bcign,bcgrpn->bcigrp', cc, h_prev) * jnp.exp(acs)[..., None]
    y = (y_diag + y_off).reshape(bsz, seq_len, SSD_HEADS, SSD_HEAD_DIM)
    return y, h_last.reshape(bsz, SSD_HEADS, SSD_HEAD_DIM, SSD_STATE)

def ssd_mixer(h, h0, w_in, conv_w, conv_b, dt_bias, a_log, d_skip, norm_g, w_out):
    bsz, seq_len, _ = h.shape
    proj = h @ w_in
    z = proj[..., :SSD_D_INNER]
    xbc = jax.nn.silu(depthwise_conv(proj[..., SSD_D_INNER:SSD_D_INNER + SSD_CONV_DIM], conv_w, conv_b))
    dt_raw = proj[..., SSD_D_INNER + SSD_CONV_DIM:].reshape(bsz, seq_len, 2, SSD_HEADS).astype(jnp.float32)
    x = xbc[..., :SSD_D_INNER].reshape(bsz, seq_len, SSD_HEADS, SSD_HEAD_DIM).astype(jnp.float32)
    bm = xbc[..., SSD_D_INNER:SSD_D_INNER + SSD_GN].reshape(bsz, seq_len, SSD_GROUPS, SSD_STATE).astype(jnp.float32)
    cm = xbc[..., SSD_D_INNER + SSD_GN:].reshape(bsz, seq_len, SSD_GROUPS, SSD_STATE).astype(jnp.float32)
    dt = jax.nn.softplus(dt_raw + dt_bias.astype(jnp.float32))
    a = -jnp.exp(a_log.astype(jnp.float32))
    y_f, s_f = ssd_scan(x, dt[:, :, 0], a[0], bm, cm, h0[:, 0])
    flip = lambda t: jnp.flip(t, axis=1)
    y_b, s_b = ssd_scan(flip(x), flip(dt[:, :, 1]), a[1], flip(bm), flip(cm), h0[:, 1])
    skip = jnp.sum(d_skip.astype(jnp.float32), axis=0)[:, None]
    y = (y_f + flip(y_b) + x * skip).reshape(bsz, seq_len, SSD_D_INNER).astype(h.dtype)
    y = rms_norm(y * jax.nn.silu(z), norm_g)
    return y @ w_out, jnp.stack([s_f, s_b], axis=1)

def conformer_conv(h, w_in, b_in, dw, dw_b, ln_g, ln_b, w_out, b_out):
    u = h @ w_in + b_in
    u = u[..., :D_MODEL] * jax.nn.sigmoid(u[..., D_MODEL:])
    u = depthwise_conv(u, dw, dw_b)
    u = jax.nn.silu(layer_norm(u, ln_g, ln_b))
    return u @ w_out + b_out

def axial_rope_tables(seq_len):
    rows = seq_len // GRID_W
    row = jnp.repeat(jnp.arange(rows), GRID_W).astype(jnp.float32)
    col = jnp.tile(jnp.arange(GRID_W), rows).astype(jnp.float32)
    n_freq = ATTN_HEAD_DIM // 4
    inv = ROPE_THETA ** (-jnp.arange(n_freq, dtype=jnp.float32) / n_freq)
    ang = jnp.stack([row[:, None] * inv, col[:, None] * inv], axis=1)
    return jnp.cos(ang), jnp.sin(ang)

def axial_rope(x, cos, sin):
    n_freq = ATTN_HEAD_DIM // 4
    xs = x.astype(jnp.float32).reshape(x.shape[:-1] + (2, 2, n_freq))
    x1, x2 = xs[..., 0, :], xs[..., 1, :]
    cs, sn = cos[None, :, None], sin[None, :, None]
    out = jnp.stack([x1 * cs - x2 * sn, x2 * cs + x1 * sn], axis=-2)
    return out.reshape(x.shape).astype(x.dtype)

def attn_qkv(h, w_qkv, q_g, k_g):
    bsz, seq_len, _ = h.shape
    nq, nk = ATTN_HEADS * ATTN_HEAD_DIM, ATTN_KV_HEADS * ATTN_HEAD_DIM
    qkv = h @ w_qkv
    q = rms_norm(qkv[..., :nq].reshape(bsz, seq_len, ATTN_HEADS, ATTN_HEAD_DIM), q_g)
    k = rms_norm(qkv[..., nq:nq + nk].reshape(bsz, seq_len, ATTN_KV_HEADS, ATTN_HEAD_DIM), k_g)
    v = qkv[..., nq + nk:].reshape(bsz, seq_len, ATTN_KV_HEADS, ATTN_HEAD_DIM)
    return q, k, v

def block_attention(q, k, v):
    bsz, lq = q.shape[:2]
    nb = lq // Q_BLOCK
    r = ATTN_HEADS // ATTN_KV_HEADS
    qb = jnp.moveaxis(q.reshape(bsz, nb, Q_BLOCK, ATTN_KV_HEADS, r, ATTN_HEAD_DIM), 1, 0)
    scale = ATTN_HEAD_DIM ** -0.5

    def one_block(qblk):
        s = jnp.einsum('bqgrd,bkgd->bgrqk', qblk, k).astype(jnp.float32) * scale
        p = jax.nn.softmax(s, axis=-1).astype(v.dtype)
        return jnp.einsum('bgrqk,bkgd->bqgrd', p, v)

    o = lax.map(one_block, qb)
    return jnp.moveaxis(o, 0, 1).reshape(bsz, lq, ATTN_HEADS * ATTN_HEAD_DIM)

def attn_context(h, w_qkv, q_g, k_g, w_o):
    q, k, v = attn_qkv(h, w_qkv, q_g, k_g)
    return block_attention(q, k, v) @ w_o, k, v

def attn_latent(h, ctx_k, ctx_v, w_qkv, q_g, k_g, w_o):
    q, k, v = attn_qkv(h, w_qkv, q_g, k_g)
    cos, sin = axial_rope_tables(h.shape[1])
    q = axial_rope(q, cos, sin)
    k = axial_rope(k, cos, sin)
    k_all = jnp.concatenate([ctx_k.astype(k.dtype), k], axis=1)
    v_all = jnp.concatenate([ctx_v.astype(v.dtype), v], axis=1)
    return block_attention(q, k_all, v_all) @ w_o

def conv_ffn(h, w_in, dw, dw_b, w_out):
    u = depthwise_conv(h @ w_in, dw, dw_b)
    return (jax.nn.silu(u[..., :FFN_DIM]) * u[..., FFN_DIM:]) @ w_out

def ffn_sublayer(x, mod, g_pre, g_post, w_in, dw, dw_b, w_out):
    h = modulate_in(x, mod, 1, g_pre)
    return gated_residual(x, conv_ffn(h, w_in, dw, dw_b, w_out), mod, 1, g_post)

def _nrm(k, shape, scale):
    return jax.random.normal(k, shape, jnp.float32) * scale

def setup_inputs(seed: int = 0) -> dict:
    key = jax.random.key(seed)
    k = jax.random.split(key, 36)
    D = D_MODEL
    nq = (ATTN_HEADS + 2 * ATTN_KV_HEADS) * ATTN_HEAD_DIM
    dt0 = jnp.exp(jax.random.uniform(k[15], (N_LAYERS_SSD, 2, SSD_HEADS), jnp.float32,
                                     minval=math.log(1e-3), maxval=math.log(1e-1)))
    return {
        'x_prompt': _nrm(k[0], (BATCH, SEQ, D), 1.0),
        'x_sample': _nrm(k[1], (DEC_BATCH, DEC_SEQ, D), 1.0),
        'state_ssd': _nrm(k[2], (DEC_BATCH, N_LAYERS_SSD, 2, SSD_HEADS, SSD_HEAD_DIM, SSD_STATE), 0.5),
        'cache_k': _nrm(k[3], (DEC_BATCH, N_LAYERS_ATTN, PAST_LEN, ATTN_KV_HEADS, ATTN_HEAD_DIM), 1.0),
        'cache_v': _nrm(k[4], (DEC_BATCH, N_LAYERS_ATTN, PAST_LEN, ATTN_KV_HEADS, ATTN_HEAD_DIM), 1.0),
        'c': _nrm(k[5], (DEC_BATCH, D), 1.0),
        'c_ctx': _nrm(k[6], (D,), 1.0),
        'w_mod': _nrm(k[7], (DEPTH, D, N_MOD * D), 0.5 * D ** -0.5),
        'b_mod': _nrm(k[8], (DEPTH, N_MOD * D), 0.02),
        'norm_g': 1.0 + _nrm(k[9], (DEPTH, 4, D), 0.1),
        'pool_w': _nrm(k[10], (N_LAYERS_POOL, len(POOL_WINDOWS), POOL_GROUP, POOL_GROUP), POOL_GROUP ** -0.5),
        'pool_scale': 1.0 + _nrm(k[11], (N_LAYERS_POOL, D), 0.1),
        'ssd_w_in': _nrm(k[12], (N_LAYERS_SSD, D, SSD_IN_DIM), D ** -0.5),
        'ssd_conv_w': _nrm(k[13], (N_LAYERS_SSD, SSD_CONV, SSD_CONV_DIM), SSD_CONV ** -0.5),
        'ssd_conv_b': _nrm(k[14], (N_LAYERS_SSD, SSD_CONV_DIM), 0.02),
        'ssd_dt_bias': dt0 + jnp.log(-jnp.expm1(-dt0)),
        'ssd_a_log': jnp.log(jax.random.uniform(k[16], (N_LAYERS_SSD, 2, SSD_HEADS), jnp.float32, minval=1.0, maxval=16.0)),
        'ssd_d': 1.0 + _nrm(k[17], (N_LAYERS_SSD, 2, SSD_HEADS), 0.1),
        'ssd_norm_g': 1.0 + _nrm(k[18], (N_LAYERS_SSD, SSD_D_INNER), 0.1),
        'ssd_w_out': _nrm(k[19], (N_LAYERS_SSD, SSD_D_INNER, D), SSD_D_INNER ** -0.5),
        'conf_w_in': _nrm(k[20], (N_LAYERS_CONV, D, 2 * D), D ** -0.5),
        'conf_b_in': _nrm(k[21], (N_LAYERS_CONV, 2 * D), 0.02),
        'conf_dw': _nrm(k[22], (N_LAYERS_CONV, CONF_KERNEL, D), CONF_KERNEL ** -0.5),
        'conf_dw_b': _nrm(k[23], (N_LAYERS_CONV, D), 0.02),
        'conf_ln_g': 1.0 + _nrm(k[24], (N_LAYERS_CONV, D), 0.1),
        'conf_ln_b': _nrm(k[25], (N_LAYERS_CONV, D), 0.02),
        'conf_w_out': _nrm(k[26], (N_LAYERS_CONV, D, D), D ** -0.5),
        'conf_b_out': _nrm(k[27], (N_LAYERS_CONV, D), 0.02),
        'attn_w_qkv': _nrm(k[28], (N_LAYERS_ATTN, D, nq), D ** -0.5),
        'attn_q_g': 1.0 + _nrm(k[29], (N_LAYERS_ATTN, ATTN_HEAD_DIM), 0.1),
        'attn_k_g': 1.0 + _nrm(k[30], (N_LAYERS_ATTN, ATTN_HEAD_DIM), 0.1),
        'attn_w_o': _nrm(k[31], (N_LAYERS_ATTN, ATTN_HEADS * ATTN_HEAD_DIM, D), (ATTN_HEADS * ATTN_HEAD_DIM) ** -0.5),
        'ffn_w_in': _nrm(k[32], (DEPTH, D, 2 * FFN_DIM), D ** -0.5),
        'ffn_dw': _nrm(k[33], (DEPTH, FFN_CONV, 2 * FFN_DIM), FFN_CONV ** -0.5),
        'ffn_dw_b': _nrm(k[34], (DEPTH, 2 * FFN_DIM), 0.02),
        'ffn_w_out': _nrm(k[35], (DEPTH, FFN_DIM, D), FFN_DIM ** -0.5),
    }

def reference(x_prompt, x_sample, state_ssd, cache_k, cache_v, c, c_ctx,
              w_mod, b_mod, norm_g, pool_w, pool_scale,
              ssd_w_in, ssd_conv_w, ssd_conv_b, ssd_dt_bias, ssd_a_log, ssd_d, ssd_norm_g, ssd_w_out,
              conf_w_in, conf_b_in, conf_dw, conf_dw_b, conf_ln_g, conf_ln_b, conf_w_out, conf_b_out,
              attn_w_qkv, attn_q_g, attn_k_g, attn_w_o,
              ffn_w_in, ffn_dw, ffn_dw_b, ffn_w_out):
    x = x_prompt
    ssd_states, ctx_ks, ctx_vs = [], [], []
    for i in range(DEPTH):
        kind, j = i % N_MIXERS, i // N_MIXERS
        mod = modulation(c_ctx[None], w_mod[i], b_mod[i])
        h = modulate_in(x, mod, 0, norm_g[i, 0])
        if kind == 0:
            out = pool_mixer(h, pool_w[j], pool_scale[j])
        elif kind == 1:
            h0 = jnp.zeros((h.shape[0], 2, SSD_HEADS, SSD_HEAD_DIM, SSD_STATE), jnp.float32)
            out, st = ssd_mixer(h, h0, ssd_w_in[j], ssd_conv_w[j], ssd_conv_b[j], ssd_dt_bias[j],
                                ssd_a_log[j], ssd_d[j], ssd_norm_g[j], ssd_w_out[j])
            ssd_states.append(st)
        elif kind == 2:
            out = conformer_conv(h, conf_w_in[j], conf_b_in[j], conf_dw[j], conf_dw_b[j],
                                 conf_ln_g[j], conf_ln_b[j], conf_w_out[j], conf_b_out[j])
        else:
            out, kc, vc = attn_context(h, attn_w_qkv[j], attn_q_g[j], attn_k_g[j], attn_w_o[j])
            ctx_ks.append(kc)
            ctx_vs.append(vc)
        x = gated_residual(x, out, mod, 0, norm_g[i, 1])
        x = ffn_sublayer(x, mod, norm_g[i, 2], norm_g[i, 3], ffn_w_in[i], ffn_dw[i], ffn_dw_b[i], ffn_w_out[i])
    y_prompt = x
    new_state_ssd = jnp.stack(ssd_states, axis=1)
    new_cache_k = jnp.stack(ctx_ks, axis=1)
    new_cache_v = jnp.stack(ctx_vs, axis=1)

    x = x_sample
    for i in range(DEPTH):
        kind, j = i % N_MIXERS, i // N_MIXERS
        mod = modulation(c, w_mod[i], b_mod[i])
        h = modulate_in(x, mod, 0, norm_g[i, 0])
        if kind == 0:
            out = pool_mixer(h, pool_w[j], pool_scale[j])
        elif kind == 1:
            out, _ = ssd_mixer(h, state_ssd[:, j], ssd_w_in[j], ssd_conv_w[j], ssd_conv_b[j], ssd_dt_bias[j],
                               ssd_a_log[j], ssd_d[j], ssd_norm_g[j], ssd_w_out[j])
        elif kind == 2:
            out = conformer_conv(h, conf_w_in[j], conf_b_in[j], conf_dw[j], conf_dw_b[j],
                                 conf_ln_g[j], conf_ln_b[j], conf_w_out[j], conf_b_out[j])
        else:
            out = attn_latent(h, cache_k[:, j], cache_v[:, j], attn_w_qkv[j], attn_q_g[j], attn_k_g[j], attn_w_o[j])
        x = gated_residual(x, out, mod, 0, norm_g[i, 1])
        x = ffn_sublayer(x, mod, norm_g[i, 2], norm_g[i, 3], ffn_w_in[i], ffn_dw[i], ffn_dw_b[i], ffn_w_out[i])
    y_sample = x
    return (y_prompt, y_sample, new_state_ssd, new_cache_k, new_cache_v)


_drawn_inputs = setup_inputs


def setup_inputs(seed=0):
    import zlib

    import numpy as np

    out = dict(_drawn_inputs(seed))
    spreads = {}
    factors = {'ssd_d': 3.948,
     'conf_b_in': 8.0,
     'conf_dw_b': 5.236,
     'conf_ln_b': 8.0,
     'conf_b_out': 5.872,
     'attn_q_g': 6.632,
     'ffn_dw_b': 3.939}
    for name, (base, spread) in spreads.items():
        noise = np.random.default_rng([zlib.crc32(name.encode()), seed]).standard_normal(out[name].shape)
        drawn = base * np.exp(spread * noise) if base else spread * noise
        out[name] = __import__('jax').numpy.asarray(drawn.astype(out[name].dtype))
    for name, factor in factors.items():
        out[name] = (out[name] * factor).astype(out[name].dtype)
    return out
```

```python
from contextlib import ExitStack

import numpy as np

import concourse.bass as bass
from concourse import mybir

F32 = mybir.dt.float32
F32R = mybir.dt.float32r
ALU = mybir.AluOpType
ACT = mybir.ActivationFunctionType
AX = mybir.AxisListType

P = 128
D = 1024
KD = D // P
CTX, LAT = 128, 256
LAT0 = CTX + 1
COLS = CTX + 1 + LAT + 1
CHUNKS = [(0, 0), (LAT0, 1), (LAT0 + P, 1)]
STREAMS = [(0, CTX, 0), (LAT0, LAT, 1)]
EPS = 1e-6

DEPTH = 4
FFN = 2816
KF = FFN // P
PAIRS = KF
FFN_TILES = 2 * KF
HALF = KF // 2

WINDOWS = (2, 4, 8, 16)
EDGE = max(WINDOWS) // 2
GAPPED = EDGE + CTX + 2 * EDGE + LAT + EDGE
GAP_AT = [EDGE, EDGE + CTX + 2 * EDGE]

INNER = 2048
SSD_HEADS, HEAD = 32, 64
GROUPS, STATE = 8, 128
HPG = SSD_HEADS // GROUPS
GW = HPG * HEAD
KI = INNER // P
SSD_CONV_TILES = KI + 2 * GROUPS
NDT = 2 * SSD_HEADS

TAPS31 = 31
REACH = TAPS31 // 2
CGAP = REACH + CTX + REACH + LAT + REACH
CGAP_AT = [REACH, 2 * REACH + CTX]
CONVOLVED = CGAP - TAPS31 + 1
CONVOLVED_AT = [at - REACH for at in CGAP_AT]
C_BIN = KD * TAPS31
C_DWB, C_LNG, C_LNB, C_BOUT, C_ALL = (C_BIN + k * KD for k in (2, 3, 4, 5, 6))

AH, AKV, AD = 8, 2, 128
REP = AH // AKV
PAST = 128
SCALE = AD ** -0.5
QK = AH + AKV
GRID_W, ROPE_THETA = 64, 10000.0
A_COS, A_SIN, A_PERM, A_G, A_V, A_ALL = 0, LAT, 2 * LAT, 2 * LAT + AD, 2 * LAT + AD + 2, 2 * LAT + AD + 2 + AKV * AD

RAW_SLOTS, SPLIT_SLOTS, BANKS = 4, 2, 4
MOD_COLS = 256
MOD_PIECES = 6 * D // MOD_COLS
MOD_TILES = MOD_COLS // P
MAXK = HALF


class Linear:

    def __init__(self, name, chunks, tiles, per, outs, width=P):
        self.name, self.chunks, self.tiles, self.per, self.outs, self.width = name, chunks, tiles, per, outs, width


def plan():
    lins = [Linear("pool", 2, KD, 1, 8)]
    for l in range(DEPTH):
        if l == 1:
            lins += [Linear("ssd_conv", SSD_CONV_TILES, KD, 1, SSD_CONV_TILES),
                     Linear("ssd_z", KI, KD, 1, KI), Linear("ssd_dt", 1, KD, 1, 1, NDT),
                     Linear("ssd_out", 2 * KD, KD, 2, KD)]
        if l == 2:
            lins += [Linear("conf_in", 2 * KD, KD, 1, 2 * KD), Linear("conf_out", KD, KD, 1, KD)]
        if l == 3:
            lins += [Linear("qkv", AH + 2 * AKV, KD, 1, AH + 2 * AKV), Linear("attn_out", KD, KD, 1, KD)]
        lins += [Linear(f"ffn_in{l}", FFN_TILES, KD, 1, FFN_TILES), Linear(f"ffn_out{l}", 2 * KD, HALF, 2, KD)]
    n = t = conv = evac = 0
    for x in lins:
        x.n0, x.t0, x.conv0, x.evac0 = n, t, conv, evac
        n += x.chunks
        t += x.outs
        if x.name.startswith("ffn_in") or x.name == "ssd_conv":
            conv += x.outs
        else:
            evac += x.outs
    return {x.name: x for x in lins}, lins



def norm_plan():
    order = []
    for l in range(DEPTH):
        order += [(f"pre{l}.0", KD)]
        if l == 1:
            order += [("ssd", KI)]
        if l == 2:
            order += [("ln", KD)]
        if l == 3:
            order += [("qk", AH + AKV)]
        order += [(f"post{l}.0", KD), (f"pre{l}.1", KD), (f"post{l}.1", KD)]
    out, base, event = {}, 0, 0
    for name, k in order:
        out[name] = (event, base, k)
        base += k
        event += name != "qk"
    return out


def operand_plan():
    out, base = {}, 0
    for l in range(DEPTH):
        for name, k in [(f"mix{l}", KD), *([("ssd_y", KI)] if l == 1 else []),
                        *([(f"mid{l}", KD)] if l in (2, 3) else []), (f"ffn{l}", KD)]:
            out[name] = base
            base += k
    return out


def build_trunk(nc, a, out):
    lin, order = plan()
    norm = norm_plan()
    opnd = operand_plan()

    with ExitStack() as ctx:
        def sb(name, shape, dt=F32, stack=ctx):
            return stack.enter_context(nc.sbuf_tensor(name, shape, dt))

        def bank(name, shape=(P, 512)):
            return ctx.enter_context(nc.psum_tensor(name, list(shape), F32))

        def sem(name):
            return ctx.enter_context(nc.semaphore(name))

        x = sb("x", [P, KD, COLS])
        work = sb("work", [P, KD, COLS])
        h_hi = sb("h_hi", [P, KD, COLS], F32R)
        h_lo = sb("h_lo", [P, KD, COLS], F32R)
        sq = sb("sq", [P, 4, COLS])
        raw = sb("raw", [P, RAW_SLOTS, MAXK * P])
        w_hi = sb("w_hi", [P, SPLIT_SLOTS, MAXK * P], F32R)
        w_lo = sb("w_lo", [P, SPLIT_SLOTS, MAXK * P], F32R)
        mean_col = sb("mean_col", [P, 3])
        ident = sb("ident", [P, P + 4])
        spare = sb("spare", [P, 8])
        eps_col = sb("eps_col", [P, 1])
        std = sb("std", [P, 3])
        rstd = sb("rstd", [P, 3])
        modc = sb("modc", [P, 2, 6 * KD, 2])
        coef = sb("coef", [P, 4, KD, 2])
        gains = sb("gains", [P, DEPTH, 4, KD])
        b_mod = sb("b_mod", [P, DEPTH, 6 * KD])
        cond = sb("cond", [P, KD, 2])
        cond32 = sb("cond32", [P, KD, 32])
        cond_sel = sb("cond_sel", [P, 2])
        taps = sb("taps", [P, DEPTH, FFN_TILES, 4])
        pool_scale = sb("pool_scale", [P, KD])
        tri = sb("tri", [P, 2, P])
        ones = sb("ones", [P, P])
        ssd_taps = sb("ssd_taps", [P, SSD_CONV_TILES, 4])
        dt_rows = sb("dt_rows", [P, 2, NDT])
        ssd_cols = sb("ssd_cols", [P, 3, KI])

        mod_raw = sb("mod_raw", [P, 2, KD * MOD_COLS])
        mod_rows = sb("mod_rows", [P, 2, MOD_COLS])

        with ExitStack() as part:
            g_hi = sb("g_hi", [P, KF, COLS], F32R, part)
            g_lo = sb("g_lo", [P, KF, COLS], F32R, part)
            acc = sb("acc", [P, 4, COLS], F32, part)
            sil = sb("sil", [P, 2, COLS], F32, part)
            gate = sb("gate", [P, 2, COLS], F32, part)
        with ExitStack() as part:
            gapped = sb("gapped", [P, KD, GAPPED], F32, part)
            sums_a = sb("sums_a", [P, KD, GAPPED], F32, part)
            sums_b = sb("sums_b", [P, KD, GAPPED], F32, part)
            inv_count = sb("inv_count", [P, len(WINDOWS), CTX + LAT], F32, part)

        with ExitStack() as part:
            zt = sb("zt", [P, KI, COLS], F32, part)
            xbc = sb("xbc", [P, SSD_CONV_TILES, COLS], F32, part)
            state0 = sb("state0", [P, 2, 2, GW], F32, part)
            state1 = sb("state1", [P, 2, GW], F32, part)
            cb_mask = sb("cb_mask", [P, 2, P], F32, part)
            dtv = sb("dtv", [P, 3, NDT], F32, part)
            adt = sb("adt", [P, 3, NDT], F32, part)
            neg_cum = sb("neg_cum", [P, 3, NDT], F32, part)
        with ExitStack() as part:
            y_hi = sb("y_hi", [P, KI, COLS], F32R, part)
            sb("y_between", [P, KI, COLS], F32, part)
            y_lo = sb("y_lo", [P, KI, COLS], F32R, part)
        with ExitStack() as part:
            conf_tab = sb("conf_tab", [P, C_ALL], F32, part)
            linear_half = sb("linear_half", [P, KD, COLS], F32, part)
            gate_half = sb("gate_half", [P, KD, COLS], F32, part)
            glu = sb("glu", [P, KD, CGAP], F32, part)
            convolved = sb("convolved", [P, KD, CONVOLVED], F32, part)
            ln_mean = sb("ln_mean", [P, 3], F32, part)
        with ExitStack() as part:
            attn_tab = sb("attn_tab", [P, A_ALL], F32, part)
            qkv = sb("qkv", [P, QK + AKV, COLS], F32, part)
            q_turned = sb("q_turned", [P, AH, LAT], F32, part)
            k_all = sb("k_all", [P, AKV, PAST + LAT], F32, part)
            v_rows = sb("v_rows", [P, AKV, len(CHUNKS) * AD], F32, part)
            rot_sin = sb("rot_sin", [P, 2, LAT], F32, part)
            prob = sb("prob", [P, 2, PAST + LAT], F32, part)
            prob_t = sb("prob_t", [P, 2, PAST + LAT], F32, part)
            qk_std = sb("qk_std", [P, 3 * QK], F32, part)
            qk_rstd = sb("qk_rstd", [P, 3 * QK], F32, part)
            row_max = sb("row_max", [P, 2], F32, part)
            neg_max = sb("neg_max", [P, 2], F32, part)
            row_sum = sb("row_sum", [P, 2], F32, part)
            inv_sum = sb("inv_sum", [P, 2], F32, part)
        decay = mod_raw[:, 0, :].rearrange("p (u d n) -> p u d n", u=2, d=2)
        c_scaled = mod_raw[:, 1, :].rearrange("p (u d n) -> p u d n", u=2, d=2)
        to_end = sq[:, 2, 192:384].rearrange("p (c h) -> p c h", c=3)
        full_decay = sq[:, 3, 0:192].rearrange("p (c h) -> p c h", c=3)
        flat = work[:, :, :].rearrange("p k n -> p (k n)")
        turned = flat[:, 0:1024].rearrange("p (u n) -> p u n", u=2)
        x_dt = flat[:, 1024:2048].rearrange("p (u d n) -> p u d n", u=2, d=2)
        x_end = flat[:, 2048:2560].rearrange("p (d n) -> p d n", d=2)
        state_new = flat[:, 2560:3072].rearrange("p (d n) -> p d n", d=2)

        tile_bank = [bank(f"tile_bank{i}") for i in range(BANKS)]
        mod_bank = bank("mod_bank")
        col_bank = bank("col_bank")
        stat_bank = bank("stat_bank")
        rstd_bank = bank("rstd_bank")

        consts = sem("consts")
        loaded0 = sem("loaded0")
        vec_init = sem("vec_init")
        w_loaded = [sem(f"w_loaded{i}") for i in range(RAW_SLOTS)]
        w_rounded = sem("w_rounded")
        w_low_pool = sem("w_low_pool")
        w_low_dve = sem("w_low_dve")
        w_used = sem("w_used")
        mod_loaded = [sem(f"mod_loaded{i}") for i in range(2)]
        mod_used = sem("mod_used")
        rows_ready = sem("rows_ready")
        cols_ready = sem("cols_ready")
        mod_done = sem("mod_done")
        cond_ready = sem("cond_ready")
        acc_ready = sem("acc_ready")
        tap_first = sem("tap_first")
        conv_done = sem("conv_done")
        sil_ready = sem("sil_ready")
        gate_ready = sem("gate_ready")
        g_hi_ready = sem("g_hi_ready")
        g_lo_ready = sem("g_lo_ready")
        evac = sem("evac")
        sq_ready = sem("sq_ready")
        sq_used = sem("sq_used")
        std_ready = sem("std_ready")
        rstd_ready = sem("rstd_ready")
        rstd_spread = sem("rstd_spread")
        x_ready = sem("x_ready")
        opnd_ready = sem("opnd_ready")
        opnd_hi = sem("opnd_hi")
        opnd_lo = sem("opnd_lo")
        dve = sem("dve")
        pe = sem("pe")
        stored = sem("stored")
        z_dt = sem("z_dt")
        dt_pe = sem("dt_pe")
        dt_act = sem("dt_act")
        xbc_ready = sem("xbc_ready")
        s_turned = sem("s_turned")
        s_copied = sem("s_copied")
        s_cum = sem("s_cum")
        s_cexp = sem("s_cexp")
        s_seg = sem("s_seg")
        s_exp = sem("s_exp")
        s_w = sem("s_w")
        s_xdt = sem("s_xdt")
        s_xend = sem("s_xend")
        s_cs = sem("s_cs")
        s_state = sem("s_state")
        s_taken = sem("s_taken")
        s_y = sem("s_y")
        s_out = sem("s_out")
        state_loaded = [sem(f"state_loaded{i}") for i in range(2)]
        state_stored = sem("state_stored")
        yz_ready = sem("yz_ready")
        late_loaded = sem("late_loaded")
        glu_ready = sem("glu_ready")
        conf_tap = sem("conf_tap")
        ln_sums = sem("ln_sums")
        ln_mean_ready = sem("ln_mean_ready")
        ln_spread = sem("ln_spread")
        ln_centred = sem("ln_centred")
        ln_scaled = sem("ln_scaled")
        v_turned = sem("v_turned")
        v_copied = sem("v_copied")
        qk_std_ready = sem("qk_std_ready")
        qk_rstd_ready = sem("qk_rstd_ready")
        qk_spread = sem("qk_spread")
        qk_normed = sem("qk_normed")
        qk_rot = sem("qk_rot")
        qk_cos = sem("qk_cos")
        qk_sin = sem("qk_sin")
        qk_turned = sem("qk_turned")
        cache_stored = sem("cache_stored")
        att_score = sem("att_score")
        att_rowmax = sem("att_rowmax")
        att_max = sem("att_max")
        att_exp = sem("att_exp")
        att_inv = sem("att_inv")
        att_prob = sem("att_prob")
        att_turned = sem("att_turned")
        att_pt = sem("att_pt")
        att_pv = sem("att_pv")
        att_part = sem("att_part")

        block = ctx.enter_context(nc.Block())

        def slot(n):
            return n % RAW_SLOTS

        def fetched(n, i=0, per=0):
            return 16 * (n // RAW_SLOTS + 1) + i * (16 * per // RAW_SLOTS)

        def weights(t, n, tiles):
            return t[:, n % SPLIT_SLOTS, 0:tiles * P]

        def split_at(s):
            return (s.tiles if s.name.startswith("conf") else s.tiles // 2) * s.width

        def units():
            for h in range(AH):
                for c in range(3):
                    yield h, c, 3 * h + c

        def copied_out(engine, u):
            h, c = u // 3, u % 3
            if c == 2:
                engine.wait_ge(opnd_ready, opnd["mid3"] + h + 1)
            else:
                engine.wait_ge(att_part, 2 * h + c + 1)

        LOADS0 = 16 * 10
        DT_DVE = 20
        CONSTS = 15

        class Chain:

            def __init__(self, engine, semaphore):
                self.engine, self.sem, self.n = engine, semaphore, 0

            def did(self, ins):
                ins.then_inc(self.sem, 1)
                self.n += 1
                return self.n

            def wait(self, n=None):
                self.engine.wait_ge(self.sem, self.n if n is None else n)

        def steps():
            for g in range(GROUPS):
                for c in range(3):
                    yield g, c, 3 * g + c, 2 * g + c - 1

        def state_dirs(c):
            return [(0, 1), (0,), (1,)][c]

        def linears(l):
            return {0: ["pool"], 1: ["ssd_conv", "ssd_z", "ssd_dt", "ssd_out"], 2: ["conf_in", "conf_out"],
                    3: ["qkv", "attn_out"]}[l]

        def owner(n):
            for s in order:
                if s.n0 <= n < s.n0 + s.chunks:
                    return s
            return None

        @block.sync
        def _(sp):
            sp.dma_start(cond[:, :, :], a["cond"]).then_inc(loaded0, 16)
            sp.dma_start(x[:, :, :], a["x"]).then_inc(loaded0, 16)
            sp.dma_start(gains[:, :, :, :], a["gains"]).then_inc(loaded0, 16)
            sp.dma_start(b_mod[:, :, :], a["b_mod"]).then_inc(loaded0, 16)
            sp.dma_start(taps[:, :, :, :], a["taps"]).then_inc(loaded0, 16)
            sp.dma_start(pool_scale[:, :], a["pool_scale"]).then_inc(loaded0, 16)

            sp.dma_start(inv_count[:, :, :], a["inv_count"]).then_inc(loaded0, 16)
            sp.dma_start(ssd_taps[:, :, :], a["ssd_taps"]).then_inc(loaded0, 16)
            sp.dma_start(dt_rows[:, :, :], a["dt_rows"]).then_inc(loaded0, 16)
            sp.dma_start(ssd_cols[:, :, :], a["ssd_cols"]).then_inc(loaded0, 16)

            def load_chunk(s, j, i=None, per=0):
                n = s.n0 + j
                src = a[s.name]
                width = s.tiles * s.width
                if i is None:
                    sp.wait_ge(w_low_pool, n + 1)
                    sp.wait_ge(w_low_dve, n + 1)
                    sp.dma_start(raw[:, slot(n), 0:width], src[j]).then_inc(w_loaded[slot(n)], 16)
                else:
                    sp.wait_ge(w_low_pool, i * per + (n + 1))
                    sp.wait_ge(w_low_dve, i * per + (n + 1))
                    sp.dma_start(raw[:, slot(n), 0:width],
                                 src[bass.ds(i * per + j, 1), :, :].rearrange("a p n -> p (a n)")
                                 ).then_inc(w_loaded[slot(n)], 16)

            def load_mod(l, piece, i=None, per=0, first=False):
                g = l * MOD_PIECES + piece
                if i is None:
                    if g >= 2:
                        sp.wait_ge(mod_used, g - 1)
                    src = a["w_mod"][g]
                else:
                    if not first:
                        sp.wait_ge(mod_used, i * per + g - 1)
                    src = a["w_mod"][bass.ds(i * per + g, 1), :, :].rearrange("a p n -> p (a n)")
                sp.dma_start(mod_raw[:, g % 2, :], src).then_inc(mod_loaded[g % 2], 16)

            for j in range(2):
                load_mod(0, j)
            with sp.Fori(0, MOD_PIECES // 2 - 1) as i:
                for j in range(2):
                    load_mod(0, j + 2, i, 2)
            def scan_traffic():
                for g in range(GROUPS):
                    if g >= 2:
                        sp.wait_ge(s_y, 3 * (g - 2) + 3)
                        sp.wait_ge(s_taken, 3 * (g - 2) + 3)
                    else:
                        sp.wait_ge(opnd_lo, opnd["mix1"] + KD)
                    sp.dma_start(state0[:, g % 2, :, :], a["state_in"][:, :, g * GW:(g + 1) * GW]
                                 ).then_inc(state_loaded[g % 2], 16)
                    if g >= 1:
                        sp.wait_ge(s_taken, 3 * (g - 1) + 1)
                        sp.dma_start(out["state"][:, :, (g - 1) * GW:g * GW], state_new).then_inc(state_stored, 16)
                sp.wait_ge(s_taken, 3 * (GROUPS - 1) + 1)
                sp.dma_start(out["state"][:, :, (GROUPS - 1) * GW:], state_new).then_inc(state_stored, 16)
                sp.wait_ge(state_stored, 16 * GROUPS)

            for s in order:
                if s.name == "ssd_out":
                    for j in range(RAW_SLOTS):
                        load_chunk(s, j)
                    scan_traffic()
                    with sp.Fori(0, s.chunks // 4 - 1) as i:
                        for j in range(4):
                            load_chunk(s, j + RAW_SLOTS, i, 4)
                elif s.name == "attn_out":
                    for j in range(RAW_SLOTS):
                        load_chunk(s, j)
                    sp.wait_ge(qk_normed, QK)
                    sp.dma_start(out["cache_k"], qkv[:, AH:QK, 0:CTX]).then_inc(cache_stored, 16)
                    sp.dma_start(out["cache_v"], qkv[:, QK:, 0:CTX]).then_inc(cache_stored, 16)
                    for j in range(RAW_SLOTS, s.chunks):
                        load_chunk(s, j)
                elif s.name.startswith("ffn_in"):
                    l = int(s.name[-1])
                    more = l + 1 < DEPTH
                    with sp.Fori(0, FFN_TILES // 4) as i:
                        for j in range(4):
                            load_chunk(s, j, i, 4)
                            if more and j % 2:
                                load_mod(l + 1, j // 2, i, 2)
                    if more:
                        load_mod(l + 1, MOD_PIECES - 2)
                        load_mod(l + 1, MOD_PIECES - 1)
                elif s.chunks >= 8:
                    with sp.Fori(0, s.chunks // 4) as i:
                        for j in range(4):
                            load_chunk(s, j, i, 4)
                    for j in range(s.chunks // 4 * 4, s.chunks):
                        load_chunk(s, j)
                else:
                    for j in range(s.chunks):
                        load_chunk(s, j)
            sp.wait_ge(x_ready, KD * (2 * DEPTH + 1))
            sp.dma_start(out["y"], x[:, :, :]).then_inc(stored, 16)
            sp.wait_ge(stored, 16)
            sp.wait_ge(cache_stored, 32)

        @block.gpsimd
        def _(pool):
            pool.memset(spare[:, 6:7], 0.0).then_inc(w_low_pool, RAW_SLOTS)
            pool.memset(ident[:, :], 0.0).then_inc(consts, 1)
            pool.memset(mean_col[:, 0:1], 1.0 / D).then_inc(consts, 1)
            pool.memset(mean_col[:, 1:2], 1.0 / INNER).then_inc(consts, 1)
            pool.memset(mean_col[:, 2:3], 1.0 / AD).then_inc(consts, 1)
            pool.memset(eps_col[:, :], EPS).then_inc(consts, 1)
            pool.memset(cond_sel[:, :], 0.0).then_inc(consts, 1)
            pool.wait_ge(consts, 6)
            pool.affine_select(out=ident[:, 0:P], in_=ident[:, 0:P], compare_op=ALU.not_equal, fill=1.0, base=0,
                               pattern=[[-1, P]], channel_multiplier=1).then_inc(consts, 1)
            for g in range(4):
                pool.wait_ge(consts, 7 + g)
                pool.affine_select(out=cond_sel[:, :], in_=cond_sel[:, :], compare_op=ALU.not_equal, fill=1.0,
                                   base=-32 * g, pattern=[[-1, 2]], channel_multiplier=1).then_inc(consts, 1)

            pool.memset(tri[:, :, :], 1.0).then_inc(consts, 1)
            pool.memset(ones[:, :], 1.0).then_inc(consts, 1)
            pool.wait_ge(consts, CONSTS - 2)
            for d in range(2):
                sign = -1 if d else 1
                pool.affine_select(out=tri[:, d, :], in_=tri[:, d, :], compare_op=ALU.is_ge, fill=0.0, base=0,
                                   pattern=[[sign, P]], channel_multiplier=-sign).then_inc(consts, 1)

            def low_part(s, j, i=None, per=0):
                n = s.n0 + j
                w = split_at(s)
                pool.wait_ge(w_rounded, n + 1 if i is None else i * per + (n + 1))
                pool.tensor_tensor(w_lo[:, n % SPLIT_SLOTS, 0:w], raw[:, slot(n), 0:w],
                                   w_hi[:, n % SPLIT_SLOTS, 0:w].bitcast(F32), ALU.subtract).then_inc(w_low_pool, 1)

            def scan_pool():
                for g, c, u, v in steps():
                    pool.wait_ge(s_copied, u + 1)
                    if u >= 2:
                        pool.wait_ge(s_y, u - 1)
                    xt = turned[:, u % 2, P:P + GW].rearrange("p (h q) -> p h q", h=HPG)
                    for d in range(2):
                        h0 = d * SSD_HEADS + g * HPG
                        pool.tensor_tensor(x_dt[:, u % 2, d, :].rearrange("p (h q) -> p h q", h=HPG), xt,
                                           dtv[:, c, h0:h0 + HPG].unsqueeze(2).broadcast_to([P, HPG, HEAD]),
                                           ALU.mult).then_inc(s_xdt, 1)
                    if u >= 1:
                        pool.wait_ge(s_state, u)
                    for d in state_dirs(c):
                        h0 = d * SSD_HEADS + g * HPG
                        ins = pool.tensor_tensor(x_end[:, d, :].rearrange("p (h q) -> p h q", h=HPG), xt,
                                                 to_end[:, c, h0:h0 + HPG].unsqueeze(2).broadcast_to([P, HPG, HEAD]),
                                                 ALU.mult)
                    ins.then_inc(s_xend, 1)
                    if c:
                        for d in range(2):
                            pool.wait_ge(s_cexp, 2 * v + d + 1)
                            cs = c_scaled[:, u % 2, d, :].rearrange("p (h i) -> p h i", h=HPG)
                            c0 = CHUNKS[c][0]
                            pool.tensor_tensor(cs, cs, xbc[:, KI + GROUPS + g, c0:c0 + P].unsqueeze(1).broadcast_to(
                                [P, HPG, P]), ALU.mult).then_inc(s_cs, 1)

            def conf_pool():
                s = lin["conf_in"]
                pool.wait_ge(w_used, s.n0)
                pool.memset(glu[:, :, :], 0.0).then_inc(glu_ready, 1)
                low_part(s, 0)
                low_part(s, 1)
                pool.wait_ge(glu_ready, 1)
                for m in range(KD):
                    if m + 1 < KD:
                        low_part(s, 2 * m + 2)
                    pool.wait_ge(evac, 4 + s.evac0 + 2 * m + 2)
                    for c0, w, k in STREAMS:
                        pool.tensor_tensor(glu[:, m, CGAP_AT[k]:CGAP_AT[k] + w], linear_half[:, m, c0:c0 + w],
                                           gate_half[:, m, c0:c0 + w], ALU.mult).then_inc(glu_ready, 1)
                    if m + 1 < KD:
                        low_part(s, 2 * m + 3)

            def rope_pool():
                pool.wait_ge(late_loaded, 48)
                for t in range(QK):
                    pool.wait_ge(qk_normed, t + 1)
                    to = q_turned[:, t, :] if t < AH else k_all[:, t - AH, PAST:]
                    pool.tensor_tensor(to, qkv[:, t, LAT0:LAT0 + LAT], attn_tab[:, A_COS:A_COS + LAT],
                                       ALU.mult).then_inc(qk_cos, 1)

            for s in order:
                if s.name == "conf_in":
                    conf_pool()
                    continue
                if s.name == "attn_out":
                    rope_pool()
                if s.name == "ssd_out":
                    pool.wait_ge(z_dt, DT_DVE)
                    scan_pool()
                done = 0
                if s.chunks >= 8:
                    done = s.chunks // 4 * 4
                    with pool.Fori(0, s.chunks // 4) as i:
                        for j in range(4):
                            low_part(s, j, i, 4)
                for j in range(done, s.chunks):
                    low_part(s, j)

        @block.scalar
        def _(act):
            def apart():
                act.wait_ge(consts, CONSTS)

            def round_chunk(s, j, i=None, per=0):
                n = s.n0 + j
                w = s.tiles * s.width
                act.wait_ge(w_loaded[slot(n)], fetched(n) if i is None else fetched(n, i, per))
                if i is not None:
                    act.wait_ge(w_used, i * per + (n - SPLIT_SLOTS + 1))
                elif n >= SPLIT_SLOTS:
                    act.wait_ge(w_used, n - SPLIT_SLOTS + 1)
                act.activation(w_hi[:, n % SPLIT_SLOTS, 0:w], raw[:, slot(n), 0:w], ACT.Copy).then_inc(w_rounded, 1)

            def round_next(n):
                s = owner(n)
                if s is not None:
                    round_chunk(s, n - s.n0)

            def mod_row(l, piece, i=None, per=0):
                g = l * MOD_PIECES + piece
                at = (lambda v: v) if i is None else (lambda v: i * per + v)
                act.wait_ge(mod_used, at(g + 1))
                act.wait_ge(cols_ready, at(2 + g - 1))
                act.activation(mod_rows[:, g % 2, :], mod_bank[:, 0:MOD_COLS],
                               ACT.Copy).then_inc(rows_ready, 1)

            def square(src, count):
                if count >= 4:
                    act.wait_ge(sq_used, count - 3)
                act.activation(sq[:, count % 4, :], src, ACT.Square).then_inc(sq_ready, 1)

            def take_std(name):
                e, base, k = norm[name]
                act.wait_ge(sq_used, base + k)
                act.activation(std[:, :], stat_bank[:, 0:3], ACT.Sqrt, bias=eps_col[:, 0:1]).then_inc(std_ready, 1)

            def tiles_out(s, name, bias=None):
                e, base, k = norm[name]
                for m in range(KD):
                    if s.per == 1:
                        round_next(s.n0 + m + 1)
                        act.wait_ge(w_used, s.n0 + m + 1)
                    elif s.per == 2:
                        round_next(s.n0 + 2 * m + 1)
                        round_next(s.n0 + 2 * m + 2)
                        act.wait_ge(w_used, s.n0 + 2 * m + 2)
                    b = tile_bank[(s.t0 + m) % BANKS]
                    count = base + m
                    if count >= 4:
                        act.wait_ge(sq_used, count - 3)
                    kw = {} if bias is None else {"bias": bias[:, m:m + 1]}
                    act.activation(sq[:, count % 4, :], b[:, 0:COLS], ACT.Square, **kw).then_inc(sq_ready, 1)
                    act.activation(work[:, m, :], b[:, 0:COLS], ACT.Copy if bias is None else ACT.Identity,
                                   **kw).then_inc(evac, 1)

            def squares_of_x(name, xbase):
                e, base, k = norm[name]
                for m in range(KD):
                    act.wait_ge(x_ready, xbase + m + 1)
                    square(x[:, m, :], base + m)

            def split_high(name, src=None, hi=None):
                base = opnd[name]
                for m in range(KD):
                    act.wait_ge(opnd_ready, base + m + 1)
                    act.activation(h_hi[:, m, :], work[:, m, :], ACT.Copy).then_inc(opnd_hi, 1)

            def ffn_in(l):
                s = lin[f"ffn_in{l}"]
                more = l + 1 < DEPTH
                p0 = l * PAIRS

                def at(v, i):
                    return v if i is None else i * 4 + v

                def group(i, first=False, last=False, base=0):
                    for j in range(4):
                        c = s.conv0 + base + j
                        pair = p0 + (base + j) // 2
                        half = (lambda v: v) if i is None else (lambda v: i * 2 + v)
                        if i is not None or base + j + 1 < FFN_TILES:
                            round_chunk(s, base + j + 1, i, 4)
                        else:
                            round_next(s.n0 + base + j + 1)
                        if j % 2 == 0 and not (first and j == 0):
                            act.wait_ge(gate_ready, half(pair))
                            apart()
                            act.activation(g_hi[:, bass.ds(half(pair - p0 - 1), 1), :].rearrange("p a n -> p (a n)"),
                                           gate[:, (pair - 1) % 2, :], ACT.Copy).then_inc(g_hi_ready, 1)
                        act.wait_ge(w_used, at(s.n0 + base + j + 1, i))
                        apart()
                        k = bass.ds(at(base + j, i), 1)
                        act.activation(acc[:, c % 4, :], tile_bank[(s.t0 + base + j) % BANKS][:, 0:COLS], ACT.Identity,
                                       scale=taps[:, l, k, 1:2].rearrange("p a b -> p (a b)"),
                                       bias=taps[:, l, k, 3:4].rearrange("p a b -> p (a b)")).then_inc(acc_ready, 1)
                        if j % 2:
                            act.wait_ge(conv_done, at(4 + c, i))
                            act.activation(sil[:, pair % 2, :], acc[:, (c - 1) % 4, :], ACT.Silu).then_inc(sil_ready, 1)
                            if more:
                                mod_row(l + 1, base // 2 + j // 2, i, 2)

                group(None, first=True)
                with act.Fori(0, FFN_TILES // 4 - 2) as i:
                    group(i, base=4)
                group(None, last=True, base=FFN_TILES - 4)
                act.wait_ge(gate_ready, p0 + PAIRS)
                act.activation(g_hi[:, PAIRS - 1, :], gate[:, (p0 + PAIRS - 1) % 2, :], ACT.Copy).then_inc(g_hi_ready, 1)
                if more:
                    mod_row(l + 1, MOD_PIECES - 2)
                    mod_row(l + 1, MOD_PIECES - 1)

            def ssd_conv():
                s = lin["ssd_conv"]

                def tile(base, j, i, first=False):
                    at = (lambda v: v) if i is None else (lambda v: i * 4 + v)
                    t, c = base + j, s.conv0 + base + j
                    if i is not None or t + 1 < s.chunks:
                        round_chunk(s, t + 1, i, 4)
                    else:
                        round_next(s.n0 + t + 1)
                    if not first:
                        act.wait_ge(conv_done, at(4 + c))
                    act.wait_ge(w_used, at(s.n0 + t + 1))
                    apart()
                    k = bass.ds(at(t), 1)
                    act.activation(xbc[:, k, :].rearrange("p a n -> p (a n)"), tile_bank[(s.t0 + t) % BANKS][:, 0:COLS],
                                   ACT.Identity, scale=ssd_taps[:, k, 1:2].rearrange("p a b -> p (a b)"),
                                   bias=ssd_taps[:, k, 3:4].rearrange("p a b -> p (a b)")).then_inc(acc_ready, 1)
                    if not first:
                        silu(bass.ds(at(t - 1), 1))

                def silu(k):
                    b = xbc[:, k, :].rearrange("p a n -> p (a n)")
                    act.activation(b, b, ACT.Silu).then_inc(xbc_ready, 1)

                for j in range(4):
                    tile(0, j, None, first=j == 0)
                with act.Fori(0, s.chunks // 4 - 2) as i:
                    for j in range(4):
                        tile(4, j, i)
                for j in range(4):
                    tile(s.chunks - 4, j, None)
                act.wait_ge(conv_done, 4 + s.conv0 + s.chunks)
                silu(bass.ds(s.chunks - 1, 1))

            def ssd_z_dt():
                s = lin["ssd_z"]
                for m in range(s.chunks):
                    round_next(s.n0 + m + 1)
                    act.wait_ge(w_used, s.n0 + m + 1)
                    act.activation(zt[:, m, :], tile_bank[(s.t0 + m) % BANKS][:, 0:COLS], ACT.Silu).then_inc(evac, 1)
                s = lin["ssd_dt"]
                round_next(s.n0 + 1)
                act.wait_ge(w_used, s.n0 + 1)
                act.activation(sq[0:NDT, 0, :], tile_bank[s.t0 % BANKS][0:NDT, 0:COLS], ACT.Copy).then_inc(evac, 1)

            def dt_prepare():
                act.activation(sq[:, 3, 192:256], dt_rows[:, 1, :], ACT.Exp).then_inc(dt_act, 1)
                act.wait_ge(z_dt, 3)
                act.activation(sq[:, 3, 0:192], sq[:, 2, 0:192], ACT.Exp, scale=-1.0).then_inc(dt_act, 1)
                act.wait_ge(z_dt, DT_DVE - 1)
                t = to_end[:, :, :]
                act.activation(t, t, ACT.Exp).then_inc(dt_act, 1)
                act.activation(full_decay[:, :, :], full_decay[:, :, :], ACT.Exp).then_inc(dt_act, 1)

            def scan_act():
                for g, c, u, v in steps():
                    act.wait_ge(s_turned, u + 1)
                    if u >= 2:
                        act.wait_ge(s_state, u - 1)
                        act.wait_ge(s_xend, u - 1)
                        act.wait_ge(s_seg, 2 * (u - 2) + 2)
                    act.activation(turned[:, u % 2, :], tile_bank[u % 2][:, :], ACT.Copy).then_inc(s_copied, 1)
                    if c:
                        if u >= 2:
                            act.wait_ge(s_y, u - 1)
                        for d in range(2):
                            act.wait_ge(s_cum, 2 * u + d + 1)
                            act.activation(c_scaled[:, u % 2, d, :], tile_bank[2 + d][:, :], ACT.Exp).then_inc(s_cexp, 1)
                    for d in range(2):
                        act.wait_ge(s_seg, 2 * u + d + 1)
                        act.activation(decay[:, u % 2, d, :], decay[:, u % 2, d, :], ACT.Exp).then_inc(s_exp, 1)

            def ssd_norm():
                e, base, k = norm["ssd"]
                for m in range(k):
                    act.wait_ge(yz_ready, m + 1)
                    square(xbc[:, m, :], base + m)
                take_std("ssd")
                for m in range(k):
                    act.wait_ge(opnd_ready, opnd["ssd_y"] + m + 1)
                    act.activation(y_hi[:, m, :], xbc[:, m, :], ACT.Copy).then_inc(opnd_hi, 1)

            def conf_mix():
                s = lin["conf_in"]
                act.wait_ge(late_loaded, 16)
                for m in range(s.chunks):
                    round_next(s.n0 + m + 1)
                    act.wait_ge(w_used, s.n0 + m + 1)
                    gated = m % 2
                    act.activation((linear_half, gate_half)[gated][:, m // 2, :], tile_bank[(s.t0 + m) % BANKS][:, 0:COLS],
                                   ACT.Sigmoid if gated else ACT.Identity, bias=conf_tab[:, C_BIN + m:C_BIN + m + 1]
                                   ).then_inc(evac, 1)
                e, base, _ = norm["ln"]
                for m in range(KD):
                    act.wait_ge(ln_centred, m + 1)
                    square(work[:, m, :], base + m)
                take_std("ln")
                o = opnd["mid2"]
                for m in range(KD + 1):
                    if m < KD:
                        act.wait_ge(ln_scaled, m + 1)
                        act.activation(work[:, m, :], work[:, m, :], ACT.Silu, scale=conf_tab[:, C_LNG + m:C_LNG + m + 1],
                                       bias=conf_tab[:, C_LNB + m:C_LNB + m + 1]).then_inc(opnd_ready, 1)
                    if m:
                        act.wait_ge(opnd_ready, o + m)
                        act.activation(h_hi[:, m - 1, :], work[:, m - 1, :], ACT.Copy).then_inc(opnd_hi, 1)

            def attn_mix():
                s = lin["qkv"]
                for m in range(s.chunks):
                    round_next(s.n0 + m + 1)
                    act.wait_ge(w_used, s.n0 + m + 1)
                    act.activation(qkv[:, m, :], tile_bank[(s.t0 + m) % BANKS][:, 0:COLS], ACT.Copy).then_inc(evac, 1)
                e, base, _ = norm["qk"]
                act.wait_ge(evac, 4 + s.evac0 + s.chunks)
                for m in range(QK):
                    square(qkv[:, m, :], base + m)
                for kv in range(AKV):
                    act.wait_ge(v_turned, kv + 1)
                    act.activation(v_rows[:, kv, :], tile_bank[2 + kv][:, 0:3 * AD], ACT.Copy).then_inc(v_copied, 1)
                act.wait_ge(sq_used, base + QK)
                act.activation(qk_std[:, :], stat_bank[:, 0:3 * QK], ACT.Sqrt, bias=eps_col[:, 0:1]).then_inc(qk_std_ready, 1)
                o = opnd["mid3"]
                for u in range(3 * AH + 3):
                    if u < 3 * AH:
                        w = P if u % 3 == 0 else PAST + LAT
                        act.wait_ge(att_max, u + 1)
                        if u >= 2:
                            act.wait_ge(att_turned, u - 1)
                            act.wait_ge(att_inv, u - 1)
                        act.activation(prob[:, u % 2, 0:w], tile_bank[u % 2][:, 0:w], ACT.Exp, scale=SCALE,
                                       bias=neg_max[:, u % 2:u % 2 + 1], accum_out=row_sum[:, u % 2:u % 2 + 1]
                                       ).then_inc(att_exp, 1)
                    if 2 <= u < 3 * AH + 2:
                        b = u - 2
                        w = P if b % 3 == 0 else PAST + LAT
                        act.wait_ge(att_turned, b + 1)
                        if b >= 2:
                            act.wait_ge(att_pv, b - 1)
                        act.activation(prob_t[:, b % 2, 0:w], tile_bank[2 + b % 2][:, 0:w], ACT.Copy).then_inc(att_pt, 1)
                    if u >= 3:
                        b = u - 3
                        h, c = b // 3, b % 3
                        act.wait_ge(att_pv, b + 1)
                        act.activation(work[:, h, CHUNKS[c][0]:CHUNKS[c][0] + P], (mod_bank, col_bank)[b % 2][:, 0:P],
                                       ACT.Copy).then_inc(opnd_ready if c == 2 else att_part, 1)
                        if c == 0 and h:
                            high_head(o, h - 1)
                high_head(o, AH - 1)

            def high_head(o, h):
                act.wait_ge(att_part, 2 * h + 2)
                act.wait_ge(opnd_ready, o + h + 1)
                act.activation(h_hi[:, h, :], work[:, h, :], ACT.Copy).then_inc(opnd_hi, 1)

            act.wait_ge(loaded0, LOADS0)
            act.wait_ge(vec_init, 2)
            act.activation(cond32[:, :, 0:2], cond[:, :, :], ACT.Silu).then_inc(cond_ready, 1)
            act.wait_ge(consts, CONSTS)
            act.activation(spare[:, 4:5], eps_col[:, :], ACT.Copy).then_inc(rows_ready, 2)
            act.activation(spare[:, 5:6], eps_col[:, :], ACT.Copy).then_inc(evac, 4)
            with act.Fori(0, MOD_PIECES // 2) as i:
                for j in range(2):
                    mod_row(0, j, i, 2)
            round_next(0)
            xb = 0
            squares_of_x("pre0.0", 0)
            take_std("pre0.0")
            for l in range(DEPTH):
                if l == 0:
                    split_high("mix0")
                    s = lin["pool"]
                    e, base, k = norm["post0.0"]
                    round_next(1)
                    for m in range(KD):
                        if m == 4:
                            round_next(2)
                        if m % 4 == 3:
                            act.wait_ge(w_used, m // 4 + 1)
                        else:
                            act.wait_ge(pe, m + 1 - m // 4)
                        b = tile_bank[(s.t0 + m) % BANKS]
                        if base + m >= 4:
                            act.wait_ge(sq_used, base + m - 3)
                        act.activation(sq[:, (base + m) % 4, :], b[:, 0:COLS], ACT.Square,
                                       scale=pool_scale[:, m:m + 1]).then_inc(sq_ready, 1)
                        act.activation(work[:, m, :], b[:, 0:COLS], ACT.Identity,
                                       scale=pool_scale[:, m:m + 1]).then_inc(evac, 1)
                if l == 1:
                    split_high("mix1")
                    ssd_conv()
                    ssd_z_dt()
                    dt_prepare()
                    scan_act()
                    ssd_norm()
                    tiles_out(lin["ssd_out"], "post1.0")
                if l == 2:
                    split_high("mix2")
                    conf_mix()
                    tiles_out(lin["conf_out"], "post2.0", conf_tab[:, C_BOUT:C_BOUT + KD])
                if l == 3:
                    split_high("mix3")
                    attn_mix()
                    tiles_out(lin["attn_out"], "post3.0")
                take_std(f"post{l}.0")
                squares_of_x(f"pre{l}.1", KD * (2 * l + 1))
                take_std(f"pre{l}.1")
                split_high(f"ffn{l}")
                if l == 3:
                    act.wait_ge(cache_stored, 32)
                ffn_in(l)
                tiles_out(lin[f"ffn_out{l}"], f"post{l}.1")
                if l == 1:
                    act.dma_start(conf_tab[:, :], a["conf_tab"]).then_inc(late_loaded, 16)
                if l == 2:
                    act.dma_start(attn_tab[:, :], a["attn_tab"]).then_inc(late_loaded, 16)
                    act.dma_start(k_all[:, :, 0:PAST], a["cache_k"]).then_inc(late_loaded, 16)
                take_std(f"post{l}.1")
                if l + 1 < DEPTH:
                    squares_of_x(f"pre{l + 1}.0", KD * (2 * l + 2))
                    take_std(f"pre{l + 1}.0")

        @block.vector
        def _(vec):
            ch = Chain(vec, dve)

            def low_part(s, j, i=None, per=0):
                n = s.n0 + j
                w0, w1 = split_at(s), s.tiles * s.width
                vec.wait_ge(w_rounded, n + 1 if i is None else i * per + (n + 1))
                vec.tensor_tensor(w_lo[:, n % SPLIT_SLOTS, w0:w1], raw[:, slot(n), w0:w1],
                                  w_hi[:, n % SPLIT_SLOTS, w0:w1].bitcast(F32), ALU.subtract).then_inc(w_low_dve, 1)

            def low_next(n):
                s = owner(n)
                if s is not None and split_at(s) < s.tiles * s.width:
                    low_part(s, n - s.n0)

            def mod_column(l, piece, i=None, per=0):
                g = l * MOD_PIECES + piece
                vec.wait_ge(cols_ready, 2 + g + 1 if i is None else i * per + (2 + g + 1))
                t0 = piece * MOD_TILES if i is None else i * (per * MOD_TILES) + piece * MOD_TILES
                vec.tensor_tensor(modc[:, l % 2, bass.ds(t0, MOD_TILES), :],
                                  col_bank[:, 0:2 * MOD_TILES].rearrange(
                                      "p (t s) -> p t s", s=2),
                                  b_mod[:, l, bass.ds(t0, MOD_TILES)].unsqueeze(2).broadcast_to([P, MOD_TILES, 2]),
                                  ALU.add).then_inc(mod_done, 1)

            def take_rstd(name):
                e, base, k = norm[name]
                vec.wait_ge(std_ready, e + 1)
                vec.reciprocal(rstd[:, :], std[:, :]).then_inc(rstd_ready, 1)

            def coefficients(l):
                vec.wait_ge(mod_done, 2 + (l + 1) * MOD_PIECES)
                vec.wait_ge(x_ready, KD * (2 * l + 1))
                for k in range(2):
                    scale = modc[:, l % 2, (3 * k + 1) * KD:(3 * k + 2) * KD, :]
                    opening = modc[:, l % 2, (3 * k + 2) * KD:(3 * k + 3) * KD, :]
                    ch.did(vec.scalar_tensor_tensor(
                        out=coef[:, 2 * k, :, :], in0=scale, scalar=1.0,
                        in1=gains[:, l, 2 * k, :].unsqueeze(2).broadcast_to([P, KD, 2]), op0=ALU.add, op1=ALU.mult))
                    ch.did(vec.tensor_tensor(coef[:, 2 * k + 1, :, :], opening,
                                             gains[:, l, 2 * k + 1, :].unsqueeze(2).broadcast_to([P, KD, 2]), ALU.mult))
                ch.wait()

            def residual(name, k, evac_count):
                e, base, _ = norm[name]
                vec.wait_ge(evac, evac_count)
                vec.wait_ge(rstd_spread, e + 1)
                scaled = [0] * KD
                for m in range(KD + 1):
                    if m < KD:
                        scaled[m] = ch.did(vec.tensor_tensor(work[:, m, :], work[:, m, :], rstd_bank[:, 0:COLS], ALU.mult))
                    if m:
                        ch.wait(scaled[m - 1])
                        for c0, w, s in STREAMS:
                            ins = vec.scalar_tensor_tensor(
                                out=x[:, m - 1, c0:c0 + w], in0=work[:, m - 1, c0:c0 + w],
                                scalar=coef[:, 2 * k + 1, m - 1, s:s + 1], in1=x[:, m - 1, c0:c0 + w],
                                op0=ALU.mult, op1=ALU.add)
                            if s:
                                ins.then_inc(x_ready, 1)
                            else:
                                ch.did(ins)

            def modulate(l, name, k, xbase, opname, to_gapped=False):
                e, base, _ = norm[name]
                o = opnd[opname]
                vec.wait_ge(rstd_spread, e + 1)
                vec.wait_ge(x_ready, xbase + KD)
                scaled = [0] * KD
                for m in range(KD + 2):
                    if m < KD:
                        scaled[m] = ch.did(vec.tensor_tensor(work[:, m, :], x[:, m, :], rstd_bank[:, 0:COLS], ALU.mult))
                    if 1 <= m <= KD:
                        t = m - 1
                        ch.wait(scaled[t])
                        for c0, w, s in STREAMS:
                            dst = gapped[:, t, GAP_AT[s]:GAP_AT[s] + w] if to_gapped else work[:, t, c0:c0 + w]
                            ins = vec.tensor_scalar(dst, work[:, t, c0:c0 + w], coef[:, 2 * k, t, s:s + 1],
                                                    modc[:, l % 2, 3 * k * KD + t, s:s + 1], ALU.mult, ALU.add)
                            if s and not to_gapped:
                                ins.then_inc(opnd_ready, 1)
                            else:
                                ch.did(ins)
                    if m >= 2 and not to_gapped:
                        low_operand(o, m - 2)

            def low_operand(o, t):
                vec.wait_ge(opnd_hi, o + t + 1)
                vec.tensor_tensor(h_lo[:, t, :], work[:, t, :], h_hi[:, t, :].bitcast(F32),
                                  ALU.subtract).then_inc(opnd_lo, 1)

            def pool_mix():
                ch.wait()
                n = GAPPED
                kg = KD // len(WINDOWS)
                ch.did(vec.tensor_tensor(sums_a[:, :, 1:n], gapped[:, :, 0:n - 1], gapped[:, :, 1:n], ALU.add))
                ch.wait()
                src, dst, lo, hi, step = sums_a, sums_b, 1, n, 1
                for g in range(len(WINDOWS)):
                    k0, k1 = g * kg, (g + 1) * kg
                    if g:
                        ch.did(vec.tensor_tensor(dst[:, k0:, lo + step:hi - step], src[:, k0:, lo:hi - 2 * step],
                                                 src[:, k0:, lo + 2 * step:hi], ALU.add))
                        ch.wait()
                        src, dst, lo, hi, step = dst, src, lo + step, hi - step, 2 * step
                    for c0, w, s in STREAMS:
                        j0 = s * CTX
                        ga = slice(GAP_AT[s], GAP_AT[s] + w)
                        ch.did(vec.tensor_tensor(work[:, k0:k1, c0:c0 + w], src[:, k0:k1, ga],
                                                 inv_count[:, g, j0:j0 + w].unsqueeze(1).broadcast_to([P, kg, w]),
                                                 ALU.mult))
                    ch.wait()
                    for c0, w, s in STREAMS:
                        ga = slice(GAP_AT[s], GAP_AT[s] + w)
                        ins = vec.tensor_tensor(work[:, k0:k1, c0:c0 + w], work[:, k0:k1, c0:c0 + w],
                                                gapped[:, k0:k1, ga], ALU.subtract)
                        if s:
                            ins.then_inc(opnd_ready, kg)
                        else:
                            ch.did(ins)
                for m in range(KD):
                    low_operand(opnd["mix0"], m)

            def ffn_in(l):
                s = lin[f"ffn_in{l}"]
                more = l + 1 < DEPTH
                p0 = l * PAIRS

                def at(v, i):
                    return v if i is None else i * 4 + v

                def group(i, first=False, base=0):
                    for j in range(4):
                        c = s.conv0 + base + j
                        pair = p0 + (base + j) // 2
                        half = (lambda v: v) if i is None else (lambda v: i * 2 + v)
                        if i is not None or base + j + 1 < FFN_TILES:
                            low_part(s, base + j + 1, i, 4)
                        else:
                            low_next(s.n0 + base + j + 1)
                        b = tile_bank[(s.t0 + base + j) % BANKS]
                        k = bass.ds(at(base + j, i), 1)
                        tap = [taps[:, l, k, q:q + 1].rearrange("p a b -> p (a b)") for q in (0, 2)]
                        vec.wait_ge(acc_ready, at(c + 1, i))
                        vec.scalar_tensor_tensor(out=acc[:, c % 4, 1:COLS], in0=b[:, 0:COLS - 1], scalar=tap[0],
                                                 in1=acc[:, c % 4, 1:COLS], op0=ALU.mult, op1=ALU.add).then_inc(tap_first, 1)
                        if j % 2 == 0 and not (first and j == 0):
                            vec.wait_ge(g_hi_ready, half(pair))
                            q = bass.ds(half(pair - p0 - 1), 1)
                            vec.tensor_tensor(g_lo[:, q, :].rearrange("p a n -> p (a n)"), gate[:, (pair - 1) % 2, :],
                                              g_hi[:, q, :].bitcast(F32).rearrange("p a n -> p (a n)"),
                                              ALU.subtract).then_inc(g_lo_ready, 1)
                        vec.wait_ge(tap_first, at(c + 1, i))
                        vec.scalar_tensor_tensor(out=acc[:, c % 4, 0:COLS - 1], in0=b[:, 1:COLS], scalar=tap[1],
                                                 in1=acc[:, c % 4, 0:COLS - 1], op0=ALU.mult, op1=ALU.add
                                                 ).then_inc(conv_done, 1)
                        if j % 2:
                            if more:
                                mod_column(l + 1, base // 2 + j // 2, i, 2)
                            vec.wait_ge(sil_ready, half(pair + 1))
                            vec.wait_ge(conv_done, at(4 + c + 1, i))
                            vec.tensor_tensor(gate[:, pair % 2, :], sil[:, pair % 2, :], acc[:, c % 4, :],
                                              ALU.mult).then_inc(gate_ready, 1)

                group(None, first=True)
                with vec.Fori(0, FFN_TILES // 4 - 2) as i:
                    group(i, base=4)
                group(None, base=FFN_TILES - 4)
                vec.wait_ge(g_hi_ready, p0 + PAIRS)
                vec.tensor_tensor(g_lo[:, PAIRS - 1, :], gate[:, (p0 + PAIRS - 1) % 2, :],
                                  g_hi[:, PAIRS - 1, :].bitcast(F32), ALU.subtract).then_inc(g_lo_ready, 1)
                if more:
                    mod_column(l + 1, MOD_PIECES - 2)
                    mod_column(l + 1, MOD_PIECES - 1)

            def ssd_conv():
                s = lin["ssd_conv"]

                def tile(base, j, i):
                    at = (lambda v: v) if i is None else (lambda v: i * 4 + v)
                    t, c = base + j, s.conv0 + base + j
                    if i is not None or t + 1 < s.chunks:
                        low_part(s, t + 1, i, 4)
                    else:
                        low_next(s.n0 + t + 1)
                    b = tile_bank[(s.t0 + t) % BANKS]
                    k = bass.ds(at(t), 1)
                    tap = [ssd_taps[:, k, q:q + 1].rearrange("p a b -> p (a b)") for q in (0, 2)]
                    left = xbc[:, k, 1:COLS].rearrange("p a n -> p (a n)")
                    right = xbc[:, k, 0:COLS - 1].rearrange("p a n -> p (a n)")
                    vec.wait_ge(acc_ready, at(c + 1))
                    vec.scalar_tensor_tensor(out=left, in0=b[:, 0:COLS - 1], scalar=tap[0], in1=left,
                                             op0=ALU.mult, op1=ALU.add).then_inc(tap_first, 1)
                    vec.wait_ge(tap_first, at(c + 1))
                    vec.scalar_tensor_tensor(out=right, in0=b[:, 1:COLS], scalar=tap[1], in1=right,
                                             op0=ALU.mult, op1=ALU.add).then_inc(conv_done, 1)

                for j in range(4):
                    tile(0, j, None)
                with vec.Fori(0, s.chunks // 4 - 2) as i:
                    for j in range(4):
                        tile(4, j, i)
                for j in range(4):
                    tile(s.chunks - 4, j, None)
                lows_of(lin["ssd_z"])
                lows_of(lin["ssd_dt"])

            def dt_prepare():
                n = [0]

                def link(ins):
                    n[0] += 1
                    ins.then_inc(z_dt, 1)
                    vec.wait_ge(z_dt, n[0])

                v, mag, e, r = (sq[:, j, 0:192] for j in (1, 2, 3, 0))
                q = sq[:, 1, 192:384]
                v3 = v.rearrange("p (c h) -> p c h", c=3)
                vec.wait_ge(dt_pe, 1)
                link(vec.tensor_tensor(v3, stat_bank[:, 0:192].rearrange("p (c h) -> p c h", c=3),
                                       dt_rows[:, 0, :].unsqueeze(1).broadcast_to([P, 3, NDT]), ALU.add))
                link(vec.tensor_scalar(mag, v, -1.0, None, ALU.mult))
                link(vec.tensor_tensor(mag, mag, v, ALU.max))
                vec.wait_ge(dt_act, 2)
                link(vec.tensor_scalar(r, e, 2.0, None, ALU.add))
                link(vec.reciprocal(r, r))
                link(vec.tensor_tensor(r, r, e, ALU.mult))
                link(vec.tensor_tensor(mag, r, r, ALU.mult))
                link(vec.tensor_scalar(q, mag, 1.0 / 15, None, ALU.mult))
                for k in (13, 11, 9, 7, 5, 3):
                    link(vec.scalar_tensor_tensor(out=q, in0=q, scalar=1.0 / k, in1=mag, op0=ALU.add, op1=ALU.mult))
                link(vec.scalar_tensor_tensor(out=q, in0=q, scalar=1.0, in1=r, op0=ALU.add, op1=ALU.mult))
                link(vec.tensor_scalar(v, v, 0.0, None, ALU.max))
                flat_dt = dtv[:, :, :].rearrange("p c h -> p (c h)")
                link(vec.scalar_tensor_tensor(out=flat_dt, in0=q, scalar=2.0, in1=v, op0=ALU.mult, op1=ALU.add))
                link(vec.scalar_tensor_tensor(out=adt[:, :, :], in0=sq[:, 3, 192:256].unsqueeze(1).broadcast_to([P, 3, NDT]),
                                              scalar=-1.0, in1=dtv[:, :, :], op0=ALU.mult, op1=ALU.mult))
                assert n[0] == DT_DVE - 2
                vec.wait_ge(dt_pe, 2)
                cum = rstd_bank[:, 0:192].rearrange("p (c h) -> p c h", c=3)
                total = rstd_bank[:, 192:384].rearrange("p (c h) -> p c h", c=3)
                ch.did(vec.tensor_scalar(neg_cum[:, :, :], cum, -1.0, None, ALU.mult))
                ch.did(vec.tensor_copy(full_decay[:, :, :], total))
                ch.wait()
                link(vec.tensor_tensor(to_end[:, :, :], full_decay[:, :, :], neg_cum[:, :, :], ALU.add))
                vec.wait_ge(dt_act, 4)
                link(vec.tensor_tensor(to_end[:, :, :], to_end[:, :, :], dtv[:, :, :], ALU.mult))
                assert n[0] == DT_DVE

            def scan_dve():
                skip = ssd_cols[:, 0, :]
                ch.did(vec.tensor_tensor(skip, skip, ssd_cols[:, 1, :], ALU.add))
                ch.wait()

                def output(g, c, u):
                    vec.wait_ge(s_y, u + 1)
                    c0 = CHUNKS[c][0]
                    for t in range(2):
                        k = 2 * g + t
                        ins = vec.scalar_tensor_tensor(
                            out=xbc[:, k, c0:c0 + P], in0=xbc[:, k, c0:c0 + P], scalar=skip[:, k:k + 1],
                            in1=(mod_bank, col_bank)[u % 2][:, t * P:(t + 1) * P], op0=ALU.mult, op1=ALU.add)
                        if t:
                            ins.then_inc(s_out, 1)
                        else:
                            ch.did(ins)

                last = None
                for g, c, u, v in steps():
                    vec.wait_ge(s_copied, u + 1)
                    if u:
                        vec.wait_ge(s_w, 2 * u)
                    for d in range(2):
                        ch.did(vec.tensor_tensor(cb_mask[:, d, :], turned[:, u % 2, P + GW:], tri[:, d, :], ALU.mult))
                    masks = ch.n
                    if u >= 2:
                        vec.wait_ge(s_y, u - 1)
                    for d in range(2):
                        vec.wait_ge(s_cum, 2 * u + d + 1)
                        if c:
                            vec.wait_ge(s_cexp, 2 * v + d + 1)
                        for h in range(HPG):
                            col = d * SSD_HEADS + g * HPG + h
                            ins = vec.tensor_scalar(decay[:, u % 2, d, h * P:(h + 1) * P],
                                                    tile_bank[2 + d][:, h * P:(h + 1) * P],
                                                    neg_cum[:, c, col:col + 1], 0.0, ALU.add, ALU.min)
                            if h == HPG - 1:
                                ins.then_inc(s_seg, 1)
                            else:
                                ch.did(ins)
                    vec.wait_ge(s_state, u + 1)
                    if c == 0:
                        if g:
                            vec.wait_ge(state_stored, 16 * g)
                        vec.tensor_copy(state_new, stat_bank[:, :].rearrange("p (d n) -> p d n", d=2)).then_inc(s_taken, 1)
                    else:
                        d = c - 1
                        h0 = d * SSD_HEADS + g * HPG
                        if c == 1:
                            vec.wait_ge(state_loaded[g % 2], 16 * (g // 2 + 1))
                        if g:
                            vec.wait_ge(s_y, 3 * g)
                        n = ch.did(vec.tensor_tensor(
                            state1[:, d, :].rearrange("p (h q) -> p h q", h=HPG),
                            state0[:, g % 2, d, :].rearrange("p (h q) -> p h q", h=HPG),
                            full_decay[:, c, h0:h0 + HPG].unsqueeze(2).broadcast_to([P, HPG, HEAD]), ALU.mult))
                        ch.wait(n)
                        vec.tensor_tensor(state1[:, d, :], state1[:, d, :], stat_bank[:, d * GW:(d + 1) * GW],
                                          ALU.add).then_inc(s_taken, 1)
                    ch.wait(masks)
                    for d in range(2):
                        vec.wait_ge(s_exp, 2 * u + d + 1)
                        w = decay[:, u % 2, d, :].rearrange("p (h i) -> p h i", h=HPG)
                        vec.tensor_tensor(w, w, cb_mask[:, d, :].unsqueeze(1).broadcast_to([P, HPG, P]),
                                          ALU.mult).then_inc(s_w, 1)
                    if last is not None:
                        output(*last)
                    last = (g, c, u)
                output(*last)

            def ssd_norm():
                vec.wait_ge(s_out, 3 * GROUPS)
                for m in range(KI):
                    vec.tensor_tensor(xbc[:, m, :], xbc[:, m, :], zt[:, m, :], ALU.mult).then_inc(yz_ready, 1)
                take_rstd("ssd")
                e, base, k = norm["ssd"]
                vec.wait_ge(rstd_spread, e + 1)
                vec.wait_ge(yz_ready, KI)
                o = opnd["ssd_y"]
                for m in range(KI + 2):
                    if m < KI:
                        vec.scalar_tensor_tensor(out=xbc[:, m, :], in0=xbc[:, m, :], scalar=ssd_cols[:, 2, m:m + 1],
                                                 in1=rstd_bank[:, 0:COLS], op0=ALU.mult, op1=ALU.mult
                                                 ).then_inc(opnd_ready, 1)
                    if m >= 2:
                        vec.wait_ge(opnd_hi, o + m - 1)
                        vec.tensor_tensor(y_lo[:, m - 2, :], xbc[:, m - 2, :], y_hi[:, m - 2, :].bitcast(F32),
                                          ALU.subtract).then_inc(opnd_lo, 1)

            def conf_mix():
                vec.wait_ge(late_loaded, 16)
                n = 0

                def tap(m, k):
                    return 2 * TAPS31 * (m // 2) + 2 * k + m % 2

                for q in range(KD // 2):
                    for m in (2 * q, 2 * q + 1):
                        vec.wait_ge(glu_ready, 1 + 2 * m + 2)
                        vec.tensor_scalar(convolved[:, m, :], glu[:, m, 0:CONVOLVED],
                                          conf_tab[:, m * TAPS31:m * TAPS31 + 1],
                                          conf_tab[:, C_DWB + m:C_DWB + m + 1], ALU.mult, ALU.add).then_inc(conf_tap, 1)
                    with vec.Fori(0, (TAPS31 - 1) // 3) as i:
                        for r in range(3):
                            for m in (2 * q, 2 * q + 1):
                                vec.wait_ge(conf_tap, i * 6 + (tap(m, r) + 1))
                                vec.scalar_tensor_tensor(
                                    out=convolved[:, m, :], in0=glu[:, m, bass.ds(i * 3 + (1 + r), CONVOLVED)],
                                    scalar=conf_tab[:, bass.ds(i * 3 + (m * TAPS31 + 1 + r), 1)],
                                    in1=convolved[:, m, :], op0=ALU.mult, op1=ALU.add).then_inc(conf_tap, 1)
                vec.wait_ge(ln_sums, 1)
                vec.tensor_copy(ln_mean[:, :], stat_bank[:, 0:3]).then_inc(ln_mean_ready, 1)
                vec.wait_ge(ln_spread, 1)
                vec.wait_ge(conf_tap, KD * TAPS31)
                for m in range(KD):
                    for c0, w, k in STREAMS:
                        ins = vec.tensor_tensor(work[:, m, c0:c0 + w], convolved[:, m, CONVOLVED_AT[k]:CONVOLVED_AT[k] + w],
                                                rstd_bank[:, c0:c0 + w], ALU.subtract)
                        if k:
                            ins.then_inc(ln_centred, 1)
                        else:
                            ch.did(ins)
                take_rstd("ln")
                vec.wait_ge(rstd_spread, norm["ln"][0] + 1)
                vec.wait_ge(ln_centred, KD)
                ch.wait()
                for m in range(KD):
                    vec.tensor_tensor(work[:, m, :], work[:, m, :], rstd_bank[:, 0:COLS], ALU.mult).then_inc(ln_scaled, 1)
                for m in range(KD):
                    low_operand(opnd["mid2"], m)

            def attn_mix():
                lows_of(lin["qkv"])
                vec.wait_ge(late_loaded, 48)
                vec.wait_ge(qk_std_ready, 1)
                vec.reciprocal(qk_rstd[:, :], qk_std[:, :]).then_inc(qk_rstd_ready, 1)

                def rotate(t):
                    vec.wait_ge(qk_rot, t + 1)
                    if t >= 2:
                        vec.wait_ge(qk_turned, t - 1)
                    vec.tensor_tensor(rot_sin[:, t % 2, :], tile_bank[t % 2][:, 0:LAT], attn_tab[:, A_SIN:A_SIN + LAT],
                                      ALU.mult).then_inc(qk_sin, 1)
                    to = q_turned[:, t, :] if t < AH else k_all[:, t - AH, PAST:]
                    vec.wait_ge(qk_cos, t + 1)
                    vec.wait_ge(qk_sin, t + 1)
                    vec.tensor_tensor(to, to, rot_sin[:, t % 2, :], ALU.add).then_inc(qk_turned, 1)

                for t in range(QK + 1):
                    if t < QK:
                        g = A_G + (t >= AH)
                        vec.wait_ge(qk_spread, t + 1)
                        vec.scalar_tensor_tensor(out=qkv[:, t, :], in0=qkv[:, t, :], scalar=attn_tab[:, g:g + 1],
                                                 in1=(rstd_bank, mod_bank)[t % 2][:, 0:COLS], op0=ALU.mult,
                                                 op1=ALU.mult).then_inc(qk_normed, 1)
                    if t:
                        rotate(t - 1)
                o = opnd["mid3"]
                for u in range(3 * AH + 1):
                    if u < 3 * AH:
                        w = P if u % 3 == 0 else PAST + LAT
                        vec.wait_ge(att_score, u + 1)
                        if u >= 2:
                            vec.wait_ge(att_max, u - 1)
                        vec.tensor_reduce(row_max[:, u % 2:u % 2 + 1], tile_bank[u % 2][:, 0:w], AX.X, ALU.max
                                          ).then_inc(att_rowmax, 1)
                        vec.wait_ge(att_rowmax, u + 1)
                        if u >= 2:
                            vec.wait_ge(att_exp, u - 1)
                        vec.tensor_scalar(neg_max[:, u % 2:u % 2 + 1], row_max[:, u % 2:u % 2 + 1], -SCALE, None,
                                          ALU.mult).then_inc(att_max, 1)
                    if u:
                        b = u - 1
                        w = P if b % 3 == 0 else PAST + LAT
                        vec.wait_ge(att_exp, b + 1)
                        if b >= 2:
                            vec.wait_ge(att_prob, b - 1)
                        vec.reciprocal(inv_sum[:, b % 2:b % 2 + 1], row_sum[:, b % 2:b % 2 + 1]).then_inc(att_inv, 1)
                        vec.wait_ge(att_inv, b + 1)
                        vec.tensor_scalar(prob[:, b % 2, 0:w], prob[:, b % 2, 0:w], inv_sum[:, b % 2:b % 2 + 1], None,
                                          ALU.mult).then_inc(att_prob, 1)
                for h in range(AH):
                    low_operand(o, h)

            def lows_of(s):
                for j in range(s.chunks):
                    low_next(s.n0 + j + 1)

            vec.memset(cond32[:, :, :], 0.0).then_inc(vec_init, 1)
            vec.memset(work[:, :, :], 0.0).then_inc(vec_init, 1)
            vec.memset(gapped[:, :, :], 0.0).then_inc(vec_init, 1)
            vec.memset(spare[:, 3:4], 0.0).then_inc(w_low_dve, RAW_SLOTS)
            vec.memset(spare[:, 0:1], 0.0).then_inc(conv_done, 4)
            vec.memset(spare[:, 1:2], 0.0).then_inc(mod_done, 2)
            vec.wait_ge(loaded0, LOADS0)
            vec.wait_ge(vec_init, 3)
            vec.wait_ge(consts, CONSTS)
            vec.memset(spare[:, 2:3], 0.0).then_inc(x_ready, KD)
            with vec.Fori(0, MOD_PIECES // 2) as i:
                for j in range(2):
                    mod_column(0, j, i, 2)
            coefficients(0)
            low_next(0)
            take_rstd("pre0.0")
            modulate(0, "pre0.0", 0, 0, "mix0", to_gapped=True)
            pool_mix()
            for l in range(DEPTH):
                if l:
                    coefficients(l)
                if l == 0:
                    low_next(1)
                    low_next(2)
                    s = lin["pool"]
                if l == 1:
                    take_rstd("pre1.0")
                    modulate(1, "pre1.0", 0, KD * 2, "mix1")
                    ssd_conv()
                    dt_prepare()
                    scan_dve()
                    ssd_norm()
                    lows_of(lin["ssd_out"])
                if l == 2:
                    vec.memset(spare[:, 7:8], 0.0).then_inc(
                        w_low_dve, sum(lin[name].chunks for name in linears(2)))
                    take_rstd("pre2.0")
                    modulate(2, "pre2.0", 0, KD * 4, "mix2")
                    conf_mix()
                    low_next(lin["conf_out"].n0 + KD)
                if l == 3:
                    take_rstd("pre3.0")
                    modulate(3, "pre3.0", 0, KD * 6, "mix3")
                    attn_mix()
                    lows_of(lin["attn_out"])
                s = lin[linears(l)[-1]]
                take_rstd(f"post{l}.0")
                residual(f"post{l}.0", 0, 4 + s.evac0 + KD)
                take_rstd(f"pre{l}.1")
                modulate(l, f"pre{l}.1", 1, KD * (2 * l + 2) - KD, f"ffn{l}")
                ffn_in(l)
                s = lin[f"ffn_out{l}"]
                lows_of(s)
                take_rstd(f"post{l}.1")
                residual(f"post{l}.1", 1, 4 + s.evac0 + KD)

        @block.tensor
        def _(ten):
            ch = Chain(ten, pe)

            def products(bank_ap, hi, lo, w_tile, n, first, last):
                w = (w_hi[:, n % SPLIT_SLOTS, w_tile * P:(w_tile + 1) * P],
                     w_lo[:, n % SPLIT_SLOTS, w_tile * P:(w_tile + 1) * P])
                ten.matmul(bank_ap, w[0], hi, start=first, stop=False)
                ten.matmul(bank_ap, w[0], lo, start=False, stop=False)
                return ten.matmul(bank_ap, w[1], hi, start=False, stop=last)

            def chunk_ready(n, i=None, per=0):
                ready = RAW_SLOTS + n + 1
                ten.wait_ge(w_low_pool, ready if i is None else i * per + ready)
                ten.wait_ge(w_low_dve, ready if i is None else i * per + ready)

            def mod_rows_of(l, piece, i=None, per=0):
                g = l * MOD_PIECES + piece
                at = (lambda v: v) if i is None else (lambda v: i * per + v)
                ten.wait_ge(mod_loaded[g % 2], 16 * (g // 2 + 1) + (0 if i is None else i * (8 * per)))
                ten.wait_ge(rows_ready, at(2 + g))
                for half in range(2):
                    for q in range(4):
                        k = 2 * q + half
                        ins = ten.matmul(mod_bank[32 * q:32 * q + 32, 0:MOD_COLS],
                                         cond32[:, k, :], mod_raw[:, g % 2, k * MOD_COLS:(k + 1) * MOD_COLS],
                                         start=half == 0, stop=half == 1, skip_group_check=True)
                ins.then_inc(mod_used, 1)

            def mod_columns_of(l, piece, i=None, per=0):
                g = l * MOD_PIECES + piece
                at = (lambda v: v) if i is None else (lambda v: i * per + v)
                ten.wait_ge(rows_ready, at(2 + g + 1))
                ten.wait_ge(mod_done, at(2 + g))
                for t in range(MOD_TILES):
                    c = 2 * t
                    ins = ten.matmul(col_bank[:, c:c + 2], mod_rows[:, g % 2, t * P:(t + 1) * P], cond_sel[:, :],
                                     start=True, stop=True, skip_group_check=True)
                ins.then_inc(cols_ready, 1)

            def column_sums(base, m, i=None, per=0, first=False, col=0):
                ten.wait_ge(sq_ready, base + m + 1 if i is None else i * per + (base + m + 1))
                for c, (c0, s) in enumerate(CHUNKS):
                    ins = ten.matmul(stat_bank[:, c:c + 1], sq[:, (base + m) % 4, c0:c0 + P], mean_col[:, col:col + 1],
                                     start=first and c == 0, stop=True, skip_group_check=True)
                ins.then_inc(sq_used, 1)

            def spread_columns(b, src, at):
                for c, (c0, s) in enumerate(CHUNKS):
                    w = P if c == 1 else P + 1
                    ins = ten.matmul(b[:, c0:c0 + w], src[:, at + c:at + c + 1].broadcast_to([P, P]), ident[:, 0:w],
                                     start=c == 0, stop=True, skip_group_check=True)
                return ins

            def spread(name):
                e, base, k = norm[name]
                ten.wait_ge(rstd_ready, e + 1)
                spread_columns(rstd_bank, rstd, 0).then_inc(rstd_spread, 1)

            def norm_of_x(name):
                e, base, k = norm[name]
                for m in range(k):
                    column_sums(base, m, first=m == 0)
                spread(name)

            def ffn_in(l):
                s = lin[f"ffn_in{l}"]
                more = l + 1 < DEPTH
                o = opnd[f"ffn{l}"]
                with ten.Fori(0, FFN_TILES // 4) as i:
                    for j in range(4):
                        chunk_ready(s.n0 + j, i, 4)
                        ten.wait_ge(conv_done, i * 4 + (s.conv0 + j + 1))
                        b = tile_bank[(s.t0 + j) % BANKS][:, 0:COLS]
                        for k in range(KD):
                            if j == 0:
                                ten.wait_ge(opnd_lo, o + k + 1)
                            ins = products(b, h_hi[:, k, :], h_lo[:, k, :], k, s.n0 + j, k == 0, k == KD - 1)
                        ins.then_inc(w_used, 1)
                        if more and j % 2:
                            mod_rows_of(l + 1, j // 2, i, 2)
                        if more and j == 2:
                            mod_columns_of(l + 1, 0, i, 2)
                    if more:
                        mod_columns_of(l + 1, 1, i, 2)
                if more:
                    for q in (2, 1):
                        mod_rows_of(l + 1, MOD_PIECES - q)
                        mod_columns_of(l + 1, MOD_PIECES - q)

            def out_product(s, hi, lo, name, before, g_ready=None):
                e, base, _ = norm[name]
                with ten.Fori(0, 2) as i:
                    for m in range(4):
                        before(m)
                        ten.wait_ge(evac, i * 4 + (s.evac0 + m + 1))
                        b = tile_bank[(s.t0 + m) % BANKS][:, 0:COLS]
                        for half in range(s.per):
                            n = s.n0 + s.per * m + half
                            chunk_ready(n, i, 4 * s.per)
                            for k in range(s.tiles):
                                kk = half * s.tiles + k
                                if m == 0 and g_ready is not None:
                                    g_ready(kk)
                                ins = products(b, hi[:, kk, :], lo[:, kk, :], k, n, kk == 0, kk == s.per * s.tiles - 1)
                            ins.then_inc(w_used, 1)
                        if m == 0:
                            continue
                        column_sums(base, m - 1, i, 4)
                    column_sums(base, 3, i, 4)
                spread(name)

            def plain_product(s, name, before):
                o = opnd[name]

                def tile(j, i=None):
                    chunk_ready(s.n0 + j, i, 4)
                    before(j, i)
                    b = tile_bank[(s.t0 + j) % BANKS][0:s.width, 0:COLS]
                    for k in range(KD):
                        if j == 0:
                            ten.wait_ge(opnd_lo, o + k + 1)
                        w = s.width
                        wh = w_hi[:, (s.n0 + j) % SPLIT_SLOTS, k * w:(k + 1) * w]
                        wl = w_lo[:, (s.n0 + j) % SPLIT_SLOTS, k * w:(k + 1) * w]
                        ten.matmul(b, wh, h_hi[:, k, :], start=k == 0, stop=False)
                        ten.matmul(b, wh, h_lo[:, k, :], start=False, stop=False)
                        ins = ten.matmul(b, wl, h_hi[:, k, :], start=False, stop=k == KD - 1)
                    ins.then_inc(w_used, 1)

                if s.chunks >= 8:
                    with ten.Fori(0, s.chunks // 4) as i:
                        for j in range(4):
                            tile(j, i)
                else:
                    for j in range(s.chunks):
                        tile(j)

            def dt_prepare():
                s = lin["ssd_dt"]
                ten.wait_ge(evac, 4 + s.evac0 + 1)
                for c, (c0, _) in enumerate(CHUNKS):
                    ins = ten.transpose(stat_bank[:, c * NDT:(c + 1) * NDT], sq[0:NDT, 0, c0:c0 + P],
                                        ident[0:NDT, 0:NDT])
                ins.then_inc(dt_pe, 1)
                ten.wait_ge(z_dt, DT_DVE - 2)
                cum = rstd_bank[:, 0:192].rearrange("p (c h) -> p c h", c=3)
                for d in range(2):
                    hs = slice(d * SSD_HEADS, (d + 1) * SSD_HEADS)
                    ten.matmul(cum[:, :, hs], tri[:, d, :], adt[:, :, hs], start=True, stop=True, skip_group_check=True)
                ten.matmul(rstd_bank[:, 192:384], ones[:, :], adt[:, :, :].rearrange("p c h -> p (c h)"),
                           start=True, stop=True, skip_group_check=True).then_inc(dt_pe, 1)

            def scan_pe():
                def output(g, c, u, v):
                    if u >= 2:
                        ten.wait_ge(s_out, u - 1)
                    ten.wait_ge(s_w, 2 * u + 2)
                    ten.wait_ge(s_xdt, 2 * u + 2)
                    if c:
                        ten.wait_ge(s_cs, 2 * v + 2)
                        ten.wait_ge(s_taken, 3 * g + 3)
                        ten.wait_ge(state_loaded[g % 2], 16 * (g // 2 + 1))
                    b = (mod_bank, col_bank)[u % 2]
                    for h in range(HPG):
                        o = b[HEAD * (h % 2):HEAD * (h % 2 + 1), h // 2 * P:(h // 2 + 1) * P]
                        hs, ws = slice(h * HEAD, (h + 1) * HEAD), slice(h * P, (h + 1) * P)
                        terms = [(x_dt[:, u % 2, d, hs], decay[:, u % 2, d, ws]) for d in range(2)]
                        if c:
                            for d in range(2):
                                st = state0[:, g % 2, d, hs] if d == c - 1 else state1[:, d, hs]
                                terms.append((st, c_scaled[:, u % 2, d, ws]))
                        for n, (lhs, rhs) in enumerate(terms):
                            ins = ten.matmul(o, lhs, rhs, start=n == 0, stop=n == len(terms) - 1)
                    ins.then_inc(s_y, 1)

                last = None
                ten.wait_ge(xbc_ready, SSD_CONV_TILES)
                ten.wait_ge(z_dt, DT_DVE)
                for g, c, u, v in steps():
                    c0 = CHUNKS[c][0]
                    if u >= 2:
                        ten.wait_ge(s_copied, u - 1)
                    b = tile_bank[u % 2]
                    cols = slice(c0, c0 + P)
                    ten.transpose(b[:, 0:P], xbc[:, KI + g, cols], ident[:, 0:P])
                    for t in range(2):
                        ten.transpose(b[:, (t + 1) * P:(t + 2) * P], xbc[:, 2 * g + t, cols], ident[:, 0:P])
                    ten.matmul(b[:, 3 * P:], xbc[:, KI + g, cols], xbc[:, KI + GROUPS + g, cols],
                               start=True, stop=True).then_inc(s_turned, 1)
                    for d in range(2):
                        if u:
                            ten.wait_ge(s_seg, 2 * (u - 1) + d + 1)
                        for h in range(HPG):
                            col = d * SSD_HEADS + g * HPG + h
                            ins = ten.matmul(tile_bank[2 + d][:, h * P:(h + 1) * P],
                                             adt[:, c, col:col + 1].broadcast_to([P, P]), tri[:, d, :],
                                             start=True, stop=True, skip_group_check=True)
                        ins.then_inc(s_cum, 1)
                    ten.wait_ge(s_copied, u + 1)
                    ten.wait_ge(s_xend, u + 1)
                    if u:
                        ten.wait_ge(s_taken, u)
                    for d in state_dirs(c):
                        ins = ten.matmul(stat_bank[:, d * GW:(d + 1) * GW], turned[:, u % 2, 0:P], x_end[:, d, :],
                                         start=True, stop=True, skip_group_check=True)
                    ins.then_inc(s_state, 1)
                    if last is not None:
                        output(*last)
                    last = (g, c, u, v)
                output(*last)

            def conf_norm_pe():
                for m in range(KD):
                    if m % 2 == 0:
                        ten.wait_ge(conf_tap, 2 * TAPS31 * (m // 2 + 1))
                    for c, (c0, s) in enumerate(CHUNKS):
                        at = c0 - (LAT0 if s else 0) + CONVOLVED_AT[s]
                        ins = ten.matmul(stat_bank[:, c:c + 1], convolved[:, m, at:at + P], mean_col[:, 0:1],
                                         start=m == 0 and c == 0, stop=True, skip_group_check=True)
                ins.then_inc(ln_sums, 1)
                ten.wait_ge(ln_mean_ready, 1)
                spread_columns(rstd_bank, ln_mean, 0).then_inc(ln_spread, 1)
                norm_of_x("ln")

            def attn_pe():
                s = lin["qkv"]
                ten.wait_ge(evac, 4 + s.evac0 + s.chunks)
                e, base, _ = norm["qk"]
                for kv in range(AKV):
                    for c, (c0, _) in enumerate(CHUNKS):
                        ins = ten.transpose(tile_bank[2 + kv][:, c * AD:(c + 1) * AD], qkv[:, QK + kv, c0:c0 + P],
                                            ident[:, 0:P])
                    ins.then_inc(v_turned, 1)
                for t in range(QK):
                    ten.wait_ge(sq_ready, base + t + 1)
                    for c, (c0, _) in enumerate(CHUNKS):
                        ins = ten.matmul(stat_bank[:, 3 * t + c:3 * t + c + 1], sq[:, (base + t) % 4, c0:c0 + P],
                                         mean_col[:, 2:3], start=True, stop=True, skip_group_check=True)
                    ins.then_inc(sq_used, 1)
                ten.wait_ge(qk_rstd_ready, 1)
                ten.wait_ge(late_loaded, 48)
                for t in range(QK + 1):
                    if t < QK:
                        if t >= 2:
                            ten.wait_ge(qk_normed, t - 1)
                        spread_columns((rstd_bank, mod_bank)[t % 2], qk_rstd, 3 * t).then_inc(qk_spread, 1)
                    if t:
                        r = t - 1
                        ten.wait_ge(qk_normed, r + 1)
                        if r >= 2:
                            ten.wait_ge(qk_sin, r - 1)
                        ten.matmul(tile_bank[r % 2][:, 0:LAT], attn_tab[:, A_PERM:A_PERM + AD],
                                   qkv[:, r, LAT0:LAT0 + LAT], start=True, stop=True).then_inc(qk_rot, 1)
                ten.wait_ge(qk_turned, QK)
                ten.wait_ge(v_copied, AKV)

                def scores(h, c, u):
                    if u >= 2:
                        ten.wait_ge(att_exp, u - 1)
                    kv = h // REP
                    q = q_turned[:, h, (c - 1) * P:c * P] if c else qkv[:, h, 0:CTX]
                    keys = k_all[:, kv, :] if c else qkv[:, AH + kv, 0:CTX]
                    ten.matmul(tile_bank[u % 2][:, 0:PAST + LAT if c else CTX], q, keys, start=True, stop=True
                               ).then_inc(att_score, 1)

                def turn(h, c, u):
                    ten.wait_ge(att_prob, u + 1)
                    if u >= 2:
                        ten.wait_ge(att_pt, u - 1)
                    for k in range(3 if c else 1):
                        ins = ten.transpose(tile_bank[2 + u % 2][:, k * P:(k + 1) * P], prob[:, u % 2, k * P:(k + 1) * P],
                                            ident[:, 0:P])
                    ins.then_inc(att_turned, 1)

                def values(h, c, u):
                    ten.wait_ge(att_pt, u + 1)
                    if u >= 2:
                        copied_out(ten, u - 2)
                    kv = h // REP
                    own = v_rows[:, kv, :]
                    if c:
                        v = [attn_tab[:, A_V + kv * AD:A_V + (kv + 1) * AD], own[:, AD:2 * AD], own[:, 2 * AD:]]
                    else:
                        v = [own[:, 0:AD]]
                    for k, rows in enumerate(v):
                        ins = ten.matmul((mod_bank, col_bank)[u % 2][:, 0:P], rows, prob_t[:, u % 2, k * P:(k + 1) * P],
                                         start=k == 0, stop=k == len(v) - 1)
                    ins.then_inc(att_pv, 1)

                every = list(units())
                for n in range(len(every) + 3):
                    if n < len(every):
                        scores(*every[n])
                    if 2 <= n < len(every) + 2:
                        turn(*every[n - 2])
                    if n >= 3:
                        values(*every[n - 3])

            def clear_stats():
                ten.matmul(stat_bank[:, 0:3], ident[:, 0:P], ident[:, P + 1:P + 4], start=True, stop=True,
                           skip_group_check=True)

            ten.wait_ge(cond_ready, 1)
            ten.wait_ge(consts, CONSTS)
            ten.matmul(mod_bank[:, 0:1], ident[:, 0:P], ident[:, P:P + 1], start=True, stop=True).then_inc(cols_ready, 2)
            with ten.Fori(0, MOD_PIECES // 2) as i:
                for j in range(2):
                    mod_rows_of(0, j, i, 2)
                    mod_columns_of(0, j, i, 2)
            norm_of_x("pre0.0")
            for l in range(DEPTH):
                if l == 0:
                    s = lin["pool"]
                    e, base, _ = norm["post0.0"]
                    for m in range(KD):
                        n = s.n0 + m // 4
                        chunk_ready(n)
                        group = m // 2
                        if m >= 4:
                            ten.wait_ge(evac, 1 + m)
                        ten.wait_ge(opnd_lo, opnd["mix0"] + 2 * group + 2)
                        for k in range(2):
                            ins = products(tile_bank[(s.t0 + m) % BANKS][:, 0:COLS], h_hi[:, 2 * group + k, :],
                                           h_lo[:, 2 * group + k, :], (m % 4) * 2 + k, n, k == 0, k == 1)
                        if m % 4 == 3:
                            ins.then_inc(w_used, 1)
                        if m % 4 != 3:
                            ch.did(ins)
                        if m:
                            column_sums(base, m - 1, first=m == 1)
                    column_sums(base, KD - 1)
                    spread("post0.0")
                if l == 1:
                    conv, z, dt = lin["ssd_conv"], lin["ssd_z"], lin["ssd_dt"]
                    plain_product(conv, "mix1", lambda j, i: ten.wait_ge(conv_done, i * 4 + (conv.conv0 + j + 1)))

                    def z_before(j, i):
                        ten.wait_ge(conv_done, conv.conv0 + SSD_CONV_TILES + j + 1)
                        ten.wait_ge(evac, i * 4 + (z.evac0 + j + 1))

                    plain_product(z, "mix1", z_before)
                    plain_product(dt, "mix1", lambda j, i: ten.wait_ge(evac, dt.evac0 + 1))
                    dt_prepare()
                    scan_pe()
                    e, base, k = norm["ssd"]
                    for m in range(k):
                        column_sums(base, m, first=m == 0, col=1)
                    spread("ssd")
                    clear_stats()
                    out_product(lin["ssd_out"], y_hi, y_lo, "post1.0", lambda m: None,
                                lambda k: ten.wait_ge(opnd_lo, opnd["ssd_y"] + k + 1))
                if l == 2:
                    s = lin["conf_in"]
                    plain_product(s, "mix2", lambda j, i, s=s: ten.wait_ge(evac, i * 4 + (s.evac0 + j + 1)))
                    conf_norm_pe()
                    clear_stats()
                    out_product(lin["conf_out"], h_hi, h_lo, "post2.0", lambda m: None,
                                lambda k: ten.wait_ge(opnd_lo, opnd["mid2"] + k + 1))
                if l == 3:
                    s = lin["qkv"]
                    plain_product(s, "mix3", lambda j, i, s=s: ten.wait_ge(evac, i * 4 + (s.evac0 + j + 1)))
                    attn_pe()
                    clear_stats()
                    out_product(lin["attn_out"], h_hi, h_lo, "post3.0", lambda m: None,
                                lambda k: ten.wait_ge(opnd_lo, opnd["mid3"] + k + 1))
                norm_of_x(f"pre{l}.1")
                ffn_in(l)
                s = lin[f"ffn_in{l}"]
                clear_stats()
                out_product(lin[f"ffn_out{l}"], g_hi, g_lo, f"post{l}.1",
                            lambda m, s=s: ten.wait_ge(conv_done, s.conv0 + FFN_TILES + m + 1),
                            lambda k, l=l: ten.wait_ge(g_lo_ready, l * PAIRS + k + 1))
                if l + 1 < DEPTH:
                    norm_of_x(f"pre{l + 1}.0")


def columns(ctx_part, lat_part):
    out = np.zeros((P, KD, COLS), ctx_part.dtype)
    out[:, :, 0:CTX] = ctx_part.T.reshape(KD, P, CTX).transpose(1, 0, 2)
    out[:, :, LAT0:LAT0 + LAT] = lat_part.T.reshape(KD, P, LAT).transpose(1, 0, 2)
    return out


def tiles_of(w):
    k, m = w.shape
    return np.ascontiguousarray(w.reshape(k // P, P, m // P, P).transpose(2, 1, 0, 3)).reshape(m // P, P, k)


def per_partition(v, axis=-1):
    t = v.reshape(*v.shape[:-1], v.shape[-1] // P, P)
    return np.ascontiguousarray(np.moveaxis(t, -1, 0))


PAIRED = [t for p in range(PAIRS) for t in (p, PAIRS + p)]


def lay_out(i):
    d = {}
    d["x"] = columns(i["x_prompt"][0], i["x_sample"][0])
    d["cond"] = np.ascontiguousarray(np.stack([per_partition(i["c_ctx"]), per_partition(i["c"][0])], -1))
    d["gains"] = per_partition(i["norm_g"])
    d["b_mod"] = per_partition(i["b_mod"])
    d["pool_scale"] = per_partition(i["pool_scale"][0])
    d["taps"] = np.ascontiguousarray(np.stack(
        [per_partition(v)[:, :, PAIRED] for v in (i["ffn_dw"][:, 0], i["ffn_dw"][:, 1], i["ffn_dw"][:, 2], i["ffn_dw_b"])], -1))
    inv = np.ones((len(WINDOWS), CTX + LAT), np.float32)
    for g, win in enumerate(WINDOWS):
        at = 0
        for n in (CTX, LAT):
            t = np.arange(n)
            inv[g, at:at + n] = 1.0 / (np.minimum(t + win - win // 2, n) - np.maximum(t - win // 2, 0))
            at += n
    d["inv_count"] = np.broadcast_to(inv, (P, len(WINDOWS), CTX + LAT)).copy()
    d["w_mod"] = np.ascontiguousarray(
        i["w_mod"].reshape(DEPTH, KD, P, MOD_PIECES, MOD_COLS).transpose(0, 3, 2, 1, 4)
    ).reshape(DEPTH * MOD_PIECES, P, KD * MOD_COLS)
    pw = i["pool_w"][0].reshape(2, 2, 2, P, 2, P)
    d["pool"] = np.ascontiguousarray(pw.transpose(0, 3, 1, 4, 2, 5)).reshape(2, P, D)
    w = i["ssd_w_in"][0]
    d["ssd_conv"] = tiles_of(w[:, INNER:INNER + SSD_CONV_TILES * P])
    d["ssd_z"] = tiles_of(w[:, 0:INNER])
    d["ssd_dt"] = np.ascontiguousarray(
        w[:, INNER + SSD_CONV_TILES * P:].reshape(KD, P, NDT).transpose(1, 0, 2)).reshape(1, P, KD * NDT)
    d["ssd_out"] = np.ascontiguousarray(
        tiles_of(i["ssd_w_out"][0]).reshape(KD, P, 2, D).transpose(0, 2, 1, 3)).reshape(2 * KD, P, D)
    d["ssd_taps"] = np.ascontiguousarray(np.stack([per_partition(v) for v in (*i["ssd_conv_w"][0], i["ssd_conv_b"][0])], -1))
    d["dt_rows"] = np.broadcast_to(np.stack([i["ssd_dt_bias"][0].reshape(-1), i["ssd_a_log"][0].reshape(-1)]), (P, 2, NDT)).copy()
    d["ssd_cols"] = np.ascontiguousarray(np.stack(
        [*(per_partition(np.repeat(v, HEAD)) for v in i["ssd_d"][0]), per_partition(i["ssd_norm_g"][0])], 1))
    d["state_in"] = np.ascontiguousarray(i["state_ssd"][0, 0].transpose(3, 0, 1, 2)).reshape(P, 2, INNER)
    halves = [t for p in range(KD) for t in (p, KD + p)]
    d["conf_in"] = tiles_of(i["conf_w_in"][0])[halves]
    d["conf_out"] = tiles_of(i["conf_w_out"][0])
    d["conf_tab"] = np.concatenate(
        [per_partition(i["conf_dw"][0]).transpose(0, 2, 1).reshape(P, C_BIN), per_partition(i["conf_b_in"][0])[:, halves],
         *(per_partition(i["conf_" + n][0]) for n in ("dw_b", "ln_g", "ln_b", "b_out"))], 1)
    d["qkv"] = tiles_of(i["attn_w_qkv"][0])
    d["attn_out"] = tiles_of(i["attn_w_o"][0])
    n_freq = AD // 4
    inv_freq = np.float32(ROPE_THETA) ** (-np.arange(n_freq, dtype=np.float32) / np.float32(n_freq))
    t = np.arange(LAT)
    place = np.stack([t // GRID_W, t % GRID_W]).astype(np.float32)
    angle = np.broadcast_to((inv_freq[None, :, None] * place[:, None, :])[:, None], (2, 2, n_freq, LAT)).reshape(AD, LAT)
    perm = np.zeros((2, 2, n_freq, 2, 2, n_freq), np.float32)
    for axis in range(2):
        for f in range(n_freq):
            perm[axis, 1, f, axis, 0, f] = -1.0
            perm[axis, 0, f, axis, 1, f] = 1.0
    d["attn_tab"] = np.concatenate(
        [np.cos(angle), np.sin(angle), perm.reshape(AD, AD), i["attn_q_g"].T, i["attn_k_g"].T,
         i["cache_v"][0, 0].reshape(PAST, AKV * AD)], 1)
    d["cache_k"] = np.ascontiguousarray(i["cache_k"][0, 0].transpose(2, 1, 0))
    for l in range(DEPTH):
        d[f"ffn_in{l}"] = tiles_of(i["ffn_w_in"][l])[PAIRED]
        w = tiles_of(i["ffn_w_out"][l]).reshape(KD, P, 2, HALF * P)
        d[f"ffn_out{l}"] = np.ascontiguousarray(w.transpose(0, 2, 1, 3)).reshape(2 * KD, P, HALF * P)
    return d


OUTS = {"y": [P, KD, COLS], "state": [P, 2, INNER], "cache_k": [P, AKV, CTX], "cache_v": [P, AKV, CTX]}


def kernel(**inputs):
    import concourse.bacc as bacc
    from concourse.bass_utils import run_bass_kernel_spmd

    d = lay_out({k: np.asarray(v) for k, v in inputs.items()})
    nc = bacc.Bacc("TRN2", target_bir_lowering=False, num_devices=1)
    a = {k: nc.dram_tensor("in_" + k, list(v.shape), F32, kind="ExternalInput").ap() for k, v in d.items()}
    o = {k: nc.dram_tensor("out_" + k, v, F32, kind="ExternalOutput").ap() for k, v in OUTS.items()}
    build_trunk(nc, a, o)
    r = run_bass_kernel_spmd(nc, [{"in_" + k: v for k, v in d.items()}], core_ids=[0]).results[0]
    y = np.asarray(r["out_y"])
    tokens = [np.ascontiguousarray(y[:, :, c0:c0 + w].transpose(2, 1, 0)).reshape(1, w, D) for c0, w, _ in STREAMS]
    state = np.ascontiguousarray(np.asarray(r["out_state"]).transpose(1, 2, 0)).reshape(1, 1, 2, SSD_HEADS, HEAD, STATE)
    caches = [np.ascontiguousarray(np.asarray(r["out_" + n]).transpose(2, 1, 0)).reshape(1, 1, CTX, AKV, AD)
              for n in ("cache_k", "cache_v")]
    return (*tokens, state, *caches)
```

```python
from contextlib import ExitStack

import numpy as np

import concourse.bass as bass
from concourse import mybir

F32 = mybir.dt.float32
F32R = mybir.dt.float32r
ALU = mybir.AluOpType
ACT = mybir.ActivationFunctionType
AX = mybir.AxisListType

P = 128
D = 1024
KD = D // P
CTX, LAT = 128, 256
LAT0 = CTX + 1
COLS = CTX + 1 + LAT + 1
CHUNKS = [(0, 0), (LAT0, 1), (LAT0 + P, 1)]
STREAMS = [(0, CTX, 0), (LAT0, LAT, 1)]
EPS = 1e-6

DEPTH = 4
FFN = 2816
KF = FFN // P
PAIRS = KF
FFN_TILES = 2 * KF
HALF = KF // 2

WINDOWS = (2, 4, 8, 16)
EDGE = max(WINDOWS) // 2
GAPPED = EDGE + CTX + 2 * EDGE + LAT + EDGE
GAP_AT = [EDGE, EDGE + CTX + 2 * EDGE]

INNER = 2048
SSD_HEADS, HEAD = 32, 64
GROUPS, STATE = 8, 128
HPG = SSD_HEADS // GROUPS
GW = HPG * HEAD
KI = INNER // P
SSD_CONV_TILES = KI + 2 * GROUPS
NDT = 2 * SSD_HEADS

TAPS31 = 31
REACH = TAPS31 // 2
CGAP = REACH + CTX + REACH + LAT + REACH
CGAP_AT = [REACH, 2 * REACH + CTX]
CONVOLVED = CGAP - TAPS31 + 1
CONVOLVED_AT = [at - REACH for at in CGAP_AT]
C_BIN = KD * TAPS31
C_DWB, C_LNG, C_LNB, C_BOUT, C_ALL = (C_BIN + k * KD for k in (2, 3, 4, 5, 6))

AH, AKV, AD = 8, 2, 128
REP = AH // AKV
PAST = 128
SCALE = AD ** -0.5
QK = AH + AKV
GRID_W, ROPE_THETA = 64, 10000.0
A_COS, A_SIN, A_PERM, A_G, A_V, A_ALL = 0, LAT, 2 * LAT, 2 * LAT + AD, 2 * LAT + AD + 2, 2 * LAT + AD + 2 + AKV * AD

RAW_SLOTS, SPLIT_SLOTS, BANKS = 4, 2, 4
MOD_COLS = 256
MOD_PIECES = 6 * D // MOD_COLS
MOD_TILES = MOD_COLS // P
MOD_FIRST = 2 * D // MOD_COLS
MAXK = HALF


class Linear:

    def __init__(self, name, chunks, tiles, per, outs, width=P):
        self.name, self.chunks, self.tiles, self.per, self.outs, self.width = name, chunks, tiles, per, outs, width


def plan():
    lins = [Linear("pool", 2, KD, 1, 8)]
    for l in range(DEPTH):
        if l == 1:
            lins += [Linear("ssd_conv", SSD_CONV_TILES, KD, 1, SSD_CONV_TILES),
                     Linear("ssd_z", KI, KD, 1, KI), Linear("ssd_dt", 1, KD, 1, 1, NDT),
                     Linear("ssd_out", 2 * KD, KD, 2, KD)]
        if l == 2:
            lins += [Linear("conf_in", 2 * KD, KD, 1, 2 * KD), Linear("conf_out", KD, KD, 1, KD)]
        if l == 3:
            lins += [Linear("qkv", AH + 2 * AKV, KD, 1, AH + 2 * AKV), Linear("attn_out", KD, KD, 1, KD)]
        lins += [Linear(f"ffn_in{l}", FFN_TILES, KD, 1, FFN_TILES), Linear(f"ffn_out{l}", 2 * KD, HALF, 2, KD)]
    n = t = conv = evac = 0
    for x in lins:
        x.n0, x.t0, x.conv0, x.evac0 = n, t, conv, evac
        n += x.chunks
        t += x.outs
        if x.name.startswith("ffn_in") or x.name == "ssd_conv":
            conv += x.outs
        else:
            evac += x.outs
    return {x.name: x for x in lins}, lins



def norm_plan():
    order = []
    for l in range(DEPTH):
        order += [(f"pre{l}.0", KD)]
        if l == 1:
            order += [("ssd", KI)]
        if l == 2:
            order += [("ln", KD)]
        if l == 3:
            order += [("qk", AH + AKV)]
        order += [(f"post{l}.0", KD), (f"pre{l}.1", KD), (f"post{l}.1", KD)]
    out, base, event = {}, 0, 0
    for name, k in order:
        out[name] = (event, base, k)
        base += k
        event += name != "qk"
    return out


def operand_plan():
    out, base = {}, 0
    for l in range(DEPTH):
        for name, k in [(f"mix{l}", KD), *([("ssd_y", KI)] if l == 1 else []),
                        *([(f"mid{l}", KD)] if l in (2, 3) else []), (f"ffn{l}", KD)]:
            out[name] = base
            base += k
    return out


def sum_plan(norm):
    groups, freed = {}, []
    adds = sums = 0
    for name, (_, _, k) in norm.items():
        if name.startswith("post"):
            sizes = [KD - 1, 1]
        else:
            sizes = {"ssd": [3, 3, 3, 3, 2, 1, 1], "qk": [1] * k}.get(name, [2, 2, 2, 1, 1])
        mine, t = [], 0
        for size in sizes:
            for _ in range(size - 1):
                adds += 1
                freed.append(("added", adds))
            sums += 1
            freed.append(("used", sums))
            t += size
            mine.append((t - 1, size, adds))
        assert t == k
        groups[name] = (mine, sums)
    return groups, freed


def low_plan(opnd):
    shares = {"ssd_y": (KI, lambda k: k % 3 < 2), "mix0": (KD, lambda k: k < 6),
              "mid2": (KD, lambda k: False), "mid3": (KD, lambda k: False)}
    at, count = {}, {True: 0, False: 0}
    for name in opnd:
        k, pool = shares.get(name, (KD, lambda k: k % 4 < 3))
        at[name] = []
        for j in range(k):
            count[pool(j)] += 1
            at[name].append((pool(j), count[pool(j)]))
    return at


def build_trunk(nc, a, out):
    lin, order = plan()
    norm = norm_plan()
    sum_groups, slot_freed = sum_plan(norm)
    opnd = operand_plan()
    low_at = low_plan(opnd)

    with ExitStack() as ctx:
        def sb(name, shape, dt=F32, stack=ctx):
            return stack.enter_context(nc.sbuf_tensor(name, shape, dt))

        def bank(name, shape=(P, 512)):
            return ctx.enter_context(nc.psum_tensor(name, list(shape), F32))

        def sem(name):
            return ctx.enter_context(nc.semaphore(name))

        x = sb("x", [P, KD, COLS])
        work = sb("work", [P, KD, COLS])
        h_hi = sb("h_hi", [P, KD, COLS], F32R)
        h_lo = sb("h_lo", [P, KD, COLS], F32R)
        sq = sb("sq", [P, 4, COLS])
        raw = sb("raw", [P, RAW_SLOTS, MAXK * P])
        w_hi = sb("w_hi", [P, SPLIT_SLOTS, MAXK * P], F32R)
        w_lo = sb("w_lo", [P, SPLIT_SLOTS, MAXK * P], F32R)
        mean_col = sb("mean_col", [P, 3])
        ident = sb("ident", [P, P + 4])
        spare = sb("spare", [P, 8])
        eps_col = sb("eps_col", [P, 1])
        std = sb("std", [P, 3])
        rstd = sb("rstd", [P, 3])
        gated_bias = sb("gated_bias", [P, KD, 2])
        modc = sb("modc", [P, 2, 6 * KD, 2])
        coef = sb("coef", [P, 4, KD, 2])
        gains = sb("gains", [P, DEPTH, 4, KD])
        b_mod = sb("b_mod", [P, DEPTH, 6 * KD])
        cond = sb("cond", [P, KD, 2])
        cond32 = sb("cond32", [P, KD, 32])
        cond_sel = sb("cond_sel", [P, 2])
        taps = sb("taps", [P, DEPTH, FFN_TILES, 4])
        pool_scale = sb("pool_scale", [P, KD])
        tri = sb("tri", [P, 2, P])
        ones = sb("ones", [P, P])
        ssd_taps = sb("ssd_taps", [P, SSD_CONV_TILES, 4])
        dt_rows = sb("dt_rows", [P, 2, NDT])
        ssd_cols = sb("ssd_cols", [P, 3, KI])

        mod_raw = sb("mod_raw", [P, 2, KD * MOD_COLS])
        mod_rows = sb("mod_rows", [P, 2, MOD_COLS])

        with ExitStack() as part:
            g_hi = sb("g_hi", [P, KF, COLS], F32R, part)
            g_lo = sb("g_lo", [P, KF, COLS], F32R, part)
            acc = sb("acc", [P, 4, COLS], F32, part)
            sil = sb("sil", [P, 2, COLS], F32, part)
            gate = sb("gate", [P, 2, COLS], F32, part)
        with ExitStack() as part:
            gapped = sb("gapped", [P, KD, GAPPED], F32, part)
            sums_a = sb("sums_a", [P, KD, GAPPED], F32, part)
            sums_b = sb("sums_b", [P, KD, GAPPED], F32, part)
            inv_count = sb("inv_count", [P, len(WINDOWS), CTX + LAT], F32, part)

        with ExitStack() as part:
            zt = sb("zt", [P, KI, COLS], F32, part)
            xbc = sb("xbc", [P, SSD_CONV_TILES, COLS], F32, part)
            state0 = sb("state0", [P, 2, 2, GW], F32, part)
            state1 = sb("state1", [P, 2, GW], F32, part)
            cb_mask = sb("cb_mask", [P, 2, P], F32, part)
            dtv = sb("dtv", [P, 3, NDT], F32, part)
            adt = sb("adt", [P, 3, NDT], F32, part)
            neg_cum = sb("neg_cum", [P, 3, NDT], F32, part)
        with ExitStack() as part:
            y_hi = sb("y_hi", [P, KI, COLS], F32R, part)
            sb("y_between", [P, KI, COLS], F32, part)
            y_lo = sb("y_lo", [P, KI, COLS], F32R, part)
        with ExitStack() as part:
            conf_tab = sb("conf_tab", [P, C_ALL], F32, part)
            linear_half = sb("linear_half", [P, KD, COLS], F32, part)
            gate_half = sb("gate_half", [P, KD, COLS], F32, part)
            glu = sb("glu", [P, KD, CGAP], F32, part)
            convolved = sb("convolved", [P, KD, CONVOLVED], F32, part)
            ln_mean = sb("ln_mean", [P, 3], F32, part)
        with ExitStack() as part:
            attn_tab = sb("attn_tab", [P, A_ALL], F32, part)
            qkv = sb("qkv", [P, QK + AKV, COLS], F32, part)
            q_turned = sb("q_turned", [P, AH, LAT], F32, part)
            k_all = sb("k_all", [P, AKV, PAST + LAT], F32, part)
            v_rows = sb("v_rows", [P, AKV, len(CHUNKS) * AD], F32, part)
            rot_sin = sb("rot_sin", [P, 2, LAT], F32, part)
            prob = sb("prob", [P, 2, PAST + LAT], F32, part)
            prob_t = sb("prob_t", [P, 2, PAST + LAT], F32, part)
            qk_std = sb("qk_std", [P, 3 * QK], F32, part)
            qk_rstd = sb("qk_rstd", [P, 3 * QK], F32, part)
            row_max = sb("row_max", [P, 2], F32, part)
            neg_max = sb("neg_max", [P, 2], F32, part)
            row_sum = sb("row_sum", [P, 2], F32, part)
            inv_sum = sb("inv_sum", [P, 2], F32, part)
        decay = mod_raw[:, 0, :].rearrange("p (u d n) -> p u d n", u=2, d=2)
        c_scaled = mod_raw[:, 1, :].rearrange("p (u d n) -> p u d n", u=2, d=2)
        to_end = sq[:, 2, 192:384].rearrange("p (c h) -> p c h", c=3)
        full_decay = sq[:, 3, 0:192].rearrange("p (c h) -> p c h", c=3)
        flat = work[:, :, :].rearrange("p k n -> p (k n)")
        turned = flat[:, 0:1024].rearrange("p (u n) -> p u n", u=2)
        x_dt = flat[:, 1024:2048].rearrange("p (u d n) -> p u d n", u=2, d=2)
        x_end = flat[:, 2048:2560].rearrange("p (d n) -> p d n", d=2)
        state_new = flat[:, 2560:3072].rearrange("p (d n) -> p d n", d=2)

        tile_bank = [bank(f"tile_bank{i}") for i in range(BANKS)]
        mod_bank = bank("mod_bank")
        col_bank = bank("col_bank")
        stat_bank = bank("stat_bank")
        rstd_bank = bank("rstd_bank")

        consts = sem("consts")
        cond_loaded = sem("cond_loaded")
        loaded0 = sem("loaded0")
        vec_init = sem("vec_init")
        w_loaded = [sem(f"w_loaded{i}") for i in range(RAW_SLOTS)]
        w_rounded = sem("w_rounded")
        w_low_pool = sem("w_low_pool")
        w_low_dve = sem("w_low_dve")
        w_used = sem("w_used")
        mod_loaded = [sem(f"mod_loaded{i}") for i in range(2)]
        mod_used = sem("mod_used")
        rows_ready = sem("rows_ready")
        cols_ready = sem("cols_ready")
        mod_done = sem("mod_done")
        cond_ready = sem("cond_ready")
        acc_ready = sem("acc_ready")
        tap_first = sem("tap_first")
        conv_done = sem("conv_done")
        sil_ready = sem("sil_ready")
        gate_ready = sem("gate_ready")
        g_hi_ready = sem("g_hi_ready")
        g_lo_ready = sem("g_lo_ready")
        evac = sem("evac")
        sq_ready = sem("sq_ready")
        sq_used = sem("sq_used")
        std_ready = sem("std_ready")
        rstd_ready = sem("rstd_ready")
        rstd_spread = sem("rstd_spread")
        x_ready = sem("x_ready")
        opnd_ready = sem("opnd_ready")
        opnd_hi = sem("opnd_hi")
        lo_pool = sem("lo_pool")
        lo_dve = sem("lo_dve")
        sq_added = sem("sq_added")
        coef_ready = sem("coef_ready")
        mod_scaled = sem("mod_scaled")
        lat_ready = sem("lat_ready")
        dve = sem("dve")
        pe = sem("pe")
        stored = sem("stored")
        z_dt = sem("z_dt")
        dt_pe = sem("dt_pe")
        dt_act = sem("dt_act")
        xbc_ready = sem("xbc_ready")
        s_turned = sem("s_turned")
        s_copied = sem("s_copied")
        s_cum = sem("s_cum")
        s_cexp = sem("s_cexp")
        s_seg = sem("s_seg")
        s_exp = sem("s_exp")
        s_w = sem("s_w")
        s_xdt = sem("s_xdt")
        s_xend = sem("s_xend")
        s_cs = sem("s_cs")
        s_state = sem("s_state")
        s_taken = sem("s_taken")
        s_y = sem("s_y")
        s_out = sem("s_out")
        state_loaded = [sem(f"state_loaded{i}") for i in range(2)]
        state_stored = sem("state_stored")
        yz_ready = sem("yz_ready")
        late_loaded = sem("late_loaded")
        glu_ready = sem("glu_ready")
        conf_tap = sem("conf_tap")
        ln_sums = sem("ln_sums")
        ln_mean_ready = sem("ln_mean_ready")
        ln_spread = sem("ln_spread")
        ln_centred = sem("ln_centred")
        ln_scaled = sem("ln_scaled")
        v_turned = sem("v_turned")
        v_copied = sem("v_copied")
        qk_std_ready = sem("qk_std_ready")
        qk_rstd_ready = sem("qk_rstd_ready")
        qk_spread = sem("qk_spread")
        qk_normed = sem("qk_normed")
        qk_rot = sem("qk_rot")
        qk_cos = sem("qk_cos")
        qk_sin = sem("qk_sin")
        qk_turned = sem("qk_turned")
        cache_stored = sem("cache_stored")
        att_score = sem("att_score")
        att_rowmax = sem("att_rowmax")
        att_max = sem("att_max")
        att_exp = sem("att_exp")
        att_inv = sem("att_inv")
        att_prob = sem("att_prob")
        att_turned = sem("att_turned")
        att_pt = sem("att_pt")
        att_pv = sem("att_pv")
        att_part = sem("att_part")

        block = ctx.enter_context(nc.Block())

        def slot(n):
            return n % RAW_SLOTS

        def fetched(n, i=0, per=0):
            return 16 * (n // RAW_SLOTS + 1) + i * (16 * per // RAW_SLOTS)

        def weights(t, n, tiles):
            return t[:, n % SPLIT_SLOTS, 0:tiles * P]

        def split_at(s):
            return (s.tiles if s.name.startswith("conf") else s.tiles // 2) * s.width

        def low_ready(engine, name, k):
            by_pool, count = low_at[name][k]
            engine.wait_ge(lo_pool if by_pool else lo_dve, count)

        def units():
            for h in range(AH):
                for c in range(3):
                    yield h, c, 3 * h + c

        def copied_out(engine, u):
            h, c = u // 3, u % 3
            if c == 2:
                engine.wait_ge(opnd_ready, opnd["mid3"] + h + 1)
            else:
                engine.wait_ge(att_part, 2 * h + c + 1)

        LOADS0 = 16 * 9
        DT_DVE = 20
        CONSTS = 15

        class Chain:

            def __init__(self, engine, semaphore):
                self.engine, self.sem, self.n = engine, semaphore, 0

            def did(self, ins):
                ins.then_inc(self.sem, 1)
                self.n += 1
                return self.n

            def wait(self, n=None):
                self.engine.wait_ge(self.sem, self.n if n is None else n)

        def steps():
            for g in range(GROUPS):
                for c in range(3):
                    yield g, c, 3 * g + c, 2 * g + c - 1

        def state_dirs(c):
            return [(0, 1), (0,), (1,)][c]

        def linears(l):
            return {0: ["pool"], 1: ["ssd_conv", "ssd_z", "ssd_dt", "ssd_out"], 2: ["conf_in", "conf_out"],
                    3: ["qkv", "attn_out"]}[l]

        def owner(n):
            for s in order:
                if s.n0 <= n < s.n0 + s.chunks:
                    return s
            return None

        @block.sync
        def _(sp):
            def load_mod(l, piece, i=None, per=0):
                g = l * MOD_PIECES + piece
                if i is None:
                    if g >= 2:
                        sp.wait_ge(mod_used, g - 1)
                    src = a["w_mod"][g]
                else:
                    sp.wait_ge(mod_used, i * per + (g - 1))
                    src = a["w_mod"][bass.ds(i * per + g, 1), :, :].rearrange("a p n -> p (a n)")
                sp.dma_start(mod_raw[:, g % 2, :], src).then_inc(mod_loaded[g % 2], 16)

            sp.dma_start(cond[:, :, :], a["cond"]).then_inc(cond_loaded, 16)
            for j in range(2):
                load_mod(0, j)
            sp.dma_start(x[:, :, :], a["x"]).then_inc(loaded0, 16)
            sp.dma_start(gains[:, :, :, :], a["gains"]).then_inc(loaded0, 16)
            sp.dma_start(b_mod[:, :, :], a["b_mod"]).then_inc(loaded0, 16)
            sp.dma_start(taps[:, :, :, :], a["taps"]).then_inc(loaded0, 16)
            sp.dma_start(pool_scale[:, :], a["pool_scale"]).then_inc(loaded0, 16)

            sp.dma_start(inv_count[:, :, :], a["inv_count"]).then_inc(loaded0, 16)
            sp.dma_start(ssd_taps[:, :, :], a["ssd_taps"]).then_inc(loaded0, 16)
            sp.dma_start(dt_rows[:, :, :], a["dt_rows"]).then_inc(loaded0, 16)
            sp.dma_start(ssd_cols[:, :, :], a["ssd_cols"]).then_inc(loaded0, 16)

            def load_chunk(s, j, i=None, per=0):
                n = s.n0 + j
                src = a[s.name]
                width = s.tiles * s.width
                if i is None:
                    sp.wait_ge(w_low_pool, n + 1)
                    sp.wait_ge(w_low_dve, n + 1)
                    sp.dma_start(raw[:, slot(n), 0:width], src[j]).then_inc(w_loaded[slot(n)], 16)
                else:
                    sp.wait_ge(w_low_pool, i * per + (n + 1))
                    sp.wait_ge(w_low_dve, i * per + (n + 1))
                    sp.dma_start(raw[:, slot(n), 0:width],
                                 src[bass.ds(i * per + j, 1), :, :].rearrange("a p n -> p (a n)")
                                 ).then_inc(w_loaded[slot(n)], 16)

            with sp.Fori(0, MOD_PIECES // 2 - 1) as i:
                for j in range(2):
                    load_mod(0, j + 2, i, 2)

            def scan_traffic():
                for g in range(GROUPS):
                    if g >= 2:
                        sp.wait_ge(s_y, 3 * (g - 2) + 3)
                        sp.wait_ge(s_taken, 3 * (g - 2) + 3)
                    else:
                        low_ready(sp, "mix1", KD - 2)
                        low_ready(sp, "mix1", KD - 1)
                    sp.dma_start(state0[:, g % 2, :, :], a["state_in"][:, :, g * GW:(g + 1) * GW]
                                 ).then_inc(state_loaded[g % 2], 16)
                    if g >= 1:
                        sp.wait_ge(s_taken, 3 * (g - 1) + 1)
                        sp.dma_start(out["state"][:, :, (g - 1) * GW:g * GW], state_new).then_inc(state_stored, 16)
                sp.wait_ge(s_taken, 3 * (GROUPS - 1) + 1)
                sp.dma_start(out["state"][:, :, (GROUPS - 1) * GW:], state_new).then_inc(state_stored, 16)
                sp.wait_ge(state_stored, 16 * GROUPS)

            for s in order:
                if s.name == "ssd_out":
                    for j in range(RAW_SLOTS):
                        load_chunk(s, j)
                    scan_traffic()
                    with sp.Fori(0, s.chunks // 4 - 1) as i:
                        for j in range(4):
                            load_chunk(s, j + RAW_SLOTS, i, 4)
                elif s.name == "attn_out":
                    for j in range(RAW_SLOTS):
                        load_chunk(s, j)
                    sp.wait_ge(qk_normed, QK)
                    sp.dma_start(out["cache_k"], qkv[:, AH:QK, 0:CTX]).then_inc(cache_stored, 16)
                    sp.dma_start(out["cache_v"], qkv[:, QK:, 0:CTX]).then_inc(cache_stored, 16)
                    for j in range(RAW_SLOTS, s.chunks):
                        load_chunk(s, j)
                elif s.name.startswith("ffn_in"):
                    l = int(s.name[-1])
                    more = l + 1 < DEPTH
                    with sp.Fori(0, FFN_TILES // 4) as i:
                        for j in range(4):
                            load_chunk(s, j, i, 4)
                            if more and j % 2:
                                load_mod(l + 1, j // 2, i, 2)
                elif s.chunks >= 8:
                    with sp.Fori(0, s.chunks // 4) as i:
                        for j in range(4):
                            load_chunk(s, j, i, 4)
                    for j in range(s.chunks // 4 * 4, s.chunks):
                        load_chunk(s, j)
                else:
                    for j in range(s.chunks):
                        load_chunk(s, j)
                if s.name.startswith("ffn_out") and s is not order[-1]:
                    l = int(s.name[-1])
                    load_mod(l + 1, MOD_PIECES - 2)
                    load_mod(l + 1, MOD_PIECES - 1)
            sp.wait_ge(x_ready, KD * (2 * DEPTH + 1))
            sp.dma_start(out["y"], x[:, :, :]).then_inc(stored, 16)
            sp.wait_ge(stored, 16)
            sp.wait_ge(cache_stored, 32)

        @block.gpsimd
        def _(pool):
            pool.memset(spare[:, 6:7], 0.0).then_inc(w_low_pool, RAW_SLOTS)
            pool.memset(ident[:, :], 0.0).then_inc(consts, 1)
            pool.memset(mean_col[:, 0:1], 1.0 / D).then_inc(consts, 1)
            pool.memset(mean_col[:, 1:2], 1.0 / INNER).then_inc(consts, 1)
            pool.memset(mean_col[:, 2:3], 1.0 / AD).then_inc(consts, 1)
            pool.memset(eps_col[:, :], EPS).then_inc(consts, 1)
            pool.memset(cond_sel[:, :], 0.0).then_inc(consts, 1)
            pool.wait_ge(consts, 6)
            pool.affine_select(out=ident[:, 0:P], in_=ident[:, 0:P], compare_op=ALU.not_equal, fill=1.0, base=0,
                               pattern=[[-1, P]], channel_multiplier=1).then_inc(consts, 1)
            for g in range(4):
                pool.wait_ge(consts, 7 + g)
                pool.affine_select(out=cond_sel[:, :], in_=cond_sel[:, :], compare_op=ALU.not_equal, fill=1.0,
                                   base=-32 * g, pattern=[[-1, 2]], channel_multiplier=1).then_inc(consts, 1)

            pool.memset(tri[:, :, :], 1.0).then_inc(consts, 1)
            pool.memset(ones[:, :], 1.0).then_inc(consts, 1)
            pool.wait_ge(consts, CONSTS - 2)
            for d in range(2):
                sign = -1 if d else 1
                pool.affine_select(out=tri[:, d, :], in_=tri[:, d, :], compare_op=ALU.is_ge, fill=0.0, base=0,
                                   pattern=[[sign, P]], channel_multiplier=-sign).then_inc(consts, 1)

            def low_part(s, j, i=None, per=0):
                n = s.n0 + j
                w = split_at(s)
                pool.wait_ge(w_rounded, n + 1 if i is None else i * per + (n + 1))
                pool.tensor_tensor(w_lo[:, n % SPLIT_SLOTS, 0:w], raw[:, slot(n), 0:w],
                                   w_hi[:, n % SPLIT_SLOTS, 0:w].bitcast(F32), ALU.subtract).then_inc(w_low_pool, 1)

            def low_next(n):
                s = owner(n)
                if s is not None:
                    low_part(s, n - s.n0)

            def lows_behind(s):
                if s.chunks >= 8:
                    with pool.Fori(0, s.chunks // 4 - 1) as i:
                        for j in range(4):
                            low_part(s, j + 1, i, 4)
                for j in range(max(0, s.chunks - 4), s.chunks):
                    low_next(s.n0 + j + 1)

            def add_squares(name, m):
                _, base, _ = norm[name]
                kind, n = slot_freed[base + m - 1] if m else ("used", 0)
                if kind == "added":
                    pool.wait_ge(sq_ready, base + m + 1)
                    if n > 1:
                        pool.wait_ge(sq_added, n - 1)
                    to = sq[:, (base + m) % 4, :]
                    pool.tensor_tensor(to, to, sq[:, (base + m - 1) % 4, :], ALU.add).then_inc(sq_added, 1)

            def add_all(name):
                for m in range(norm[name][2]):
                    add_squares(name, m)

            def operand_lows(name, src=work, hi=h_hi, lo=h_lo):
                for k, (by_pool, _) in enumerate(low_at[name]):
                    if by_pool:
                        pool.wait_ge(opnd_hi, opnd[name] + k + 1)
                        pool.tensor_tensor(lo[:, k, :], src[:, k, :], hi[:, k, :].bitcast(F32),
                                           ALU.subtract).then_inc(lo_pool, 1)

            def out_lows(s, name):
                for m in range(KD):
                    for j in range(s.per):
                        low_next(s.n0 + s.per * m + j + 1)
                    add_squares(name, m)

            def scan_pool():
                for g, c, u, v in steps():
                    pool.wait_ge(s_copied, u + 1)
                    if u >= 2:
                        pool.wait_ge(s_y, u - 1)
                    xt = turned[:, u % 2, P:P + GW].rearrange("p (h q) -> p h q", h=HPG)
                    for d in range(2):
                        h0 = d * SSD_HEADS + g * HPG
                        pool.tensor_tensor(x_dt[:, u % 2, d, :].rearrange("p (h q) -> p h q", h=HPG), xt,
                                           dtv[:, c, h0:h0 + HPG].unsqueeze(2).broadcast_to([P, HPG, HEAD]),
                                           ALU.mult).then_inc(s_xdt, 1)
                    if u >= 1:
                        pool.wait_ge(s_state, u)
                    for d in state_dirs(c):
                        h0 = d * SSD_HEADS + g * HPG
                        ins = pool.tensor_tensor(x_end[:, d, :].rearrange("p (h q) -> p h q", h=HPG), xt,
                                                 to_end[:, c, h0:h0 + HPG].unsqueeze(2).broadcast_to([P, HPG, HEAD]),
                                                 ALU.mult)
                    ins.then_inc(s_xend, 1)
                    if c:
                        for d in range(2):
                            pool.wait_ge(s_cexp, 2 * v + d + 1)
                            cs = c_scaled[:, u % 2, d, :].rearrange("p (h i) -> p h i", h=HPG)
                            c0 = CHUNKS[c][0]
                            pool.tensor_tensor(cs, cs, xbc[:, KI + GROUPS + g, c0:c0 + P].unsqueeze(1).broadcast_to(
                                [P, HPG, P]), ALU.mult).then_inc(s_cs, 1)

            def conf_pool():
                s = lin["conf_in"]
                pool.wait_ge(w_used, s.n0)
                pool.memset(glu[:, :, :], 0.0).then_inc(glu_ready, 1)
                low_part(s, 1)
                pool.wait_ge(glu_ready, 1)
                for m in range(KD):
                    low_next(s.n0 + 2 * m + 2)
                    pool.wait_ge(evac, 4 + s.evac0 + 2 * m + 2)
                    for c0, w, k in STREAMS:
                        pool.tensor_tensor(glu[:, m, CGAP_AT[k]:CGAP_AT[k] + w], linear_half[:, m, c0:c0 + w],
                                           gate_half[:, m, c0:c0 + w], ALU.mult).then_inc(glu_ready, 1)
                    if m + 1 < KD:
                        low_part(s, 2 * m + 3)

            def rope_pool():
                pool.wait_ge(late_loaded, 48)
                for t in range(QK):
                    pool.wait_ge(qk_normed, t + 1)
                    to = q_turned[:, t, :] if t < AH else k_all[:, t - AH, PAST:]
                    pool.tensor_tensor(to, qkv[:, t, LAT0:LAT0 + LAT], attn_tab[:, A_COS:A_COS + LAT],
                                       ALU.mult).then_inc(qk_cos, 1)

            add_all("pre0.0")
            low_next(0)
            for l in range(DEPTH):
                if l:
                    add_all(f"pre{l}.0")
                operand_lows(f"mix{l}")
                if l == 0:
                    low_next(1)
                    for m in range(KD):
                        add_squares("post0.0", m)
                    low_next(2)
                if l == 1:
                    for name in ("ssd_conv", "ssd_z", "ssd_dt"):
                        lows_behind(lin[name])
                    pool.wait_ge(z_dt, DT_DVE)
                    scan_pool()
                    add_all("ssd")
                    operand_lows("ssd_y", xbc, y_hi, y_lo)
                    out_lows(lin["ssd_out"], "post1.0")
                if l == 2:
                    conf_pool()
                    add_all("ln")
                    out_lows(lin["conf_out"], "post2.0")
                if l == 3:
                    lows_behind(lin["qkv"])
                    rope_pool()
                    out_lows(lin["attn_out"], "post3.0")
                add_all(f"pre{l}.1")
                operand_lows(f"ffn{l}")
                lows_behind(lin[f"ffn_in{l}"])
                out_lows(lin[f"ffn_out{l}"], f"post{l}.1")

        @block.scalar
        def _(act):
            def apart():
                act.wait_ge(consts, CONSTS)

            def round_chunk(s, j, i=None, per=0):
                n = s.n0 + j
                w = s.tiles * s.width
                act.wait_ge(w_loaded[slot(n)], fetched(n) if i is None else fetched(n, i, per))
                if i is not None:
                    act.wait_ge(w_used, i * per + (n - SPLIT_SLOTS + 1))
                elif n >= SPLIT_SLOTS:
                    act.wait_ge(w_used, n - SPLIT_SLOTS + 1)
                act.activation(w_hi[:, n % SPLIT_SLOTS, 0:w], raw[:, slot(n), 0:w], ACT.Copy).then_inc(w_rounded, 1)

            def round_next(n):
                s = owner(n)
                if s is not None:
                    round_chunk(s, n - s.n0)

            def mod_row(l, piece, i=None, per=0):
                g = l * MOD_PIECES + piece
                at = (lambda v: v) if i is None else (lambda v: i * per + v)
                act.wait_ge(mod_used, at(g + 1))
                act.wait_ge(cols_ready, at(2 + g - 1))
                act.activation(mod_rows[:, g % 2, :], mod_bank[:, 0:MOD_COLS],
                               ACT.Copy).then_inc(rows_ready, 1)

            def free_slot(count):
                if count >= 4:
                    kind, n = slot_freed[count - 4]
                    act.wait_ge(sq_added if kind == "added" else sq_used, n)

            def square(src, count):
                free_slot(count)
                act.activation(sq[:, count % 4, :], src, ACT.Square).then_inc(sq_ready, 1)

            def take_std(name):
                act.wait_ge(sq_used, sum_groups[name][1])
                act.activation(std[:, :], stat_bank[:, 0:3], ACT.Sqrt, bias=eps_col[:, 0:1]).then_inc(std_ready, 1)

            def tile_out(s, name, m, gates, scale=None, bias=None):
                _, base, _ = norm[name]
                b = tile_bank[(s.t0 + m) % BANKS]
                kw = {"scale": scale[:, m:m + 1]} if scale is not None else {}
                if bias is not None:
                    kw["bias"] = bias[:, m:m + 1]
                free_slot(base + m)
                act.activation(sq[:, (base + m) % 4, :], b[:, 0:COLS], ACT.Square, **kw).then_inc(sq_ready, 1)
                for c0, w, st in ((0, LAT0, 0), (LAT0, COLS - LAT0, 1)):
                    kw = {} if bias is None else {"bias": gated_bias[:, m, st:st + 1]}
                    ins = act.activation(work[:, m, c0:c0 + w], b[:, c0:c0 + w], ACT.Identity,
                                         scale=coef[:, gates, m, st:st + 1], **kw)
                ins.then_inc(evac, 1)

            def tiles_out(s, name, gates, bias=None):
                for m in range(KD):
                    for j in range(s.per):
                        round_next(s.n0 + s.per * m + j + 1)
                    act.wait_ge(w_used, s.n0 + s.per * (m + 1))
                    tile_out(s, name, m, gates, bias=bias)

            def squares_of_x(name, xbase):
                e, base, k = norm[name]
                for m in range(KD):
                    act.wait_ge(x_ready, xbase + m + 1)
                    square(x[:, m, :], base + m)

            def split_high(name):
                base = opnd[name]
                for m in range(KD):
                    act.wait_ge(opnd_ready, base + m + 1)
                    act.activation(h_hi[:, m, :], work[:, m, :], ACT.Copy).then_inc(opnd_hi, 1)

            def modulate_high(l, name, k):
                base, at = opnd[name], KD * (2 * l + k - 1)
                lat = slice(LAT0, LAT0 + LAT)
                for m in range(KD + 1):
                    if m < KD:
                        act.wait_ge(mod_scaled, at + m + 1)
                        act.activation(work[:, m, lat], work[:, m, lat], ACT.Identity, scale=coef[:, 2 * k, m, 1:2],
                                       bias=modc[:, l % 2, 3 * k * KD + m, 1:2]).then_inc(lat_ready, 1)
                    if m:
                        act.wait_ge(lat_ready, at + m)
                        act.wait_ge(opnd_ready, base + m)
                        act.activation(h_hi[:, m - 1, :], work[:, m - 1, :], ACT.Copy).then_inc(opnd_hi, 1)

            def ffn_in(l):
                s = lin[f"ffn_in{l}"]
                more = l + 1 < DEPTH
                p0 = l * PAIRS

                def at(v, i):
                    return v if i is None else i * 4 + v

                def group(i, first=False, last=False, base=0):
                    for j in range(4):
                        c = s.conv0 + base + j
                        pair = p0 + (base + j) // 2
                        half = (lambda v: v) if i is None else (lambda v: i * 2 + v)
                        if i is not None or base + j + 1 < FFN_TILES:
                            round_chunk(s, base + j + 1, i, 4)
                        else:
                            round_next(s.n0 + base + j + 1)
                        if j % 2 == 0 and not (first and j == 0):
                            act.wait_ge(gate_ready, half(pair))
                            apart()
                            act.activation(g_hi[:, bass.ds(half(pair - p0 - 1), 1), :].rearrange("p a n -> p (a n)"),
                                           gate[:, (pair - 1) % 2, :], ACT.Copy).then_inc(g_hi_ready, 1)
                        act.wait_ge(w_used, at(s.n0 + base + j + 1, i))
                        apart()
                        k = bass.ds(at(base + j, i), 1)
                        act.activation(acc[:, c % 4, :], tile_bank[(s.t0 + base + j) % BANKS][:, 0:COLS], ACT.Identity,
                                       scale=taps[:, l, k, 1:2].rearrange("p a b -> p (a b)"),
                                       bias=taps[:, l, k, 3:4].rearrange("p a b -> p (a b)")).then_inc(acc_ready, 1)
                        if j % 2:
                            act.wait_ge(conv_done, at(4 + c, i))
                            act.activation(sil[:, pair % 2, :], acc[:, (c - 1) % 4, :], ACT.Silu).then_inc(sil_ready, 1)
                        elif more:
                            mod_row(l + 1, base // 2 + j // 2, i, 2)

                group(None, first=True)
                with act.Fori(0, FFN_TILES // 4 - 2) as i:
                    group(i, base=4)
                group(None, last=True, base=FFN_TILES - 4)
                act.wait_ge(gate_ready, p0 + PAIRS)
                act.activation(g_hi[:, PAIRS - 1, :], gate[:, (p0 + PAIRS - 1) % 2, :], ACT.Copy).then_inc(g_hi_ready, 1)
            def ssd_conv():
                s = lin["ssd_conv"]

                def tile(base, j, i, first=False):
                    at = (lambda v: v) if i is None else (lambda v: i * 4 + v)
                    t, c = base + j, s.conv0 + base + j
                    if i is not None or t + 1 < s.chunks:
                        round_chunk(s, t + 1, i, 4)
                    else:
                        round_next(s.n0 + t + 1)
                    if not first:
                        act.wait_ge(conv_done, at(4 + c))
                    act.wait_ge(w_used, at(s.n0 + t + 1))
                    apart()
                    k = bass.ds(at(t), 1)
                    act.activation(xbc[:, k, :].rearrange("p a n -> p (a n)"), tile_bank[(s.t0 + t) % BANKS][:, 0:COLS],
                                   ACT.Identity, scale=ssd_taps[:, k, 1:2].rearrange("p a b -> p (a b)"),
                                   bias=ssd_taps[:, k, 3:4].rearrange("p a b -> p (a b)")).then_inc(acc_ready, 1)
                    if not first:
                        silu(bass.ds(at(t - 1), 1))

                def silu(k):
                    b = xbc[:, k, :].rearrange("p a n -> p (a n)")
                    act.activation(b, b, ACT.Silu).then_inc(xbc_ready, 1)

                for j in range(4):
                    tile(0, j, None, first=j == 0)
                with act.Fori(0, s.chunks // 4 - 2) as i:
                    for j in range(4):
                        tile(4, j, i)
                for j in range(4):
                    tile(s.chunks - 4, j, None)
                act.wait_ge(conv_done, 4 + s.conv0 + s.chunks)
                silu(bass.ds(s.chunks - 1, 1))

            def ssd_z_dt():
                s = lin["ssd_z"]
                for m in range(s.chunks):
                    round_next(s.n0 + m + 1)
                    act.wait_ge(w_used, s.n0 + m + 1)
                    act.activation(zt[:, m, :], tile_bank[(s.t0 + m) % BANKS][:, 0:COLS], ACT.Silu).then_inc(evac, 1)
                s = lin["ssd_dt"]
                round_next(s.n0 + 1)
                act.wait_ge(w_used, s.n0 + 1)
                act.activation(sq[0:NDT, 0, :], tile_bank[s.t0 % BANKS][0:NDT, 0:COLS], ACT.Copy).then_inc(evac, 1)

            def dt_prepare():
                act.activation(sq[:, 3, 192:256], dt_rows[:, 1, :], ACT.Exp).then_inc(dt_act, 1)
                act.wait_ge(z_dt, 3)
                act.activation(sq[:, 3, 0:192], sq[:, 2, 0:192], ACT.Exp, scale=-1.0).then_inc(dt_act, 1)
                act.wait_ge(z_dt, DT_DVE - 1)
                t = to_end[:, :, :]
                act.activation(t, t, ACT.Exp).then_inc(dt_act, 1)
                act.activation(full_decay[:, :, :], full_decay[:, :, :], ACT.Exp).then_inc(dt_act, 1)

            def scan_act():
                for g, c, u, v in steps():
                    act.wait_ge(s_turned, u + 1)
                    if u >= 2:
                        act.wait_ge(s_state, u - 1)
                        act.wait_ge(s_xend, u - 1)
                        act.wait_ge(s_seg, 2 * (u - 2) + 2)
                    act.activation(turned[:, u % 2, :], tile_bank[u % 2][:, :], ACT.Copy).then_inc(s_copied, 1)
                    if c:
                        if u >= 2:
                            act.wait_ge(s_y, u - 1)
                        for d in range(2):
                            act.wait_ge(s_cum, 2 * u + d + 1)
                            act.activation(c_scaled[:, u % 2, d, :], tile_bank[2 + d][:, :], ACT.Exp).then_inc(s_cexp, 1)
                    for d in range(2):
                        act.wait_ge(s_seg, 2 * u + d + 1)
                        act.activation(decay[:, u % 2, d, :], decay[:, u % 2, d, :], ACT.Exp).then_inc(s_exp, 1)

            def ssd_norm():
                e, base, k = norm["ssd"]
                for m in range(k):
                    act.wait_ge(yz_ready, m + 1)
                    square(xbc[:, m, :], base + m)
                take_std("ssd")
                for m in range(k):
                    act.wait_ge(opnd_ready, opnd["ssd_y"] + m + 1)
                    act.activation(y_hi[:, m, :], xbc[:, m, :], ACT.Copy).then_inc(opnd_hi, 1)

            def conf_mix():
                s = lin["conf_in"]
                act.wait_ge(late_loaded, 16)
                for m in range(s.chunks):
                    round_next(s.n0 + m + 1)
                    act.wait_ge(w_used, s.n0 + m + 1)
                    gated = m % 2
                    act.activation((linear_half, gate_half)[gated][:, m // 2, :], tile_bank[(s.t0 + m) % BANKS][:, 0:COLS],
                                   ACT.Sigmoid if gated else ACT.Identity, bias=conf_tab[:, C_BIN + m:C_BIN + m + 1]
                                   ).then_inc(evac, 1)
                e, base, _ = norm["ln"]
                for m in range(KD):
                    act.wait_ge(ln_centred, m + 1)
                    square(work[:, m, :], base + m)
                take_std("ln")
                o = opnd["mid2"]
                for m in range(KD + 1):
                    if m < KD:
                        act.wait_ge(ln_scaled, m + 1)
                        act.activation(work[:, m, :], work[:, m, :], ACT.Silu, scale=conf_tab[:, C_LNG + m:C_LNG + m + 1],
                                       bias=conf_tab[:, C_LNB + m:C_LNB + m + 1]).then_inc(opnd_ready, 1)
                    if m:
                        act.wait_ge(opnd_ready, o + m)
                        act.activation(h_hi[:, m - 1, :], work[:, m - 1, :], ACT.Copy).then_inc(opnd_hi, 1)

            def attn_mix():
                s = lin["qkv"]
                for m in range(s.chunks):
                    round_next(s.n0 + m + 1)
                    act.wait_ge(w_used, s.n0 + m + 1)
                    act.activation(qkv[:, m, :], tile_bank[(s.t0 + m) % BANKS][:, 0:COLS], ACT.Copy).then_inc(evac, 1)
                e, base, _ = norm["qk"]
                act.wait_ge(evac, 4 + s.evac0 + s.chunks)
                for m in range(QK):
                    square(qkv[:, m, :], base + m)
                for kv in range(AKV):
                    act.wait_ge(v_turned, kv + 1)
                    act.activation(v_rows[:, kv, :], tile_bank[2 + kv][:, 0:3 * AD], ACT.Copy).then_inc(v_copied, 1)
                act.wait_ge(sq_used, sum_groups["qk"][1])
                act.activation(qk_std[:, :], stat_bank[:, 0:3 * QK], ACT.Sqrt, bias=eps_col[:, 0:1]).then_inc(qk_std_ready, 1)
                o = opnd["mid3"]
                for u in range(3 * AH + 3):
                    if u < 3 * AH:
                        w = P if u % 3 == 0 else PAST + LAT
                        act.wait_ge(att_max, u + 1)
                        if u >= 2:
                            act.wait_ge(att_turned, u - 1)
                            act.wait_ge(att_inv, u - 1)
                        act.activation(prob[:, u % 2, 0:w], tile_bank[u % 2][:, 0:w], ACT.Exp, scale=SCALE,
                                       bias=neg_max[:, u % 2:u % 2 + 1], accum_out=row_sum[:, u % 2:u % 2 + 1]
                                       ).then_inc(att_exp, 1)
                    if 2 <= u < 3 * AH + 2:
                        b = u - 2
                        w = P if b % 3 == 0 else PAST + LAT
                        act.wait_ge(att_turned, b + 1)
                        if b >= 2:
                            act.wait_ge(att_pv, b - 1)
                        act.activation(prob_t[:, b % 2, 0:w], tile_bank[2 + b % 2][:, 0:w], ACT.Copy).then_inc(att_pt, 1)
                    if u >= 3:
                        b = u - 3
                        h, c = b // 3, b % 3
                        act.wait_ge(att_pv, b + 1)
                        act.activation(work[:, h, CHUNKS[c][0]:CHUNKS[c][0] + P], (mod_bank, col_bank)[b % 2][:, 0:P],
                                       ACT.Copy).then_inc(opnd_ready if c == 2 else att_part, 1)
                        if c == 0 and h:
                            high_head(o, h - 1)
                high_head(o, AH - 1)

            def high_head(o, h):
                act.wait_ge(att_part, 2 * h + 2)
                act.wait_ge(opnd_ready, o + h + 1)
                act.activation(h_hi[:, h, :], work[:, h, :], ACT.Copy).then_inc(opnd_hi, 1)

            act.wait_ge(cond_loaded, 16)
            act.wait_ge(vec_init, 1)
            act.activation(cond32[:, :, 0:2], cond[:, :, :], ACT.Silu).then_inc(cond_ready, 1)
            act.wait_ge(consts, CONSTS)
            act.activation(spare[:, 4:5], eps_col[:, :], ACT.Copy).then_inc(rows_ready, 2)
            act.activation(spare[:, 5:6], eps_col[:, :], ACT.Copy).then_inc(evac, 4)
            with act.Fori(0, MOD_FIRST // 2) as i:
                for j in range(2):
                    mod_row(0, j, i, 2)
            squares_of_x("pre0.0", 0)
            take_std("pre0.0")
            with act.Fori(0, (MOD_PIECES - MOD_FIRST) // 2) as i:
                for j in range(2):
                    mod_row(0, MOD_FIRST + j, i, 2)
            round_next(0)
            for l in range(DEPTH):
                if l == 0:
                    split_high("mix0")
                    s = lin["pool"]
                    round_next(1)
                    act.wait_ge(coef_ready, 1)
                    for m in range(KD):
                        if m == 4:
                            round_next(2)
                        if m % 4 == 3:
                            act.wait_ge(w_used, m // 4 + 1)
                        else:
                            act.wait_ge(pe, m + 1 - m // 4)
                        tile_out(s, "post0.0", m, 1, scale=pool_scale)
                if l == 1:
                    modulate_high(1, "mix1", 0)
                    act.wait_ge(coef_ready, 2)
                    ssd_conv()
                    ssd_z_dt()
                    dt_prepare()
                    scan_act()
                    ssd_norm()
                    tiles_out(lin["ssd_out"], "post1.0", 1)
                if l == 2:
                    modulate_high(2, "mix2", 0)
                    act.wait_ge(coef_ready, 3)
                    conf_mix()
                    tiles_out(lin["conf_out"], "post2.0", 1, conf_tab[:, C_BOUT:C_BOUT + KD])
                if l == 3:
                    modulate_high(3, "mix3", 0)
                    act.wait_ge(coef_ready, 4)
                    attn_mix()
                    tiles_out(lin["attn_out"], "post3.0", 1)
                take_std(f"post{l}.0")
                squares_of_x(f"pre{l}.1", KD * (2 * l + 1))
                take_std(f"pre{l}.1")
                modulate_high(l, f"ffn{l}", 1)
                if l == 3:
                    act.wait_ge(cache_stored, 32)
                ffn_in(l)
                tiles_out(lin[f"ffn_out{l}"], f"post{l}.1", 3)
                if l == 1:
                    act.dma_start(conf_tab[:, :], a["conf_tab"]).then_inc(late_loaded, 16)
                if l == 2:
                    act.dma_start(attn_tab[:, :], a["attn_tab"]).then_inc(late_loaded, 16)
                    act.dma_start(k_all[:, :, 0:PAST], a["cache_k"]).then_inc(late_loaded, 16)
                take_std(f"post{l}.1")
                if l + 1 < DEPTH:
                    mod_row(l + 1, MOD_PIECES - 2)
                    mod_row(l + 1, MOD_PIECES - 1)
                    squares_of_x(f"pre{l + 1}.0", KD * (2 * l + 2))
                    take_std(f"pre{l + 1}.0")

        @block.vector
        def _(vec):
            ch = Chain(vec, dve)

            def low_part(s, j, i=None, per=0):
                n = s.n0 + j
                w0, w1 = split_at(s), s.tiles * s.width
                vec.wait_ge(w_rounded, n + 1 if i is None else i * per + (n + 1))
                vec.tensor_tensor(w_lo[:, n % SPLIT_SLOTS, w0:w1], raw[:, slot(n), w0:w1],
                                  w_hi[:, n % SPLIT_SLOTS, w0:w1].bitcast(F32), ALU.subtract).then_inc(w_low_dve, 1)

            def low_next(n):
                s = owner(n)
                if s is not None and split_at(s) < s.tiles * s.width:
                    low_part(s, n - s.n0)

            def mod_column(l, piece, i=None, per=0):
                g = l * MOD_PIECES + piece
                vec.wait_ge(cols_ready, 2 + g + 1 if i is None else i * per + (2 + g + 1))
                t0 = piece * MOD_TILES if i is None else i * (per * MOD_TILES) + piece * MOD_TILES
                vec.tensor_tensor(modc[:, l % 2, bass.ds(t0, MOD_TILES), :],
                                  col_bank[:, 0:2 * MOD_TILES].rearrange(
                                      "p (t s) -> p t s", s=2),
                                  b_mod[:, l, bass.ds(t0, MOD_TILES)].unsqueeze(2).broadcast_to([P, MOD_TILES, 2]),
                                  ALU.add).then_inc(mod_done, 1)

            def take_rstd(name):
                e, base, k = norm[name]
                vec.wait_ge(std_ready, e + 1)
                vec.reciprocal(rstd[:, :], std[:, :]).then_inc(rstd_ready, 1)

            def coefficients(l, parts=(0, 1, 2, 3)):
                for part in parts:
                    k = part // 2
                    gain = gains[:, l, part, :].unsqueeze(2).broadcast_to([P, KD, 2])
                    if part % 2 == 0:
                        ch.did(vec.scalar_tensor_tensor(
                            out=coef[:, part, :, :], in0=modc[:, l % 2, (3 * k + 1) * KD:(3 * k + 2) * KD, :],
                            scalar=1.0, in1=gain, op0=ALU.add, op1=ALU.mult))
                    else:
                        ch.did(vec.tensor_tensor(coef[:, part, :, :], modc[:, l % 2, (3 * k + 2) * KD:(3 * k + 3) * KD, :],
                                                 gain, ALU.mult))
                ch.wait()
                if 1 in parts:
                    gate = coef[:, 1, :, :]
                    if l == 2:
                        vec.wait_ge(late_loaded, 16)
                        vec.tensor_tensor(gated_bias[:, :, :], gate, conf_tab[:, C_BOUT:C_BOUT + KD].unsqueeze(2)
                                          .broadcast_to([P, KD, 2]), ALU.mult).then_inc(coef_ready, 1)
                    elif l == 0:
                        vec.tensor_tensor(gate, gate, pool_scale[:, :].unsqueeze(2).broadcast_to([P, KD, 2]),
                                          ALU.mult).then_inc(coef_ready, 1)
                    else:
                        vec.memset(spare[:, 0:1], 0.0).then_inc(coef_ready, 1)

            def residual(name, evac_count):
                e, _, _ = norm[name]
                vec.wait_ge(evac, evac_count)
                vec.wait_ge(rstd_spread, e + 1)
                scaled = [0] * KD
                for m in range(KD + 1):
                    if m < KD:
                        scaled[m] = ch.did(vec.tensor_tensor(work[:, m, :], work[:, m, :], rstd_bank[:, 0:COLS], ALU.mult))
                    if m:
                        ch.wait(scaled[m - 1])
                        vec.tensor_tensor(x[:, m - 1, :], x[:, m - 1, :], work[:, m - 1, :], ALU.add).then_inc(x_ready, 1)

            def modulate_gapped():
                vec.wait_ge(rstd_spread, norm["pre0.0"][0] + 1)
                scaled = [0] * KD
                for m in range(KD + 1):
                    if m < KD:
                        scaled[m] = ch.did(vec.tensor_tensor(work[:, m, :], x[:, m, :], rstd_bank[:, 0:COLS], ALU.mult))
                    if m:
                        t = m - 1
                        ch.wait(scaled[t])
                        for c0, w, s in STREAMS:
                            ch.did(vec.tensor_scalar(gapped[:, t, GAP_AT[s]:GAP_AT[s] + w], work[:, t, c0:c0 + w],
                                                     coef[:, 0, t, s:s + 1], modc[:, 0, t, s:s + 1], ALU.mult, ALU.add))

            def modulate(l, name, k, xbase, opname):
                e, _, _ = norm[name]
                o, at = opnd[opname], KD * (2 * l + k - 1)
                vec.wait_ge(rstd_spread, e + 1)
                vec.wait_ge(x_ready, xbase + KD)
                for m in range(KD + 2):
                    if m < KD:
                        vec.tensor_tensor(work[:, m, :], x[:, m, :], rstd_bank[:, 0:COLS], ALU.mult).then_inc(mod_scaled, 1)
                    if 1 <= m <= KD:
                        t = m - 1
                        vec.wait_ge(mod_scaled, at + t + 1)
                        vec.tensor_scalar(work[:, t, 0:CTX], work[:, t, 0:CTX], coef[:, 2 * k, t, 0:1],
                                          modc[:, l % 2, 3 * k * KD + t, 0:1], ALU.mult, ALU.add).then_inc(opnd_ready, 1)
                    if m >= 2 and not low_at[opname][m - 2][0]:
                        low_operand(o, m - 2)

            def low_operand(o, t):
                vec.wait_ge(opnd_hi, o + t + 1)
                vec.tensor_tensor(h_lo[:, t, :], work[:, t, :], h_hi[:, t, :].bitcast(F32),
                                  ALU.subtract).then_inc(lo_dve, 1)

            def pool_mix():
                pieces = iter(range(MOD_FIRST, MOD_PIECES))

                def next_piece():
                    piece = next(pieces, None)
                    if piece is not None:
                        mod_column(0, piece)

                ch.wait()
                n = GAPPED
                kg = KD // len(WINDOWS)
                ch.did(vec.tensor_tensor(sums_a[:, :, 1:n], gapped[:, :, 0:n - 1], gapped[:, :, 1:n], ALU.add))
                next_piece()
                ch.wait()
                src, dst, lo, hi, step = sums_a, sums_b, 1, n, 1
                for g in range(len(WINDOWS)):
                    k0, k1 = g * kg, (g + 1) * kg
                    if g:
                        ch.did(vec.tensor_tensor(dst[:, k0:, lo + step:hi - step], src[:, k0:, lo:hi - 2 * step],
                                                 src[:, k0:, lo + 2 * step:hi], ALU.add))
                        next_piece()
                        ch.wait()
                        src, dst, lo, hi, step = dst, src, lo + step, hi - step, 2 * step
                    for c0, w, s in STREAMS:
                        j0 = s * CTX
                        ga = slice(GAP_AT[s], GAP_AT[s] + w)
                        ch.did(vec.tensor_tensor(work[:, k0:k1, c0:c0 + w], src[:, k0:k1, ga],
                                                 inv_count[:, g, j0:j0 + w].unsqueeze(1).broadcast_to([P, kg, w]),
                                                 ALU.mult))
                    next_piece()
                    ch.wait()
                    for c0, w, s in STREAMS:
                        ga = slice(GAP_AT[s], GAP_AT[s] + w)
                        ins = vec.tensor_tensor(work[:, k0:k1, c0:c0 + w], work[:, k0:k1, c0:c0 + w],
                                                gapped[:, k0:k1, ga], ALU.subtract)
                        if s:
                            ins.then_inc(opnd_ready, kg)
                        else:
                            ch.did(ins)
                    next_piece()
                for piece in pieces:
                    mod_column(0, piece)
                low_next(0)
                vec.wait_ge(mod_done, 2 + MOD_PIECES)
                coefficients(0, (1, 2, 3))
                for m in range(KD):
                    if not low_at["mix0"][m][0]:
                        low_operand(opnd["mix0"], m)

            def ffn_in(l):
                s = lin[f"ffn_in{l}"]
                more = l + 1 < DEPTH
                p0 = l * PAIRS

                def at(v, i):
                    return v if i is None else i * 4 + v

                def group(i, first=False, base=0):
                    for j in range(4):
                        c = s.conv0 + base + j
                        pair = p0 + (base + j) // 2
                        half = (lambda v: v) if i is None else (lambda v: i * 2 + v)
                        if i is not None or base + j + 1 < FFN_TILES:
                            low_part(s, base + j + 1, i, 4)
                        else:
                            low_next(s.n0 + base + j + 1)
                        b = tile_bank[(s.t0 + base + j) % BANKS]
                        k = bass.ds(at(base + j, i), 1)
                        tap = [taps[:, l, k, q:q + 1].rearrange("p a b -> p (a b)") for q in (0, 2)]
                        vec.wait_ge(acc_ready, at(c + 1, i))
                        vec.scalar_tensor_tensor(out=acc[:, c % 4, 1:COLS], in0=b[:, 0:COLS - 1], scalar=tap[0],
                                                 in1=acc[:, c % 4, 1:COLS], op0=ALU.mult, op1=ALU.add).then_inc(tap_first, 1)
                        if j % 2 == 0 and not (first and j == 0):
                            vec.wait_ge(g_hi_ready, half(pair))
                            q = bass.ds(half(pair - p0 - 1), 1)
                            vec.tensor_tensor(g_lo[:, q, :].rearrange("p a n -> p (a n)"), gate[:, (pair - 1) % 2, :],
                                              g_hi[:, q, :].bitcast(F32).rearrange("p a n -> p (a n)"),
                                              ALU.subtract).then_inc(g_lo_ready, 1)
                        vec.wait_ge(tap_first, at(c + 1, i))
                        vec.scalar_tensor_tensor(out=acc[:, c % 4, 0:COLS - 1], in0=b[:, 1:COLS], scalar=tap[1],
                                                 in1=acc[:, c % 4, 0:COLS - 1], op0=ALU.mult, op1=ALU.add
                                                 ).then_inc(conv_done, 1)
                        if j % 2:
                            vec.wait_ge(sil_ready, half(pair + 1))
                            vec.wait_ge(conv_done, at(4 + c + 1, i))
                            vec.tensor_tensor(gate[:, pair % 2, :], sil[:, pair % 2, :], acc[:, c % 4, :],
                                              ALU.mult).then_inc(gate_ready, 1)
                            if more:
                                mod_column(l + 1, base // 2 + j // 2, i, 2)

                group(None, first=True)
                with vec.Fori(0, FFN_TILES // 4 - 2) as i:
                    group(i, base=4)
                group(None, base=FFN_TILES - 4)
                vec.wait_ge(g_hi_ready, p0 + PAIRS)
                vec.tensor_tensor(g_lo[:, PAIRS - 1, :], gate[:, (p0 + PAIRS - 1) % 2, :],
                                  g_hi[:, PAIRS - 1, :].bitcast(F32), ALU.subtract).then_inc(g_lo_ready, 1)
            def ssd_conv():
                s = lin["ssd_conv"]

                def tile(base, j, i):
                    at = (lambda v: v) if i is None else (lambda v: i * 4 + v)
                    t, c = base + j, s.conv0 + base + j
                    if i is not None or t + 1 < s.chunks:
                        low_part(s, t + 1, i, 4)
                    else:
                        low_next(s.n0 + t + 1)
                    b = tile_bank[(s.t0 + t) % BANKS]
                    k = bass.ds(at(t), 1)
                    tap = [ssd_taps[:, k, q:q + 1].rearrange("p a b -> p (a b)") for q in (0, 2)]
                    left = xbc[:, k, 1:COLS].rearrange("p a n -> p (a n)")
                    right = xbc[:, k, 0:COLS - 1].rearrange("p a n -> p (a n)")
                    vec.wait_ge(acc_ready, at(c + 1))
                    vec.scalar_tensor_tensor(out=left, in0=b[:, 0:COLS - 1], scalar=tap[0], in1=left,
                                             op0=ALU.mult, op1=ALU.add).then_inc(tap_first, 1)
                    vec.wait_ge(tap_first, at(c + 1))
                    vec.scalar_tensor_tensor(out=right, in0=b[:, 1:COLS], scalar=tap[1], in1=right,
                                             op0=ALU.mult, op1=ALU.add).then_inc(conv_done, 1)

                for j in range(4):
                    tile(0, j, None)
                with vec.Fori(0, s.chunks // 4 - 2) as i:
                    for j in range(4):
                        tile(4, j, i)
                for j in range(4):
                    tile(s.chunks - 4, j, None)
                lows_of(lin["ssd_z"])
                lows_of(lin["ssd_dt"])

            def dt_prepare():
                n = [0]

                def link(ins):
                    n[0] += 1
                    ins.then_inc(z_dt, 1)
                    vec.wait_ge(z_dt, n[0])

                v, mag, e, r = (sq[:, j, 0:192] for j in (1, 2, 3, 0))
                q = sq[:, 1, 192:384]
                v3 = v.rearrange("p (c h) -> p c h", c=3)
                vec.wait_ge(dt_pe, 1)
                link(vec.tensor_tensor(v3, stat_bank[:, 0:192].rearrange("p (c h) -> p c h", c=3),
                                       dt_rows[:, 0, :].unsqueeze(1).broadcast_to([P, 3, NDT]), ALU.add))
                link(vec.tensor_scalar(mag, v, -1.0, None, ALU.mult))
                link(vec.tensor_tensor(mag, mag, v, ALU.max))
                vec.wait_ge(dt_act, 2)
                link(vec.tensor_scalar(r, e, 2.0, None, ALU.add))
                link(vec.reciprocal(r, r))
                link(vec.tensor_tensor(r, r, e, ALU.mult))
                link(vec.tensor_tensor(mag, r, r, ALU.mult))
                link(vec.tensor_scalar(q, mag, 1.0 / 15, None, ALU.mult))
                for k in (13, 11, 9, 7, 5, 3):
                    link(vec.scalar_tensor_tensor(out=q, in0=q, scalar=1.0 / k, in1=mag, op0=ALU.add, op1=ALU.mult))
                link(vec.scalar_tensor_tensor(out=q, in0=q, scalar=1.0, in1=r, op0=ALU.add, op1=ALU.mult))
                link(vec.tensor_scalar(v, v, 0.0, None, ALU.max))
                flat_dt = dtv[:, :, :].rearrange("p c h -> p (c h)")
                link(vec.scalar_tensor_tensor(out=flat_dt, in0=q, scalar=2.0, in1=v, op0=ALU.mult, op1=ALU.add))
                link(vec.scalar_tensor_tensor(out=adt[:, :, :], in0=sq[:, 3, 192:256].unsqueeze(1).broadcast_to([P, 3, NDT]),
                                              scalar=-1.0, in1=dtv[:, :, :], op0=ALU.mult, op1=ALU.mult))
                assert n[0] == DT_DVE - 2
                vec.wait_ge(dt_pe, 2)
                cum = rstd_bank[:, 0:192].rearrange("p (c h) -> p c h", c=3)
                total = rstd_bank[:, 192:384].rearrange("p (c h) -> p c h", c=3)
                ch.did(vec.tensor_scalar(neg_cum[:, :, :], cum, -1.0, None, ALU.mult))
                ch.did(vec.tensor_copy(full_decay[:, :, :], total))
                ch.wait()
                link(vec.tensor_tensor(to_end[:, :, :], full_decay[:, :, :], neg_cum[:, :, :], ALU.add))
                vec.wait_ge(dt_act, 4)
                link(vec.tensor_tensor(to_end[:, :, :], to_end[:, :, :], dtv[:, :, :], ALU.mult))
                assert n[0] == DT_DVE

            def scan_dve():
                skip = ssd_cols[:, 0, :]
                ch.did(vec.tensor_tensor(skip, skip, ssd_cols[:, 1, :], ALU.add))
                ch.wait()

                def output(g, c, u):
                    vec.wait_ge(s_y, u + 1)
                    c0 = CHUNKS[c][0]
                    for t in range(2):
                        k = 2 * g + t
                        ins = vec.scalar_tensor_tensor(
                            out=xbc[:, k, c0:c0 + P], in0=xbc[:, k, c0:c0 + P], scalar=skip[:, k:k + 1],
                            in1=(mod_bank, col_bank)[u % 2][:, t * P:(t + 1) * P], op0=ALU.mult, op1=ALU.add)
                        if t:
                            ins.then_inc(s_out, 1)
                        else:
                            ch.did(ins)

                last = None
                for g, c, u, v in steps():
                    vec.wait_ge(s_copied, u + 1)
                    if u:
                        vec.wait_ge(s_w, 2 * u)
                    for d in range(2):
                        ch.did(vec.tensor_tensor(cb_mask[:, d, :], turned[:, u % 2, P + GW:], tri[:, d, :], ALU.mult))
                    masks = ch.n
                    if u >= 2:
                        vec.wait_ge(s_y, u - 1)
                    for d in range(2):
                        vec.wait_ge(s_cum, 2 * u + d + 1)
                        if c:
                            vec.wait_ge(s_cexp, 2 * v + d + 1)
                        for h in range(HPG):
                            col = d * SSD_HEADS + g * HPG + h
                            ins = vec.tensor_scalar(decay[:, u % 2, d, h * P:(h + 1) * P],
                                                    tile_bank[2 + d][:, h * P:(h + 1) * P],
                                                    neg_cum[:, c, col:col + 1], 0.0, ALU.add, ALU.min)
                            if h == HPG - 1:
                                ins.then_inc(s_seg, 1)
                            else:
                                ch.did(ins)
                    vec.wait_ge(s_state, u + 1)
                    if c == 0:
                        if g:
                            vec.wait_ge(state_stored, 16 * g)
                        vec.tensor_copy(state_new, stat_bank[:, :].rearrange("p (d n) -> p d n", d=2)).then_inc(s_taken, 1)
                    else:
                        d = c - 1
                        h0 = d * SSD_HEADS + g * HPG
                        if c == 1:
                            vec.wait_ge(state_loaded[g % 2], 16 * (g // 2 + 1))
                        if g:
                            vec.wait_ge(s_y, 3 * g)
                        n = ch.did(vec.tensor_tensor(
                            state1[:, d, :].rearrange("p (h q) -> p h q", h=HPG),
                            state0[:, g % 2, d, :].rearrange("p (h q) -> p h q", h=HPG),
                            full_decay[:, c, h0:h0 + HPG].unsqueeze(2).broadcast_to([P, HPG, HEAD]), ALU.mult))
                        ch.wait(n)
                        vec.tensor_tensor(state1[:, d, :], state1[:, d, :], stat_bank[:, d * GW:(d + 1) * GW],
                                          ALU.add).then_inc(s_taken, 1)
                    ch.wait(masks)
                    for d in range(2):
                        vec.wait_ge(s_exp, 2 * u + d + 1)
                        w = decay[:, u % 2, d, :].rearrange("p (h i) -> p h i", h=HPG)
                        vec.tensor_tensor(w, w, cb_mask[:, d, :].unsqueeze(1).broadcast_to([P, HPG, P]),
                                          ALU.mult).then_inc(s_w, 1)
                    if last is not None:
                        output(*last)
                    last = (g, c, u)
                output(*last)

            def ssd_norm():
                vec.wait_ge(s_out, 3 * GROUPS)
                for m in range(KI):
                    vec.tensor_tensor(xbc[:, m, :], xbc[:, m, :], zt[:, m, :], ALU.mult).then_inc(yz_ready, 1)
                take_rstd("ssd")
                e, base, k = norm["ssd"]
                vec.wait_ge(rstd_spread, e + 1)
                vec.wait_ge(yz_ready, KI)
                o = opnd["ssd_y"]
                for m in range(KI + 2):
                    if m < KI:
                        vec.scalar_tensor_tensor(out=xbc[:, m, :], in0=xbc[:, m, :], scalar=ssd_cols[:, 2, m:m + 1],
                                                 in1=rstd_bank[:, 0:COLS], op0=ALU.mult, op1=ALU.mult
                                                 ).then_inc(opnd_ready, 1)
                    if m >= 2 and not low_at["ssd_y"][m - 2][0]:
                        vec.wait_ge(opnd_hi, o + m - 1)
                        vec.tensor_tensor(y_lo[:, m - 2, :], xbc[:, m - 2, :], y_hi[:, m - 2, :].bitcast(F32),
                                          ALU.subtract).then_inc(lo_dve, 1)

            def conf_mix():
                vec.wait_ge(late_loaded, 16)
                n = 0

                def tap(m, k):
                    return 2 * TAPS31 * (m // 2) + 2 * k + m % 2

                for q in range(KD // 2):
                    for m in (2 * q, 2 * q + 1):
                        vec.wait_ge(glu_ready, 1 + 2 * m + 2)
                        vec.tensor_scalar(convolved[:, m, :], glu[:, m, 0:CONVOLVED],
                                          conf_tab[:, m * TAPS31:m * TAPS31 + 1],
                                          conf_tab[:, C_DWB + m:C_DWB + m + 1], ALU.mult, ALU.add).then_inc(conf_tap, 1)
                    with vec.Fori(0, (TAPS31 - 1) // 3) as i:
                        for r in range(3):
                            for m in (2 * q, 2 * q + 1):
                                vec.wait_ge(conf_tap, i * 6 + (tap(m, r) + 1))
                                vec.scalar_tensor_tensor(
                                    out=convolved[:, m, :], in0=glu[:, m, bass.ds(i * 3 + (1 + r), CONVOLVED)],
                                    scalar=conf_tab[:, bass.ds(i * 3 + (m * TAPS31 + 1 + r), 1)],
                                    in1=convolved[:, m, :], op0=ALU.mult, op1=ALU.add).then_inc(conf_tap, 1)
                vec.wait_ge(ln_sums, 1)
                vec.tensor_copy(ln_mean[:, :], stat_bank[:, 0:3]).then_inc(ln_mean_ready, 1)
                vec.wait_ge(ln_spread, 1)
                vec.wait_ge(conf_tap, KD * TAPS31)
                for m in range(KD):
                    for c0, w, k in STREAMS:
                        ins = vec.tensor_tensor(work[:, m, c0:c0 + w], convolved[:, m, CONVOLVED_AT[k]:CONVOLVED_AT[k] + w],
                                                rstd_bank[:, c0:c0 + w], ALU.subtract)
                        if k:
                            ins.then_inc(ln_centred, 1)
                        else:
                            ch.did(ins)
                take_rstd("ln")
                vec.wait_ge(rstd_spread, norm["ln"][0] + 1)
                vec.wait_ge(ln_centred, KD)
                ch.wait()
                for m in range(KD):
                    vec.tensor_tensor(work[:, m, :], work[:, m, :], rstd_bank[:, 0:COLS], ALU.mult).then_inc(ln_scaled, 1)
                for m in range(KD):
                    low_operand(opnd["mid2"], m)

            def attn_mix():
                lows_of(lin["qkv"])
                vec.wait_ge(late_loaded, 48)
                vec.wait_ge(qk_std_ready, 1)
                vec.reciprocal(qk_rstd[:, :], qk_std[:, :]).then_inc(qk_rstd_ready, 1)

                def rotate(t):
                    vec.wait_ge(qk_rot, t + 1)
                    if t >= 2:
                        vec.wait_ge(qk_turned, t - 1)
                    vec.tensor_tensor(rot_sin[:, t % 2, :], tile_bank[t % 2][:, 0:LAT], attn_tab[:, A_SIN:A_SIN + LAT],
                                      ALU.mult).then_inc(qk_sin, 1)
                    to = q_turned[:, t, :] if t < AH else k_all[:, t - AH, PAST:]
                    vec.wait_ge(qk_cos, t + 1)
                    vec.wait_ge(qk_sin, t + 1)
                    vec.tensor_tensor(to, to, rot_sin[:, t % 2, :], ALU.add).then_inc(qk_turned, 1)

                for t in range(QK + 1):
                    if t < QK:
                        g = A_G + (t >= AH)
                        vec.wait_ge(qk_spread, t + 1)
                        vec.scalar_tensor_tensor(out=qkv[:, t, :], in0=qkv[:, t, :], scalar=attn_tab[:, g:g + 1],
                                                 in1=(rstd_bank, mod_bank)[t % 2][:, 0:COLS], op0=ALU.mult,
                                                 op1=ALU.mult).then_inc(qk_normed, 1)
                    if t:
                        rotate(t - 1)
                o = opnd["mid3"]
                for u in range(3 * AH + 1):
                    if u < 3 * AH:
                        w = P if u % 3 == 0 else PAST + LAT
                        vec.wait_ge(att_score, u + 1)
                        if u >= 2:
                            vec.wait_ge(att_max, u - 1)
                        vec.tensor_reduce(row_max[:, u % 2:u % 2 + 1], tile_bank[u % 2][:, 0:w], AX.X, ALU.max
                                          ).then_inc(att_rowmax, 1)
                        vec.wait_ge(att_rowmax, u + 1)
                        if u >= 2:
                            vec.wait_ge(att_exp, u - 1)
                        vec.tensor_scalar(neg_max[:, u % 2:u % 2 + 1], row_max[:, u % 2:u % 2 + 1], -SCALE, None,
                                          ALU.mult).then_inc(att_max, 1)
                    if u:
                        b = u - 1
                        w = P if b % 3 == 0 else PAST + LAT
                        vec.wait_ge(att_exp, b + 1)
                        if b >= 2:
                            vec.wait_ge(att_prob, b - 1)
                        vec.reciprocal(inv_sum[:, b % 2:b % 2 + 1], row_sum[:, b % 2:b % 2 + 1]).then_inc(att_inv, 1)
                        vec.wait_ge(att_inv, b + 1)
                        vec.tensor_scalar(prob[:, b % 2, 0:w], prob[:, b % 2, 0:w], inv_sum[:, b % 2:b % 2 + 1], None,
                                          ALU.mult).then_inc(att_prob, 1)
                for h in range(AH):
                    low_operand(o, h)

            def lows_of(s):
                for j in range(s.chunks):
                    low_next(s.n0 + j + 1)

            vec.memset(cond32[:, :, :], 0.0).then_inc(vec_init, 1)
            vec.memset(work[:, :, :], 0.0).then_inc(vec_init, 1)
            vec.memset(gapped[:, :, :], 0.0).then_inc(vec_init, 1)
            vec.memset(spare[:, 3:4], 0.0).then_inc(w_low_dve, RAW_SLOTS)
            vec.memset(spare[:, 0:1], 0.0).then_inc(conv_done, 4)
            vec.memset(spare[:, 1:2], 0.0).then_inc(mod_done, 2)
            vec.wait_ge(loaded0, LOADS0)
            vec.wait_ge(vec_init, 3)
            vec.wait_ge(consts, CONSTS)
            vec.memset(spare[:, 2:3], 0.0).then_inc(x_ready, KD)
            with vec.Fori(0, MOD_FIRST // 2) as i:
                for j in range(2):
                    mod_column(0, j, i, 2)
            vec.wait_ge(mod_done, 2 + MOD_FIRST)
            coefficients(0, (0,))
            take_rstd("pre0.0")
            modulate_gapped()
            pool_mix()
            for l in range(DEPTH):
                if l:
                    vec.wait_ge(mod_done, 2 + (l + 1) * MOD_PIECES)
                    vec.wait_ge(x_ready, KD * (2 * l + 1))
                    coefficients(l)
                if l == 0:
                    low_next(1)
                    low_next(2)
                    s = lin["pool"]
                if l == 1:
                    take_rstd("pre1.0")
                    modulate(1, "pre1.0", 0, KD * 2, "mix1")
                    ssd_conv()
                    dt_prepare()
                    scan_dve()
                    ssd_norm()
                    lows_of(lin["ssd_out"])
                if l == 2:
                    vec.memset(spare[:, 7:8], 0.0).then_inc(
                        w_low_dve, sum(lin[name].chunks for name in linears(2)))
                    take_rstd("pre2.0")
                    modulate(2, "pre2.0", 0, KD * 4, "mix2")
                    conf_mix()
                    low_next(lin["conf_out"].n0 + KD)
                if l == 3:
                    take_rstd("pre3.0")
                    modulate(3, "pre3.0", 0, KD * 6, "mix3")
                    attn_mix()
                    lows_of(lin["attn_out"])
                s = lin[linears(l)[-1]]
                take_rstd(f"post{l}.0")
                residual(f"post{l}.0", 4 + s.evac0 + KD)
                take_rstd(f"pre{l}.1")
                modulate(l, f"pre{l}.1", 1, KD * (2 * l + 2) - KD, f"ffn{l}")
                ffn_in(l)
                s = lin[f"ffn_out{l}"]
                lows_of(s)
                take_rstd(f"post{l}.1")
                residual(f"post{l}.1", 4 + s.evac0 + KD)
                if l + 1 < DEPTH:
                    mod_column(l + 1, MOD_PIECES - 2)
                    mod_column(l + 1, MOD_PIECES - 1)

        @block.tensor
        def _(ten):
            ch = Chain(ten, pe)

            def products(bank_ap, hi, lo, w_tile, n, first, last):
                w = (w_hi[:, n % SPLIT_SLOTS, w_tile * P:(w_tile + 1) * P],
                     w_lo[:, n % SPLIT_SLOTS, w_tile * P:(w_tile + 1) * P])
                ten.matmul(bank_ap, w[0], hi, start=first, stop=False)
                ten.matmul(bank_ap, w[0], lo, start=False, stop=False)
                return ten.matmul(bank_ap, w[1], hi, start=False, stop=last)

            def chunk_ready(n, i=None, per=0):
                ready = RAW_SLOTS + n + 1
                ten.wait_ge(w_low_pool, ready if i is None else i * per + ready)
                ten.wait_ge(w_low_dve, ready if i is None else i * per + ready)

            def mod_rows_of(l, piece, i=None, per=0):
                g = l * MOD_PIECES + piece
                at = (lambda v: v) if i is None else (lambda v: i * per + v)
                ten.wait_ge(mod_loaded[g % 2], 16 * (g // 2 + 1) + (0 if i is None else i * (8 * per)))
                ten.wait_ge(rows_ready, at(2 + g))
                for half in range(2):
                    for q in range(4):
                        k = 2 * q + half
                        ins = ten.matmul(mod_bank[32 * q:32 * q + 32, 0:MOD_COLS],
                                         cond32[:, k, :], mod_raw[:, g % 2, k * MOD_COLS:(k + 1) * MOD_COLS],
                                         start=half == 0, stop=half == 1, skip_group_check=True)
                ins.then_inc(mod_used, 1)

            def mod_columns_of(l, piece, i=None, per=0):
                g = l * MOD_PIECES + piece
                at = (lambda v: v) if i is None else (lambda v: i * per + v)
                ten.wait_ge(rows_ready, at(2 + g + 1))
                ten.wait_ge(mod_done, at(2 + g))
                for t in range(MOD_TILES):
                    c = 2 * t
                    ins = ten.matmul(col_bank[:, c:c + 2], mod_rows[:, g % 2, t * P:(t + 1) * P], cond_sel[:, :],
                                     start=True, stop=True, skip_group_check=True)
                ins.then_inc(cols_ready, 1)

            def column_sums(name, col=0):
                _, base, _ = norm[name]
                for t, size, adds in sum_groups[name][0]:
                    if size > 1:
                        ten.wait_ge(sq_added, adds)
                    else:
                        ten.wait_ge(sq_ready, base + t + 1)
                    for c, (c0, s) in enumerate(CHUNKS):
                        ins = ten.matmul(stat_bank[:, c:c + 1], sq[:, (base + t) % 4, c0:c0 + P], mean_col[:, col:col + 1],
                                         start=t == sum_groups[name][0][0][0] and c == 0, stop=True,
                                         skip_group_check=True)
                    ins.then_inc(sq_used, 1)

            def spread_columns(b, src, at):
                for c, (c0, s) in enumerate(CHUNKS):
                    w = P if c == 1 else P + 1
                    ins = ten.matmul(b[:, c0:c0 + w], src[:, at + c:at + c + 1].broadcast_to([P, P]), ident[:, 0:w],
                                     start=c == 0, stop=True, skip_group_check=True)
                return ins

            def spread(name):
                e, base, k = norm[name]
                ten.wait_ge(rstd_ready, e + 1)
                spread_columns(rstd_bank, rstd, 0).then_inc(rstd_spread, 1)

            def norm_of(name, col=0):
                column_sums(name, col)
                spread(name)

            def ffn_in(l):
                s = lin[f"ffn_in{l}"]
                more = l + 1 < DEPTH
                with ten.Fori(0, FFN_TILES // 4) as i:
                    for j in range(4):
                        chunk_ready(s.n0 + j, i, 4)
                        ten.wait_ge(conv_done, i * 4 + (s.conv0 + j + 1))
                        b = tile_bank[(s.t0 + j) % BANKS][:, 0:COLS]
                        for k in range(KD):
                            if j == 0:
                                low_ready(ten, f"ffn{l}", k)
                            ins = products(b, h_hi[:, k, :], h_lo[:, k, :], k, s.n0 + j, k == 0, k == KD - 1)
                        ins.then_inc(w_used, 1)
                        if more:
                            (mod_columns_of if j % 2 else mod_rows_of)(l + 1, j // 2, i, 2)

            def out_product(s, hi, lo, name, before, g_ready):
                with ten.Fori(0, 2) as i:
                    for m in range(4):
                        before(m)
                        ten.wait_ge(evac, i * 4 + (s.evac0 + m + 1))
                        b = tile_bank[(s.t0 + m) % BANKS][:, 0:COLS]
                        for half in range(s.per):
                            n = s.n0 + s.per * m + half
                            chunk_ready(n, i, 4 * s.per)
                            for k in range(s.tiles):
                                kk = half * s.tiles + k
                                if m == 0:
                                    g_ready(kk)
                                ins = products(b, hi[:, kk, :], lo[:, kk, :], k, n, kk == 0, kk == s.per * s.tiles - 1)
                            ins.then_inc(w_used, 1)
                norm_of(name)

            def plain_product(s, name, before):
                def tile(j, i=None):
                    chunk_ready(s.n0 + j, i, 4)
                    before(j, i)
                    b = tile_bank[(s.t0 + j) % BANKS][0:s.width, 0:COLS]
                    for k in range(KD):
                        if j == 0:
                            low_ready(ten, name, k)
                        w = s.width
                        wh = w_hi[:, (s.n0 + j) % SPLIT_SLOTS, k * w:(k + 1) * w]
                        wl = w_lo[:, (s.n0 + j) % SPLIT_SLOTS, k * w:(k + 1) * w]
                        ten.matmul(b, wh, h_hi[:, k, :], start=k == 0, stop=False)
                        ten.matmul(b, wh, h_lo[:, k, :], start=False, stop=False)
                        ins = ten.matmul(b, wl, h_hi[:, k, :], start=False, stop=k == KD - 1)
                    ins.then_inc(w_used, 1)

                if s.chunks >= 8:
                    with ten.Fori(0, s.chunks // 4) as i:
                        for j in range(4):
                            tile(j, i)
                else:
                    for j in range(s.chunks):
                        tile(j)

            def dt_prepare():
                s = lin["ssd_dt"]
                ten.wait_ge(evac, 4 + s.evac0 + 1)
                for c, (c0, _) in enumerate(CHUNKS):
                    ins = ten.transpose(stat_bank[:, c * NDT:(c + 1) * NDT], sq[0:NDT, 0, c0:c0 + P],
                                        ident[0:NDT, 0:NDT])
                ins.then_inc(dt_pe, 1)
                ten.wait_ge(z_dt, DT_DVE - 2)
                cum = rstd_bank[:, 0:192].rearrange("p (c h) -> p c h", c=3)
                for d in range(2):
                    hs = slice(d * SSD_HEADS, (d + 1) * SSD_HEADS)
                    ten.matmul(cum[:, :, hs], tri[:, d, :], adt[:, :, hs], start=True, stop=True, skip_group_check=True)
                ten.matmul(rstd_bank[:, 192:384], ones[:, :], adt[:, :, :].rearrange("p c h -> p (c h)"),
                           start=True, stop=True, skip_group_check=True).then_inc(dt_pe, 1)

            def scan_pe():
                def output(g, c, u, v):
                    if u >= 2:
                        ten.wait_ge(s_out, u - 1)
                    ten.wait_ge(s_w, 2 * u + 2)
                    ten.wait_ge(s_xdt, 2 * u + 2)
                    if c:
                        ten.wait_ge(s_cs, 2 * v + 2)
                        ten.wait_ge(s_taken, 3 * g + 3)
                        ten.wait_ge(state_loaded[g % 2], 16 * (g // 2 + 1))
                    b = (mod_bank, col_bank)[u % 2]
                    for h in range(HPG):
                        o = b[HEAD * (h % 2):HEAD * (h % 2 + 1), h // 2 * P:(h // 2 + 1) * P]
                        hs, ws = slice(h * HEAD, (h + 1) * HEAD), slice(h * P, (h + 1) * P)
                        terms = [(x_dt[:, u % 2, d, hs], decay[:, u % 2, d, ws]) for d in range(2)]
                        if c:
                            for d in range(2):
                                st = state0[:, g % 2, d, hs] if d == c - 1 else state1[:, d, hs]
                                terms.append((st, c_scaled[:, u % 2, d, ws]))
                        for n, (lhs, rhs) in enumerate(terms):
                            ins = ten.matmul(o, lhs, rhs, start=n == 0, stop=n == len(terms) - 1)
                    ins.then_inc(s_y, 1)

                last = None
                ten.wait_ge(xbc_ready, SSD_CONV_TILES)
                ten.wait_ge(z_dt, DT_DVE)
                for g, c, u, v in steps():
                    c0 = CHUNKS[c][0]
                    if u >= 2:
                        ten.wait_ge(s_copied, u - 1)
                    b = tile_bank[u % 2]
                    cols = slice(c0, c0 + P)
                    ten.transpose(b[:, 0:P], xbc[:, KI + g, cols], ident[:, 0:P])
                    for t in range(2):
                        ten.transpose(b[:, (t + 1) * P:(t + 2) * P], xbc[:, 2 * g + t, cols], ident[:, 0:P])
                    ten.matmul(b[:, 3 * P:], xbc[:, KI + g, cols], xbc[:, KI + GROUPS + g, cols],
                               start=True, stop=True).then_inc(s_turned, 1)
                    for d in range(2):
                        if u:
                            ten.wait_ge(s_seg, 2 * (u - 1) + d + 1)
                        for h in range(HPG):
                            col = d * SSD_HEADS + g * HPG + h
                            ins = ten.matmul(tile_bank[2 + d][:, h * P:(h + 1) * P],
                                             adt[:, c, col:col + 1].broadcast_to([P, P]), tri[:, d, :],
                                             start=True, stop=True, skip_group_check=True)
                        ins.then_inc(s_cum, 1)
                    ten.wait_ge(s_copied, u + 1)
                    ten.wait_ge(s_xend, u + 1)
                    if u:
                        ten.wait_ge(s_taken, u)
                    for d in state_dirs(c):
                        ins = ten.matmul(stat_bank[:, d * GW:(d + 1) * GW], turned[:, u % 2, 0:P], x_end[:, d, :],
                                         start=True, stop=True, skip_group_check=True)
                    ins.then_inc(s_state, 1)
                    if last is not None:
                        output(*last)
                    last = (g, c, u, v)
                output(*last)

            def conf_norm_pe():
                for m in range(KD):
                    if m % 2 == 0:
                        ten.wait_ge(conf_tap, 2 * TAPS31 * (m // 2 + 1))
                    for c, (c0, s) in enumerate(CHUNKS):
                        at = c0 - (LAT0 if s else 0) + CONVOLVED_AT[s]
                        ins = ten.matmul(stat_bank[:, c:c + 1], convolved[:, m, at:at + P], mean_col[:, 0:1],
                                         start=m == 0 and c == 0, stop=True, skip_group_check=True)
                ins.then_inc(ln_sums, 1)
                ten.wait_ge(ln_mean_ready, 1)
                spread_columns(rstd_bank, ln_mean, 0).then_inc(ln_spread, 1)
                norm_of("ln")

            def attn_pe():
                s = lin["qkv"]
                ten.wait_ge(evac, 4 + s.evac0 + s.chunks)
                e, base, _ = norm["qk"]
                for kv in range(AKV):
                    for c, (c0, _) in enumerate(CHUNKS):
                        ins = ten.transpose(tile_bank[2 + kv][:, c * AD:(c + 1) * AD], qkv[:, QK + kv, c0:c0 + P],
                                            ident[:, 0:P])
                    ins.then_inc(v_turned, 1)
                for t in range(QK):
                    ten.wait_ge(sq_ready, base + t + 1)
                    for c, (c0, _) in enumerate(CHUNKS):
                        ins = ten.matmul(stat_bank[:, 3 * t + c:3 * t + c + 1], sq[:, (base + t) % 4, c0:c0 + P],
                                         mean_col[:, 2:3], start=True, stop=True, skip_group_check=True)
                    ins.then_inc(sq_used, 1)
                ten.wait_ge(qk_rstd_ready, 1)
                ten.wait_ge(late_loaded, 48)
                for t in range(QK + 1):
                    if t < QK:
                        if t >= 2:
                            ten.wait_ge(qk_normed, t - 1)
                        spread_columns((rstd_bank, mod_bank)[t % 2], qk_rstd, 3 * t).then_inc(qk_spread, 1)
                    if t:
                        r = t - 1
                        ten.wait_ge(qk_normed, r + 1)
                        if r >= 2:
                            ten.wait_ge(qk_sin, r - 1)
                        ten.matmul(tile_bank[r % 2][:, 0:LAT], attn_tab[:, A_PERM:A_PERM + AD],
                                   qkv[:, r, LAT0:LAT0 + LAT], start=True, stop=True).then_inc(qk_rot, 1)
                ten.wait_ge(qk_turned, QK)
                ten.wait_ge(v_copied, AKV)

                def scores(h, c, u):
                    if u >= 2:
                        ten.wait_ge(att_exp, u - 1)
                    kv = h // REP
                    q = q_turned[:, h, (c - 1) * P:c * P] if c else qkv[:, h, 0:CTX]
                    keys = k_all[:, kv, :] if c else qkv[:, AH + kv, 0:CTX]
                    ten.matmul(tile_bank[u % 2][:, 0:PAST + LAT if c else CTX], q, keys, start=True, stop=True
                               ).then_inc(att_score, 1)

                def turn(h, c, u):
                    ten.wait_ge(att_prob, u + 1)
                    if u >= 2:
                        ten.wait_ge(att_pt, u - 1)
                    for k in range(3 if c else 1):
                        ins = ten.transpose(tile_bank[2 + u % 2][:, k * P:(k + 1) * P], prob[:, u % 2, k * P:(k + 1) * P],
                                            ident[:, 0:P])
                    ins.then_inc(att_turned, 1)

                def values(h, c, u):
                    ten.wait_ge(att_pt, u + 1)
                    if u >= 2:
                        copied_out(ten, u - 2)
                    kv = h // REP
                    own = v_rows[:, kv, :]
                    if c:
                        v = [attn_tab[:, A_V + kv * AD:A_V + (kv + 1) * AD], own[:, AD:2 * AD], own[:, 2 * AD:]]
                    else:
                        v = [own[:, 0:AD]]
                    for k, rows in enumerate(v):
                        ins = ten.matmul((mod_bank, col_bank)[u % 2][:, 0:P], rows, prob_t[:, u % 2, k * P:(k + 1) * P],
                                         start=k == 0, stop=k == len(v) - 1)
                    ins.then_inc(att_pv, 1)

                every = list(units())
                for n in range(len(every) + 3):
                    if n < len(every):
                        scores(*every[n])
                    if 2 <= n < len(every) + 2:
                        turn(*every[n - 2])
                    if n >= 3:
                        values(*every[n - 3])

            ten.wait_ge(cond_ready, 1)
            ten.wait_ge(consts, CONSTS)
            ten.matmul(mod_bank[:, 0:1], ident[:, 0:P], ident[:, P:P + 1], start=True, stop=True).then_inc(cols_ready, 2)
            with ten.Fori(0, MOD_FIRST // 2) as i:
                for j in range(2):
                    mod_rows_of(0, j, i, 2)
                    mod_columns_of(0, j, i, 2)
            norm_of("pre0.0")
            with ten.Fori(0, (MOD_PIECES - MOD_FIRST) // 2) as i:
                for j in range(2):
                    mod_rows_of(0, MOD_FIRST + j, i, 2)
                    mod_columns_of(0, MOD_FIRST + j, i, 2)
            for l in range(DEPTH):
                if l == 0:
                    s = lin["pool"]
                    for m in range(KD):
                        n = s.n0 + m // 4
                        chunk_ready(n)
                        group = m // 2
                        if m >= 4:
                            ten.wait_ge(evac, 1 + m)
                        low_ready(ten, "mix0", 2 * group)
                        low_ready(ten, "mix0", 2 * group + 1)
                        for k in range(2):
                            ins = products(tile_bank[(s.t0 + m) % BANKS][:, 0:COLS], h_hi[:, 2 * group + k, :],
                                           h_lo[:, 2 * group + k, :], (m % 4) * 2 + k, n, k == 0, k == 1)
                        if m % 4 == 3:
                            ins.then_inc(w_used, 1)
                        if m % 4 != 3:
                            ch.did(ins)
                    norm_of("post0.0")
                if l == 1:
                    conv, z, dt = lin["ssd_conv"], lin["ssd_z"], lin["ssd_dt"]
                    plain_product(conv, "mix1", lambda j, i: ten.wait_ge(conv_done, i * 4 + (conv.conv0 + j + 1)))

                    def z_before(j, i):
                        ten.wait_ge(conv_done, conv.conv0 + SSD_CONV_TILES + j + 1)
                        ten.wait_ge(evac, i * 4 + (z.evac0 + j + 1))

                    plain_product(z, "mix1", z_before)
                    plain_product(dt, "mix1", lambda j, i: ten.wait_ge(evac, dt.evac0 + 1))
                    dt_prepare()
                    scan_pe()
                    norm_of("ssd", 1)
                    out_product(lin["ssd_out"], y_hi, y_lo, "post1.0", lambda m: None,
                                lambda k: low_ready(ten, "ssd_y", k))
                if l == 2:
                    s = lin["conf_in"]
                    plain_product(s, "mix2", lambda j, i, s=s: ten.wait_ge(evac, i * 4 + (s.evac0 + j + 1)))
                    conf_norm_pe()
                    out_product(lin["conf_out"], h_hi, h_lo, "post2.0", lambda m: None,
                                lambda k: low_ready(ten, "mid2", k))
                if l == 3:
                    s = lin["qkv"]
                    plain_product(s, "mix3", lambda j, i, s=s: ten.wait_ge(evac, i * 4 + (s.evac0 + j + 1)))
                    attn_pe()
                    out_product(lin["attn_out"], h_hi, h_lo, "post3.0", lambda m: None,
                                lambda k: low_ready(ten, "mid3", k))
                norm_of(f"pre{l}.1")
                ffn_in(l)
                s = lin[f"ffn_in{l}"]
                out_product(lin[f"ffn_out{l}"], g_hi, g_lo, f"post{l}.1",
                            lambda m, s=s: ten.wait_ge(conv_done, s.conv0 + FFN_TILES + m + 1),
                            lambda k, l=l: ten.wait_ge(g_lo_ready, l * PAIRS + k + 1))
                if l + 1 < DEPTH:
                    for piece in (MOD_PIECES - 2, MOD_PIECES - 1):
                        mod_rows_of(l + 1, piece)
                        mod_columns_of(l + 1, piece)
                    norm_of(f"pre{l + 1}.0")


def columns(ctx_part, lat_part):
    out = np.zeros((P, KD, COLS), ctx_part.dtype)
    out[:, :, 0:CTX] = ctx_part.T.reshape(KD, P, CTX).transpose(1, 0, 2)
    out[:, :, LAT0:LAT0 + LAT] = lat_part.T.reshape(KD, P, LAT).transpose(1, 0, 2)
    return out


def tiles_of(w):
    k, m = w.shape
    return np.ascontiguousarray(w.reshape(k // P, P, m // P, P).transpose(2, 1, 0, 3)).reshape(m // P, P, k)


def per_partition(v, axis=-1):
    t = v.reshape(*v.shape[:-1], v.shape[-1] // P, P)
    return np.ascontiguousarray(np.moveaxis(t, -1, 0))


PAIRED = [t for p in range(PAIRS) for t in (p, PAIRS + p)]


def lay_out(i):
    d = {}
    d["x"] = columns(i["x_prompt"][0], i["x_sample"][0])
    d["cond"] = np.ascontiguousarray(np.stack([per_partition(i["c_ctx"]), per_partition(i["c"][0])], -1))
    d["gains"] = per_partition(i["norm_g"])
    d["b_mod"] = per_partition(i["b_mod"])
    d["pool_scale"] = per_partition(i["pool_scale"][0])
    d["taps"] = np.ascontiguousarray(np.stack(
        [per_partition(v)[:, :, PAIRED] for v in (i["ffn_dw"][:, 0], i["ffn_dw"][:, 1], i["ffn_dw"][:, 2], i["ffn_dw_b"])], -1))
    inv = np.ones((len(WINDOWS), CTX + LAT), np.float32)
    for g, win in enumerate(WINDOWS):
        at = 0
        for n in (CTX, LAT):
            t = np.arange(n)
            inv[g, at:at + n] = 1.0 / (np.minimum(t + win - win // 2, n) - np.maximum(t - win // 2, 0))
            at += n
    d["inv_count"] = np.broadcast_to(inv, (P, len(WINDOWS), CTX + LAT)).copy()
    d["w_mod"] = np.ascontiguousarray(
        i["w_mod"].reshape(DEPTH, KD, P, MOD_PIECES, MOD_COLS).transpose(0, 3, 2, 1, 4)
    ).reshape(DEPTH * MOD_PIECES, P, KD * MOD_COLS)
    pw = i["pool_w"][0].reshape(2, 2, 2, P, 2, P)
    d["pool"] = np.ascontiguousarray(pw.transpose(0, 3, 1, 4, 2, 5)).reshape(2, P, D)
    w = i["ssd_w_in"][0]
    d["ssd_conv"] = tiles_of(w[:, INNER:INNER + SSD_CONV_TILES * P])
    d["ssd_z"] = tiles_of(w[:, 0:INNER])
    d["ssd_dt"] = np.ascontiguousarray(
        w[:, INNER + SSD_CONV_TILES * P:].reshape(KD, P, NDT).transpose(1, 0, 2)).reshape(1, P, KD * NDT)
    d["ssd_out"] = np.ascontiguousarray(
        tiles_of(i["ssd_w_out"][0]).reshape(KD, P, 2, D).transpose(0, 2, 1, 3)).reshape(2 * KD, P, D)
    d["ssd_taps"] = np.ascontiguousarray(np.stack([per_partition(v) for v in (*i["ssd_conv_w"][0], i["ssd_conv_b"][0])], -1))
    d["dt_rows"] = np.broadcast_to(np.stack([i["ssd_dt_bias"][0].reshape(-1), i["ssd_a_log"][0].reshape(-1)]), (P, 2, NDT)).copy()
    d["ssd_cols"] = np.ascontiguousarray(np.stack(
        [*(per_partition(np.repeat(v, HEAD)) for v in i["ssd_d"][0]), per_partition(i["ssd_norm_g"][0])], 1))
    d["state_in"] = np.ascontiguousarray(i["state_ssd"][0, 0].transpose(3, 0, 1, 2)).reshape(P, 2, INNER)
    halves = [t for p in range(KD) for t in (p, KD + p)]
    d["conf_in"] = tiles_of(i["conf_w_in"][0])[halves]
    d["conf_out"] = tiles_of(i["conf_w_out"][0])
    d["conf_tab"] = np.concatenate(
        [per_partition(i["conf_dw"][0]).transpose(0, 2, 1).reshape(P, C_BIN), per_partition(i["conf_b_in"][0])[:, halves],
         *(per_partition(i["conf_" + n][0]) for n in ("dw_b", "ln_g", "ln_b", "b_out"))], 1)
    d["qkv"] = tiles_of(i["attn_w_qkv"][0])
    d["attn_out"] = tiles_of(i["attn_w_o"][0])
    n_freq = AD // 4
    inv_freq = np.float32(ROPE_THETA) ** (-np.arange(n_freq, dtype=np.float32) / np.float32(n_freq))
    t = np.arange(LAT)
    place = np.stack([t // GRID_W, t % GRID_W]).astype(np.float32)
    angle = np.broadcast_to((inv_freq[None, :, None] * place[:, None, :])[:, None], (2, 2, n_freq, LAT)).reshape(AD, LAT)
    perm = np.zeros((2, 2, n_freq, 2, 2, n_freq), np.float32)
    for axis in range(2):
        for f in range(n_freq):
            perm[axis, 1, f, axis, 0, f] = -1.0
            perm[axis, 0, f, axis, 1, f] = 1.0
    d["attn_tab"] = np.concatenate(
        [np.cos(angle), np.sin(angle), perm.reshape(AD, AD), i["attn_q_g"].T, i["attn_k_g"].T,
         i["cache_v"][0, 0].reshape(PAST, AKV * AD)], 1)
    d["cache_k"] = np.ascontiguousarray(i["cache_k"][0, 0].transpose(2, 1, 0))
    for l in range(DEPTH):
        d[f"ffn_in{l}"] = tiles_of(i["ffn_w_in"][l])[PAIRED]
        w = tiles_of(i["ffn_w_out"][l]).reshape(KD, P, 2, HALF * P)
        d[f"ffn_out{l}"] = np.ascontiguousarray(w.transpose(0, 2, 1, 3)).reshape(2 * KD, P, HALF * P)
    return d


OUTS = {"y": [P, KD, COLS], "state": [P, 2, INNER], "cache_k": [P, AKV, CTX], "cache_v": [P, AKV, CTX]}


def kernel(**inputs):
    import concourse.bacc as bacc
    from concourse.bass_utils import run_bass_kernel_spmd

    d = lay_out({k: np.asarray(v) for k, v in inputs.items()})
    nc = bacc.Bacc("TRN2", target_bir_lowering=False, num_devices=1)
    a = {k: nc.dram_tensor("in_" + k, list(v.shape), F32, kind="ExternalInput").ap() for k, v in d.items()}
    o = {k: nc.dram_tensor("out_" + k, v, F32, kind="ExternalOutput").ap() for k, v in OUTS.items()}
    build_trunk(nc, a, o)
    r = run_bass_kernel_spmd(nc, [{"in_" + k: v for k, v in d.items()}], core_ids=[0]).results[0]
    y = np.asarray(r["out_y"])
    tokens = [np.ascontiguousarray(y[:, :, c0:c0 + w].transpose(2, 1, 0)).reshape(1, w, D) for c0, w, _ in STREAMS]
    state = np.ascontiguousarray(np.asarray(r["out_state"]).transpose(1, 2, 0)).reshape(1, 1, 2, SSD_HEADS, HEAD, STATE)
    caches = [np.ascontiguousarray(np.asarray(r["out_" + n]).transpose(2, 1, 0)).reshape(1, 1, CTX, AKV, AD)
              for n in ("cache_k", "cache_v")]
    return (*tokens, state, *caches)
```

```python
from contextlib import ExitStack

import numpy as np

import concourse.bass as bass
from concourse import mybir

F32 = mybir.dt.float32
F32R = mybir.dt.float32r
ALU = mybir.AluOpType
ACT = mybir.ActivationFunctionType
AX = mybir.AxisListType

P = 128
D = 1024
KD = D // P
CTX, LAT = 128, 256
LAT0 = CTX + 1
COLS = CTX + 1 + LAT + 1
CHUNKS = [(0, 0), (LAT0, 1), (LAT0 + P, 1)]
STREAMS = [(0, CTX, 0), (LAT0, LAT, 1)]
EPS = 1e-6

DEPTH = 4
FFN = 2816
KF = FFN // P
PAIRS = KF
FFN_TILES = 2 * KF
HALF = KF // 2

WINDOWS = (2, 4, 8, 16)
EDGE = max(WINDOWS) // 2
GAPPED = EDGE + CTX + 2 * EDGE + LAT + EDGE
GAP_AT = [EDGE, EDGE + CTX + 2 * EDGE]

INNER = 2048
SSD_HEADS, HEAD = 32, 64
GROUPS, STATE = 8, 128
HPG = SSD_HEADS // GROUPS
GW = HPG * HEAD
KI = INNER // P
SSD_CONV_TILES = KI + 2 * GROUPS
NDT = 2 * SSD_HEADS

TAPS31 = 31
REACH = TAPS31 // 2
CGAP = REACH + CTX + REACH + 1 + LAT + REACH
CGAP_AT = [REACH, 2 * REACH + 1 + CTX]
CONVOLVED = CGAP - TAPS31 + 1
CONV_PE = 3
CONV_DVE = KD - CONV_PE
CONV_GROUPS = [(0, 1), (2, 3, 4)]
HALF_SLOTS = 4
CONVOLVED_AT = [at - REACH for at in CGAP_AT]
C_BIN = KD * TAPS31
C_DWB, C_LNG, C_LNB, C_BOUT, C_ALL = (C_BIN + k * KD for k in (2, 3, 4, 5, 6))

AH, AKV, AD = 8, 2, 128
REP = AH // AKV
PAST = 128
SCALE = AD ** -0.5
QK = AH + AKV
GRID_W, ROPE_THETA = 64, 10000.0
A_COS, A_SIN, A_PERM, A_G, A_V, A_ALL = 0, LAT, 2 * LAT, 2 * LAT + AD, 2 * LAT + AD + 2, 2 * LAT + AD + 2 + AKV * AD

RAW_SLOTS, SPLIT_SLOTS, BANKS = 4, 2, 4
SCAN_LAG = 2
SCAN_SLOTS = SCAN_LAG + 1
MOD_COLS = 512
MOD_UNITS = 6 * D // MOD_COLS
MOD_PIECES = 2 * MOD_UNITS
HALF_K = KD // 2
MOD_TILES = MOD_COLS // P
MOD_FIRST, MOD_POOL, MOD_GLUE = 2 * D // MOD_COLS, 4 * D // MOD_COLS + 1, 5 * D // MOD_COLS
MOD_DURING = [MOD_GLUE, 2 * MOD_UNITS, 3 * MOD_UNITS]
MOD_BEHIND = [u + FFN_TILES // 4 for u in MOD_DURING]
MAXK = HALF


class Linear:

    def __init__(self, name, chunks, tiles, per, outs, width=P):
        self.name, self.chunks, self.tiles, self.per, self.outs, self.width = name, chunks, tiles, per, outs, width


def plan():
    lins = [Linear("pool", 2, KD, 1, 8)]
    for l in range(DEPTH):
        if l == 1:
            lins += [Linear("ssd_conv", SSD_CONV_TILES, KD, 1, SSD_CONV_TILES),
                     Linear("ssd_z", KI, KD, 1, KI), Linear("ssd_dt", 1, KD, 1, 1, NDT),
                     Linear("ssd_out", 2 * KD, KD, 2, KD)]
        if l == 2:
            lins += [Linear("conf_in", 2 * KD, KD, 1, 2 * KD), Linear("conf_out", KD, KD, 1, KD)]
        if l == 3:
            lins += [Linear("qkv", AH + 2 * AKV, KD, 1, AH + 2 * AKV), Linear("attn_out", KD, KD, 1, KD)]
        lins += [Linear(f"ffn_in{l}", FFN_TILES, KD, 1, FFN_TILES), Linear(f"ffn_out{l}", 2 * KD, HALF, 2, KD)]
    n = t = conv = evac = 0
    for x in lins:
        x.n0, x.t0, x.conv0, x.evac0 = n, t, conv, evac
        n += x.chunks
        t += x.outs
        if x.name.startswith("ffn_in") or x.name == "ssd_conv":
            conv += x.outs
        else:
            evac += x.outs
    return {x.name: x for x in lins}, lins



def norm_plan():
    order = []
    for l in range(DEPTH):
        order += [(f"pre{l}.0", KD)]
        if l == 1:
            order += [("ssd", KI)]
        if l == 2:
            order += [("ln", KD)]
        if l == 3:
            order += [("qk", AH + AKV)]
        order += [(f"post{l}.0", KD), (f"pre{l}.1", KD), (f"post{l}.1", KD)]
    out, base, event = {}, 0, 0
    for name, k in order:
        out[name] = (event, base, k)
        base += k
        event += name != "qk"
    return out


def operand_plan():
    out, base = {}, 0
    for l in range(DEPTH):
        for name, k in [(f"mix{l}", KD), *([("ssd_y", KI)] if l == 1 else []),
                        *([(f"mid{l}", KD)] if l in (2, 3) else []), (f"ffn{l}", KD)]:
            out[name] = base
            base += k
    return out


def sum_plan(norm):
    groups, freed = {}, []
    adds = sums = 0
    for name, (_, _, k) in norm.items():
        if name.startswith("post"):
            sizes = [KD - 1, 1]
        else:
            sizes = {"ssd": [3, 3, 3, 3, 2, 1, 1], "qk": [1] * k}.get(name, [2, 2, 2, 1, 1])
        mine, t = [], 0
        for size in sizes:
            for _ in range(size - 1):
                adds += 1
                freed.append(("added", adds))
            sums += 1
            freed.append(("used", sums))
            t += size
            mine.append((t - 1, size, adds))
        assert t == k
        groups[name] = (mine, sums)
    return groups, freed


def low_plan(opnd):
    shares = {"ssd_y": (KI, lambda k: k % 3 < 2), "mix0": (KD, lambda k: k < 6),
              "mid2": (KD, lambda k: False), "mid3": (KD, lambda k: False)}
    at, count = {}, {True: 0, False: 0}
    for name in opnd:
        k, pool = shares.get(name, (KD, lambda k: k % 4 < 3))
        at[name] = []
        for j in range(k):
            count[pool(j)] += 1
            at[name].append((pool(j), count[pool(j)]))
    return at


def build_trunk(nc, a, out):
    lin, order = plan()
    norm = norm_plan()
    sum_groups, slot_freed = sum_plan(norm)
    opnd = operand_plan()
    low_at = low_plan(opnd)

    with ExitStack() as ctx:
        def sb(name, shape, dt=F32, stack=ctx):
            return stack.enter_context(nc.sbuf_tensor(name, shape, dt))

        def bank(name, shape=(P, 512)):
            return ctx.enter_context(nc.psum_tensor(name, list(shape), F32))

        def sem(name):
            return ctx.enter_context(nc.semaphore(name))

        x = sb("x", [P, KD, COLS])
        work = sb("work", [P, KD, COLS])
        h_hi = sb("h_hi", [P, KD, COLS], F32R)
        h_lo = sb("h_lo", [P, KD, COLS], F32R)
        sq = sb("sq", [P, 4, COLS])
        raw = sb("raw", [P, RAW_SLOTS, MAXK * P])
        w_hi = sb("w_hi", [P, SPLIT_SLOTS, MAXK * P], F32R)
        w_lo = sb("w_lo", [P, SPLIT_SLOTS, MAXK * P], F32R)
        mean_col = sb("mean_col", [P, 3])
        ident = sb("ident", [P, P + 4])
        spare = sb("spare", [P, 8])
        eps_col = sb("eps_col", [P, 1])
        std = sb("std", [P, 3])
        rstd = sb("rstd", [P, 3])
        gated_bias = sb("gated_bias", [P, KD, 2])
        modc = sb("modc", [P, 2, 6 * KD, 2])
        coef = sb("coef", [P, 4, KD, 2])
        gains = sb("gains", [P, DEPTH, 4, KD])
        b_mod = sb("b_mod", [P, DEPTH, 6 * KD])
        cond = sb("cond", [P, KD, 2])
        cond32 = sb("cond32", [P, KD, 32])
        taps = sb("taps", [P, DEPTH, FFN_TILES, 4])
        pool_scale = sb("pool_scale", [P, KD])
        tri = sb("tri", [P, 2, P])
        ones = sb("ones", [P, P])
        ssd_taps = sb("ssd_taps", [P, SSD_CONV_TILES, 4])
        dt_rows = sb("dt_rows", [P, 2, NDT])
        ssd_cols = sb("ssd_cols", [P, 3, KI])

        mod_raw = sb("mod_raw", [P, 2, HALF_K * MOD_COLS])
        mod_turned = sb("mod_turned", [P, MOD_TILES, 32])

        with ExitStack() as part:
            g_hi = sb("g_hi", [P, KF, COLS], F32R, part)
            g_lo = sb("g_lo", [P, KF, COLS], F32R, part)
            acc = sb("acc", [P, 4, COLS], F32, part)
            sil = sb("sil", [P, 2, COLS], F32, part)
            gate = sb("gate", [P, 2, COLS], F32, part)
        with ExitStack() as part:
            gapped = sb("gapped", [P, KD, GAPPED], F32, part)
            sums_a = sb("sums_a", [P, KD, GAPPED], F32, part)
            sums_b = sb("sums_b", [P, KD, GAPPED], F32, part)
            inv_count = sb("inv_count", [P, len(WINDOWS), CTX + LAT], F32, part)

        with ExitStack() as part:
            zt = sb("zt", [P, KI, COLS], F32, part)
            xbc = sb("xbc", [P, SSD_CONV_TILES, COLS], F32, part)
            state0 = sb("state0", [P, 2, 2, GW], F32, part)
            state1 = sb("state1", [P, 2, GW], F32, part)
            cb_mask = sb("cb_mask", [P, 2, P], F32, part)
            dtv = sb("dtv", [P, 3, NDT], F32, part)
            adt = sb("adt", [P, 3, NDT], F32, part)
            neg_cum = sb("neg_cum", [P, 3, NDT], F32, part)
            back_cum = sb("back_cum", [P, 3, SSD_HEADS], F32, part)
        with ExitStack() as part:
            y_hi = sb("y_hi", [P, KI, COLS], F32R, part)
            sb("y_between", [P, KI, COLS], F32, part)
            y_lo = sb("y_lo", [P, KI, COLS], F32R, part)
        with ExitStack() as part:
            conf_tab = sb("conf_tab", [P, C_ALL], F32, part)
            linear_half = sb("linear_half", [P, HALF_SLOTS, COLS], F32, part)
            gate_half = sb("gate_half", [P, HALF_SLOTS, COLS], F32, part)
            glu_hi = sb("glu_hi", [P, CONV_PE, CGAP], F32R, part)
            glu_lo = sb("glu_lo", [P, CONV_PE, CGAP], F32R, part)
            tap_hi = sb("tap_hi", [P, CONV_PE * TAPS31], F32R, part)
            tap_lo = sb("tap_lo", [P, CONV_PE * TAPS31], F32, part)
            diagonal = sb("diagonal", [P, TAPS31, 2, P], F32R, part)
            glu = sb("glu", [P, KD, CGAP], F32, part)
            convolved = sb("convolved", [P, KD, CONVOLVED], F32, part)
            ln_mean = sb("ln_mean", [P, 3], F32, part)
        with ExitStack() as part:
            attn_tab = sb("attn_tab", [P, A_ALL], F32, part)
            qkv = sb("qkv", [P, QK + AKV, COLS], F32, part)
            q_turned = sb("q_turned", [P, AH, LAT], F32, part)
            k_all = sb("k_all", [P, AKV, PAST + LAT], F32, part)
            v_rows = sb("v_rows", [P, AKV, len(CHUNKS) * AD], F32, part)
            rot_sin = sb("rot_sin", [P, 2, LAT], F32, part)
            prob = sb("prob", [P, 2, PAST + LAT], F32, part)
            prob_t = sb("prob_t", [P, 2, PAST + LAT], F32, part)
            qk_std = sb("qk_std", [P, 3 * QK], F32, part)
            qk_rstd = sb("qk_rstd", [P, 3 * QK], F32, part)
            row_max = sb("row_max", [P, 2], F32, part)
            neg_max = sb("neg_max", [P, 2], F32, part)
            row_sum = sb("row_sum", [P, 2], F32, part)
            inv_sum = sb("inv_sum", [P, 2], F32, part)
        flat = work[:, :, :].rearrange("p k n -> p (k n)")
        flat_mod = mod_raw[:, :, :].rearrange("p s n -> p (s n)")
        flat_sq = sq[:, :, :].rearrange("p s n -> p (s n)")

        def by_dir(ap):
            return ap.rearrange("p (d n) -> p d n", d=2)

        decay = [by_dir(flat_mod[:, k * 1024:(k + 1) * 1024]) for k in range(SCAN_SLOTS)]
        c_scaled = [by_dir(flat_mod[:, 3072:4096]), by_dir(flat[:, 1024:2048])]
        turned = flat[:, 0:1024].rearrange("p (u n) -> p u n", u=2)
        x_dt = [by_dir(flat[:, 2048:2560]), by_dir(flat[:, 2560:3072]), by_dir(flat_sq[:, 0:512])]
        state_new = raw[:, 0:2, D:D + GW]
        x_end = raw[:, 2:4, D:D + GW]
        to_end = sq[:, 2, 192:384].rearrange("p (c h) -> p c h", c=3)
        full_decay = sq[:, 3, 0:192].rearrange("p (c h) -> p c h", c=3)

        tile_bank = [bank(f"tile_bank{i}") for i in range(BANKS)]
        mod_bank = bank("mod_bank")
        col_bank = bank("col_bank")
        stat_bank = bank("stat_bank")
        rstd_bank = bank("rstd_bank")

        consts = sem("consts")
        cond_loaded = sem("cond_loaded")
        loaded0 = sem("loaded0")
        vec_init = sem("vec_init")
        w_loaded = [sem(f"w_loaded{i}") for i in range(RAW_SLOTS)]
        w_rounded = sem("w_rounded")
        w_low_pool = sem("w_low_pool")
        w_low_dve = sem("w_low_dve")
        w_used = sem("w_used")
        mod_loaded = [sem(f"mod_loaded{i}") for i in range(2)]
        mod_used = sem("mod_used")
        turned_ready = sem("turned_ready")
        mod_done = sem("mod_done")
        cond_ready = sem("cond_ready")
        acc_ready = sem("acc_ready")
        tap_first = sem("tap_first")
        conv_done = sem("conv_done")
        sil_ready = sem("sil_ready")
        gate_ready = sem("gate_ready")
        g_hi_ready = sem("g_hi_ready")
        g_lo_ready = sem("g_lo_ready")
        evac = sem("evac")
        sq_ready = sem("sq_ready")
        sq_used = sem("sq_used")
        std_ready = sem("std_ready")
        rstd_ready = sem("rstd_ready")
        rstd_spread = sem("rstd_spread")
        x_ready = sem("x_ready")
        opnd_ready = sem("opnd_ready")
        opnd_hi = sem("opnd_hi")
        lo_pool = sem("lo_pool")
        lo_dve = sem("lo_dve")
        sq_added = sem("sq_added")
        coef_ready = sem("coef_ready")
        gate2_ready = sem("gate2_ready")
        mod_scaled = sem("mod_scaled")
        lat_ready = sem("lat_ready")
        dve = sem("dve")
        pe = sem("pe")
        stored = sem("stored")
        z_dt = sem("z_dt")
        dt_pe = sem("dt_pe")
        dt_act = sem("dt_act")
        xbc_ready = sem("xbc_ready")
        s_turned = sem("s_turned")
        s_copied = sem("s_copied")
        s_cum = sem("s_cum")
        s_cexp = sem("s_cexp")
        s_seg = sem("s_seg")
        s_seg_back = sem("s_seg_back")
        s_exp = sem("s_exp")
        s_w = sem("s_w")
        s_xdt = sem("s_xdt")
        s_xend = sem("s_xend")
        s_cs = sem("s_cs")
        s_state = sem("s_state")
        s_taken = sem("s_taken")
        s_y = sem("s_y")
        s_out = sem("s_out")
        state_loaded = [sem(f"state_loaded{i}") for i in range(2)]
        state_stored = sem("state_stored")
        yz_ready = sem("yz_ready")
        late_loaded = sem("late_loaded")
        glu_ready = sem("glu_ready")
        conf_tap = sem("conf_tap")
        tap_hi_ready = sem("tap_hi_ready")
        tap_lo_ready = sem("tap_lo_ready")
        diag_ready = sem("diag_ready")
        pe_tap = sem("pe_tap")
        pe_conv = sem("pe_conv")
        glu_hi_ready = sem("glu_hi_ready")
        glu_lo_ready = sem("glu_lo_ready")
        ln_sums = sem("ln_sums")
        ln_mean_ready = sem("ln_mean_ready")
        ln_spread = sem("ln_spread")
        ln_centred = sem("ln_centred")
        ln_scaled = sem("ln_scaled")
        v_turned = sem("v_turned")
        v_copied = sem("v_copied")
        qk_std_ready = sem("qk_std_ready")
        qk_rstd_ready = sem("qk_rstd_ready")
        qk_spread = sem("qk_spread")
        qk_normed = sem("qk_normed")
        qk_rot = sem("qk_rot")
        qk_cos = sem("qk_cos")
        qk_sin = sem("qk_sin")
        qk_turned = sem("qk_turned")
        cache_stored = sem("cache_stored")
        att_score = sem("att_score")
        att_rowmax = sem("att_rowmax")
        att_max = sem("att_max")
        att_exp = sem("att_exp")
        att_inv = sem("att_inv")
        att_prob = sem("att_prob")
        att_turned = sem("att_turned")
        att_pt = sem("att_pt")
        att_pv = sem("att_pv")
        att_part = sem("att_part")

        block = ctx.enter_context(nc.Block())

        def slot(n):
            return n % RAW_SLOTS

        def fetched(n, i=0, per=0):
            return 16 * (n // RAW_SLOTS + 1) + i * (16 * per // RAW_SLOTS)

        def weights(t, n, tiles):
            return t[:, n % SPLIT_SLOTS, 0:tiles * P]

        def split_at(s):
            return (s.tiles if s.name.startswith("conf") else s.tiles // 2) * s.width

        def low_ready(engine, name, k):
            by_pool, count = low_at[name][k]
            engine.wait_ge(lo_pool if by_pool else lo_dve, count)

        def units():
            for h in range(AH):
                for c in range(3):
                    yield h, c, 3 * h + c

        def copied_out(engine, u):
            h, c = u // 3, u % 3
            if c == 2:
                engine.wait_ge(opnd_ready, opnd["mid3"] + h + 1)
            else:
                engine.wait_ge(att_part, 2 * h + c + 1)

        LOADS0 = 16 * 9
        DT_DVE = 20
        CONSTS = 10

        class Chain:

            def __init__(self, engine, semaphore):
                self.engine, self.sem, self.n = engine, semaphore, 0

            def did(self, ins):
                ins.then_inc(self.sem, 1)
                self.n += 1
                return self.n

            def wait(self, n=None):
                self.engine.wait_ge(self.sem, self.n if n is None else n)

        def steps():
            for g in range(GROUPS):
                for c in range(3):
                    yield g, c, 3 * g + c, 2 * g + c - 1

        ALL_STEPS = list(steps())

        def latent_step(v):
            return 3 * (v // 2) + 1 + v % 2

        def state_dirs(c):
            return [(0, 1), (0,), (1,)][c]

        def linears(l):
            return {0: ["pool"], 1: ["ssd_conv", "ssd_z", "ssd_dt", "ssd_out"], 2: ["conf_in", "conf_out"],
                    3: ["qkv", "attn_out"]}[l]

        def owner(n):
            for s in order:
                if s.n0 <= n < s.n0 + s.chunks:
                    return s
            return None

        @block.sync
        def _(sp):
            def load_mod(g, i=None):
                if i is None:
                    if g >= 2:
                        sp.wait_ge(mod_used, g - 1)
                    src = a["w_mod"][g]
                else:
                    sp.wait_ge(mod_used, i * 2 + (g - 1))
                    src = a["w_mod"][bass.ds(i * 2 + g, 1), :, :].rearrange("a p n -> p (a n)")
                sp.dma_start(mod_raw[:, g % 2, :], src).then_inc(mod_loaded[g % 2], 16)

            sp.dma_start(cond[:, :, :], a["cond"]).then_inc(cond_loaded, 16)
            for j in range(2):
                load_mod(j)
            sp.dma_start(x[:, :, :], a["x"]).then_inc(loaded0, 16)
            sp.dma_start(gains[:, :, :, :], a["gains"]).then_inc(loaded0, 16)
            sp.dma_start(b_mod[:, :, :], a["b_mod"]).then_inc(loaded0, 16)
            sp.dma_start(taps[:, :, :, :], a["taps"]).then_inc(loaded0, 16)
            sp.dma_start(pool_scale[:, :], a["pool_scale"]).then_inc(loaded0, 16)

            sp.dma_start(inv_count[:, :, :], a["inv_count"]).then_inc(loaded0, 16)
            sp.dma_start(ssd_taps[:, :, :], a["ssd_taps"]).then_inc(loaded0, 16)
            sp.dma_start(dt_rows[:, :, :], a["dt_rows"]).then_inc(loaded0, 16)
            sp.dma_start(ssd_cols[:, :, :], a["ssd_cols"]).then_inc(loaded0, 16)

            def load_chunk(s, j, i=None, per=0):
                n = s.n0 + j
                src = a[s.name]
                width = s.tiles * s.width
                if i is None:
                    sp.wait_ge(w_low_pool, n + 1)
                    sp.wait_ge(w_low_dve, n + 1)
                    sp.dma_start(raw[:, slot(n), 0:width], src[j]).then_inc(w_loaded[slot(n)], 16)
                else:
                    sp.wait_ge(w_low_pool, i * per + (n + 1))
                    sp.wait_ge(w_low_dve, i * per + (n + 1))
                    sp.dma_start(raw[:, slot(n), 0:width],
                                 src[bass.ds(i * per + j, 1), :, :].rearrange("a p n -> p (a n)")
                                 ).then_inc(w_loaded[slot(n)], 16)

            with sp.Fori(0, MOD_POOL - 1) as i:
                for j in range(2):
                    load_mod(j + 2, i)

            def scan_traffic():
                for g in range(GROUPS):
                    if g >= 2:
                        sp.wait_ge(s_y, 3 * (g - 2) + 3)
                        sp.wait_ge(s_taken, 3 * (g - 2) + 3)
                    else:
                        low_ready(sp, "mix1", KD - 2)
                        low_ready(sp, "mix1", KD - 1)
                    sp.dma_start(state0[:, g % 2, :, :], a["state_in"][:, :, g * GW:(g + 1) * GW]
                                 ).then_inc(state_loaded[g % 2], 16)
                    if g >= 1:
                        sp.wait_ge(s_taken, 3 * (g - 1) + 1)
                        sp.dma_start(out["state"][:, :, (g - 1) * GW:g * GW], state_new).then_inc(state_stored, 16)
                sp.wait_ge(s_taken, 3 * (GROUPS - 1) + 1)
                sp.dma_start(out["state"][:, :, (GROUPS - 1) * GW:], state_new).then_inc(state_stored, 16)
                sp.wait_ge(state_stored, 16 * GROUPS)

            for s in order:
                if s.name == "ssd_out":
                    for j in range(RAW_SLOTS):
                        load_chunk(s, j)
                    scan_traffic()
                    with sp.Fori(0, s.chunks // 4 - 1) as i:
                        for j in range(4):
                            load_chunk(s, j + RAW_SLOTS, i, 4)
                elif s.name == "attn_out":
                    for j in range(RAW_SLOTS):
                        load_chunk(s, j)
                    sp.wait_ge(qk_normed, QK)
                    sp.dma_start(out["cache_k"], qkv[:, AH:QK, 0:CTX]).then_inc(cache_stored, 16)
                    sp.dma_start(out["cache_v"], qkv[:, QK:, 0:CTX]).then_inc(cache_stored, 16)
                    for j in range(RAW_SLOTS, s.chunks):
                        load_chunk(s, j)
                elif s.name.startswith("ffn_in"):
                    l = int(s.name[-1])
                    more = l + 1 < DEPTH
                    if l == 0:
                        for j in range(2):
                            load_chunk(s, j)
                        for g in range(2 * MOD_POOL, 2 * MOD_GLUE):
                            load_mod(g)
                        with sp.Fori(0, FFN_TILES // 4 - 1) as i:
                            for j in range(4):
                                load_chunk(s, j + 2, i, 4)
                                if j % 2:
                                    load_mod(2 * MOD_GLUE + j // 2, i)
                        for j in range(2):
                            load_chunk(s, FFN_TILES - 2 + j)
                            load_mod(2 * MOD_GLUE + FFN_TILES // 2 - 2 + j)
                        continue
                    with sp.Fori(0, FFN_TILES // 4) as i:
                        for j in range(4):
                            load_chunk(s, j, i, 4)
                            if more and j % 2:
                                load_mod(2 * MOD_DURING[l] + j // 2, i)
                elif s.chunks >= 8:
                    with sp.Fori(0, s.chunks // 4) as i:
                        for j in range(4):
                            load_chunk(s, j, i, 4)
                    for j in range(s.chunks // 4 * 4, s.chunks):
                        load_chunk(s, j)
                else:
                    for j in range(s.chunks):
                        load_chunk(s, j)
                if s.name.startswith("ffn_out") and s is not order[-1]:
                    unit = MOD_BEHIND[int(s.name[-1])]
                elif s.name in ("ssd_conv", "ssd_z"):
                    unit = MOD_BEHIND[0] + (1 if s.name == "ssd_conv" else 2)
                else:
                    continue
                for g in (2 * unit, 2 * unit + 1):
                    load_mod(g)
            for m in range(0, KD, 2):
                sp.wait_ge(x_ready, KD * 2 * DEPTH + m + 2)
                sp.dma_start(out["y"][:, m:m + 2, :], x[:, m:m + 2, :]).then_inc(stored, 16)
            sp.wait_ge(stored, 16 * KD // 2)
            sp.wait_ge(cache_stored, 32)

        @block.gpsimd
        def _(pool):
            pool.memset(spare[:, 6:7], 0.0).then_inc(w_low_pool, RAW_SLOTS)
            pool.memset(ident[:, :], 0.0).then_inc(consts, 1)
            pool.memset(mean_col[:, 0:1], 1.0 / D).then_inc(consts, 1)
            pool.memset(mean_col[:, 1:2], 1.0 / INNER).then_inc(consts, 1)
            pool.memset(mean_col[:, 2:3], 1.0 / AD).then_inc(consts, 1)
            pool.memset(eps_col[:, :], EPS).then_inc(consts, 1)
            pool.wait_ge(consts, 5)
            pool.affine_select(out=ident[:, 0:P], in_=ident[:, 0:P], compare_op=ALU.not_equal, fill=1.0, base=0,
                               pattern=[[-1, P]], channel_multiplier=1).then_inc(consts, 1)
            pool.memset(tri[:, :, :], 1.0).then_inc(consts, 1)
            pool.memset(ones[:, :], 1.0).then_inc(consts, 1)
            pool.wait_ge(consts, CONSTS - 2)
            for d in range(2):
                sign = -1 if d else 1
                pool.affine_select(out=tri[:, d, :], in_=tri[:, d, :], compare_op=ALU.is_ge, fill=0.0, base=0,
                                   pattern=[[sign, P]], channel_multiplier=-sign).then_inc(consts, 1)

            def low_part(s, j, i=None, per=0):
                n = s.n0 + j
                w = split_at(s)
                pool.wait_ge(w_rounded, n + 1 if i is None else i * per + (n + 1))
                pool.tensor_tensor(w_lo[:, n % SPLIT_SLOTS, 0:w], raw[:, slot(n), 0:w],
                                   w_hi[:, n % SPLIT_SLOTS, 0:w].bitcast(F32), ALU.subtract).then_inc(w_low_pool, 1)

            def low_next(n):
                s = owner(n)
                if s is not None:
                    low_part(s, n - s.n0)

            def lows_behind(s):
                if s.chunks >= 8:
                    with pool.Fori(0, s.chunks // 4 - 1) as i:
                        for j in range(4):
                            low_part(s, j + 1, i, 4)
                for j in range(max(0, s.chunks - 4), s.chunks):
                    low_next(s.n0 + j + 1)

            def add_squares(name, m):
                _, base, _ = norm[name]
                kind, n = slot_freed[base + m - 1] if m else ("used", 0)
                if kind == "added":
                    pool.wait_ge(sq_ready, base + m + 1)
                    if n > 1:
                        pool.wait_ge(sq_added, n - 1)
                    to = sq[:, (base + m) % 4, :]
                    pool.tensor_tensor(to, to, sq[:, (base + m - 1) % 4, :], ALU.add).then_inc(sq_added, 1)

            def add_all(name):
                for m in range(norm[name][2]):
                    add_squares(name, m)

            def operand_lows(name, src=work, hi=h_hi, lo=h_lo):
                for k, (by_pool, _) in enumerate(low_at[name]):
                    if by_pool:
                        pool.wait_ge(opnd_hi, opnd[name] + k + 1)
                        pool.tensor_tensor(lo[:, k, :], src[:, k, :], hi[:, k, :].bitcast(F32),
                                           ALU.subtract).then_inc(lo_pool, 1)

            def out_lows(s, name):
                for m in range(KD):
                    for j in range(s.per):
                        low_next(s.n0 + s.per * m + j + 1)
                    add_squares(name, m)

            def scan_pool():
                for g, c, u, v in steps():
                    pool.wait_ge(s_copied, u + 1)
                    xt = turned[:, u % 2, P:P + GW].rearrange("p (h q) -> p h q", h=HPG)
                    if u:
                        pool.wait_ge(s_state, u)
                    for d in state_dirs(c):
                        h0 = d * SSD_HEADS + g * HPG
                        ins = pool.tensor_tensor(x_end[:, d, :].rearrange("p (h q) -> p h q", h=HPG), xt,
                                                 to_end[:, c, h0:h0 + HPG].unsqueeze(2).broadcast_to([P, HPG, HEAD]),
                                                 ALU.mult)
                    ins.then_inc(s_xend, 1)
                    if u >= SCAN_SLOTS:
                        pool.wait_ge(s_y, u - SCAN_SLOTS + 1)
                    for d in range(2):
                        h0 = d * SSD_HEADS + g * HPG
                        pool.tensor_tensor(x_dt[u % SCAN_SLOTS][:, d, :].rearrange("p (h q) -> p h q", h=HPG), xt,
                                           dtv[:, c, h0:h0 + HPG].unsqueeze(2).broadcast_to([P, HPG, HEAD]),
                                           ALU.mult).then_inc(s_xdt, 1)
                    if c:
                        for d in range(2):
                            pool.wait_ge(s_cexp, 2 * v + d + 1)
                            cs = c_scaled[v % 2][:, d, :].rearrange("p (h i) -> p h i", h=HPG)
                            c0 = CHUNKS[c][0]
                            pool.tensor_tensor(cs, cs, xbc[:, KI + GROUPS + g, c0:c0 + P].unsqueeze(1).broadcast_to(
                                [P, HPG, P]), ALU.mult).then_inc(s_cs, 1)

            def conf_pool():
                s = lin["conf_in"]
                pool.wait_ge(w_used, s.n0)
                end = 0
                for k, (_, w, _) in enumerate(STREAMS):
                    pool.memset(glu[:, :, end:CGAP_AT[k]], 0.0)
                    end = CGAP_AT[k] + w
                pool.memset(glu[:, :, end:], 0.0).then_inc(glu_ready, 1)
                low_part(s, 1)
                for m in range(KD):
                    low_next(s.n0 + 2 * m + 2)
                    if m > CONV_DVE:
                        glu_low(m - CONV_DVE - 1)
                    pool.wait_ge(evac, 4 + s.evac0 + 2 * m + 2)
                    for c0, w, k in STREAMS:
                        pool.tensor_tensor(glu[:, m, CGAP_AT[k]:CGAP_AT[k] + w], linear_half[:, m % HALF_SLOTS, c0:c0 + w],
                                           gate_half[:, m % HALF_SLOTS, c0:c0 + w], ALU.mult).then_inc(glu_ready, 1)
                    if m + 1 < KD:
                        low_part(s, 2 * m + 3)
                    if m == 0:
                        pool.wait_ge(tap_hi_ready, 1)
                        pool.tensor_tensor(tap_lo[:, :], conf_tab[:, CONV_DVE * TAPS31:KD * TAPS31],
                                           tap_hi[:, :].bitcast(F32), ALU.subtract).then_inc(tap_lo_ready, 1)
                glu_low(CONV_PE - 1)

            def glu_low(k):
                pool.wait_ge(glu_hi_ready, k + 1)
                pool.tensor_tensor(glu_lo[:, k, :], glu[:, CONV_DVE + k, :], glu_hi[:, k, :].bitcast(F32),
                                   ALU.subtract).then_inc(glu_lo_ready, 1)

            def rope_pool():
                pool.wait_ge(late_loaded, 48)
                for t in range(QK):
                    pool.wait_ge(qk_normed, t + 1)
                    to = q_turned[:, t, :] if t < AH else k_all[:, t - AH, PAST:]
                    pool.tensor_tensor(to, qkv[:, t, LAT0:LAT0 + LAT], attn_tab[:, A_COS:A_COS + LAT],
                                       ALU.mult).then_inc(qk_cos, 1)

            add_all("pre0.0")
            low_next(0)
            for l in range(DEPTH):
                if l:
                    add_all(f"pre{l}.0")
                operand_lows(f"mix{l}")
                if l == 0:
                    low_next(1)
                    for m in range(KD):
                        add_squares("post0.0", m)
                    low_next(2)
                if l == 1:
                    for name in ("ssd_conv", "ssd_z", "ssd_dt"):
                        lows_behind(lin[name])
                    pool.wait_ge(z_dt, DT_DVE)
                    scan_pool()
                    add_all("ssd")
                    operand_lows("ssd_y", xbc, y_hi, y_lo)
                    out_lows(lin["ssd_out"], "post1.0")
                if l == 2:
                    conf_pool()
                    add_all("ln")
                    out_lows(lin["conf_out"], "post2.0")
                if l == 3:
                    lows_behind(lin["qkv"])
                    rope_pool()
                    out_lows(lin["attn_out"], "post3.0")
                add_all(f"pre{l}.1")
                operand_lows(f"ffn{l}")
                lows_behind(lin[f"ffn_in{l}"])
                out_lows(lin[f"ffn_out{l}"], f"post{l}.1")

        @block.scalar
        def _(act):
            def apart():
                act.wait_ge(consts, CONSTS)

            def round_chunk(s, j, i=None, per=0):
                n = s.n0 + j
                w = s.tiles * s.width
                act.wait_ge(w_loaded[slot(n)], fetched(n) if i is None else fetched(n, i, per))
                if i is not None:
                    act.wait_ge(w_used, i * per + (n - SPLIT_SLOTS + 1))
                elif n >= SPLIT_SLOTS:
                    act.wait_ge(w_used, n - SPLIT_SLOTS + 1)
                act.activation(w_hi[:, n % SPLIT_SLOTS, 0:w], raw[:, slot(n), 0:w], ACT.Copy).then_inc(w_rounded, 1)

            def round_next(n):
                s = owner(n)
                if s is not None:
                    round_chunk(s, n - s.n0)

            def free_slot(count):
                if count >= 4:
                    kind, n = slot_freed[count - 4]
                    act.wait_ge(sq_added if kind == "added" else sq_used, n)

            def square(src, count):
                free_slot(count)
                act.activation(sq[:, count % 4, :], src, ACT.Square).then_inc(sq_ready, 1)

            def take_std(name):
                act.wait_ge(sq_used, sum_groups[name][1])
                act.activation(std[:, :], stat_bank[:, 0:3], ACT.Sqrt, bias=eps_col[:, 0:1]).then_inc(std_ready, 1)

            def tile_out(s, name, m, gates, scale=None, bias=None):
                _, base, _ = norm[name]
                b = tile_bank[(s.t0 + m) % BANKS]
                kw = {"scale": scale[:, m:m + 1]} if scale is not None else {}
                if bias is not None:
                    kw["bias"] = bias[:, m:m + 1]
                free_slot(base + m)
                act.activation(sq[:, (base + m) % 4, :], b[:, 0:COLS], ACT.Square, **kw).then_inc(sq_ready, 1)
                for c0, w, st in ((0, LAT0, 0), (LAT0, COLS - LAT0, 1)):
                    kw = {} if bias is None else {"bias": gated_bias[:, m, st:st + 1]}
                    ins = act.activation(work[:, m, c0:c0 + w], b[:, c0:c0 + w], ACT.Identity,
                                         scale=coef[:, gates, m, st:st + 1], **kw)
                ins.then_inc(evac, 1)

            def tiles_out(s, name, gates, bias=None):
                for m in range(KD):
                    for j in range(s.per):
                        round_next(s.n0 + s.per * m + j + 1)
                    act.wait_ge(w_used, s.n0 + s.per * (m + 1))
                    tile_out(s, name, m, gates, bias=bias)

            def squares_of_x(name, xbase):
                e, base, k = norm[name]
                for m in range(KD):
                    act.wait_ge(x_ready, xbase + m + 1)
                    square(x[:, m, :], base + m)

            def split_high(name):
                base = opnd[name]
                for m in range(KD):
                    act.wait_ge(opnd_ready, base + m + 1)
                    act.activation(h_hi[:, m, :], work[:, m, :], ACT.Copy).then_inc(opnd_hi, 1)

            def modulate_high(l, name, k):
                base, at = opnd[name], KD * (2 * l + k - 1)
                lat = slice(LAT0, LAT0 + LAT)
                for m in range(KD + 1):
                    if m < KD:
                        act.wait_ge(mod_scaled, at + m + 1)
                        act.activation(work[:, m, lat], work[:, m, lat], ACT.Identity, scale=coef[:, 2 * k, m, 1:2],
                                       bias=modc[:, l % 2, 3 * k * KD + m, 1:2]).then_inc(lat_ready, 1)
                    if m:
                        act.wait_ge(lat_ready, at + m)
                        act.wait_ge(opnd_ready, base + m)
                        act.activation(h_hi[:, m - 1, :], work[:, m - 1, :], ACT.Copy).then_inc(opnd_hi, 1)

            def ffn_in(l):
                s = lin[f"ffn_in{l}"]
                more = l + 1 < DEPTH
                p0 = l * PAIRS

                def at(v, i):
                    return v if i is None else i * 4 + v

                def group(i, first=False, base=0):
                    for j in range(4):
                        c = s.conv0 + base + j
                        pair = p0 + (base + j) // 2
                        half = (lambda v: v) if i is None else (lambda v: i * 2 + v)
                        if i is not None or base + j + 1 < FFN_TILES:
                            round_chunk(s, base + j + 1, i, 4)
                        else:
                            round_next(s.n0 + base + j + 1)
                        if j % 2 == 0 and not (first and j == 0):
                            act.wait_ge(gate_ready, half(pair))
                            apart()
                            act.activation(g_hi[:, bass.ds(half(pair - p0 - 1), 1), :].rearrange("p a n -> p (a n)"),
                                           gate[:, (pair - 1) % 2, :], ACT.Copy).then_inc(g_hi_ready, 1)
                        act.wait_ge(w_used, at(s.n0 + base + j + 1, i))
                        apart()
                        k = bass.ds(at(base + j, i), 1)
                        act.activation(acc[:, c % 4, :], tile_bank[(s.t0 + base + j) % BANKS][:, 0:COLS], ACT.Identity,
                                       scale=taps[:, l, k, 1:2].rearrange("p a b -> p (a b)"),
                                       bias=taps[:, l, k, 3:4].rearrange("p a b -> p (a b)")).then_inc(acc_ready, 1)
                        if j % 2:
                            act.wait_ge(conv_done, at(4 + c, i))
                            act.activation(sil[:, pair % 2, :], acc[:, (c - 1) % 4, :], ACT.Silu).then_inc(sil_ready, 1)

                group(None, first=True)
                with act.Fori(0, FFN_TILES // 4 - 2) as i:
                    group(i, base=4)
                group(None, base=FFN_TILES - 4)
                act.wait_ge(gate_ready, p0 + PAIRS)
                act.activation(g_hi[:, PAIRS - 1, :], gate[:, (p0 + PAIRS - 1) % 2, :], ACT.Copy).then_inc(g_hi_ready, 1)
            def ssd_conv():
                s = lin["ssd_conv"]

                def tile(base, j, i, first=False):
                    at = (lambda v: v) if i is None else (lambda v: i * 4 + v)
                    t, c = base + j, s.conv0 + base + j
                    if i is not None or t + 1 < s.chunks:
                        round_chunk(s, t + 1, i, 4)
                    else:
                        round_next(s.n0 + t + 1)
                    if not first:
                        act.wait_ge(conv_done, at(4 + c))
                    act.wait_ge(w_used, at(s.n0 + t + 1))
                    apart()
                    k = bass.ds(at(t), 1)
                    act.activation(xbc[:, k, :].rearrange("p a n -> p (a n)"), tile_bank[(s.t0 + t) % BANKS][:, 0:COLS],
                                   ACT.Identity, scale=ssd_taps[:, k, 1:2].rearrange("p a b -> p (a b)"),
                                   bias=ssd_taps[:, k, 3:4].rearrange("p a b -> p (a b)")).then_inc(acc_ready, 1)
                    if not first:
                        silu(bass.ds(at(t - 1), 1))

                def silu(k):
                    b = xbc[:, k, :].rearrange("p a n -> p (a n)")
                    act.activation(b, b, ACT.Silu).then_inc(xbc_ready, 1)

                for j in range(4):
                    tile(0, j, None, first=j == 0)
                with act.Fori(0, s.chunks // 4 - 2) as i:
                    for j in range(4):
                        tile(4, j, i)
                for j in range(4):
                    tile(s.chunks - 4, j, None)
                act.wait_ge(conv_done, 4 + s.conv0 + s.chunks)
                silu(bass.ds(s.chunks - 1, 1))

            def ssd_z_dt():
                s = lin["ssd_z"]
                for m in range(s.chunks):
                    round_next(s.n0 + m + 1)
                    act.wait_ge(w_used, s.n0 + m + 1)
                    act.activation(zt[:, m, :], tile_bank[(s.t0 + m) % BANKS][:, 0:COLS], ACT.Silu).then_inc(evac, 1)
                s = lin["ssd_dt"]
                round_next(s.n0 + 1)
                act.wait_ge(w_used, s.n0 + 1)
                act.activation(sq[0:NDT, 0, :], tile_bank[s.t0 % BANKS][0:NDT, 0:COLS], ACT.Copy).then_inc(evac, 1)

            def dt_prepare():
                act.activation(sq[:, 3, 192:256], dt_rows[:, 1, :], ACT.Exp).then_inc(dt_act, 1)
                act.wait_ge(z_dt, 3)
                act.activation(sq[:, 3, 0:192], sq[:, 2, 0:192], ACT.Exp, scale=-1.0).then_inc(dt_act, 1)
                act.wait_ge(z_dt, DT_DVE - 1)
                t = to_end[:, :, :]
                act.activation(t, t, ACT.Exp).then_inc(dt_act, 1)
                act.activation(full_decay[:, :, :], full_decay[:, :, :], ACT.Exp).then_inc(dt_act, 1)

            def scan_act():
                for g, c, u, v in steps():
                    act.wait_ge(s_turned, u + 1)
                    if u >= 2:
                        act.wait_ge(s_state, u - 1)
                        act.wait_ge(s_xdt, 2 * (u - 1))
                        act.wait_ge(s_w, 2 * (u - 2) + 2)
                    act.activation(turned[:, u % 2, :], tile_bank[u % 2][:, :], ACT.Copy).then_inc(s_copied, 1)
                    if c:
                        if v >= 2:
                            act.wait_ge(s_y, latent_step(v - 2) + 1)
                        for d in range(2):
                            act.wait_ge(s_cum, 2 * u + d + 1)
                            act.activation(c_scaled[v % 2][:, d, :], tile_bank[2 + d][:, :], ACT.Exp).then_inc(s_cexp, 1)
                    if u >= SCAN_SLOTS:
                        act.wait_ge(s_y, u - SCAN_SLOTS + 1)
                    act.wait_ge(s_cum, 2 * u + 2)
                    for h in range(HPG):
                        hs = slice(h * P, (h + 1) * P)
                        ins = act.activation(decay[u % SCAN_SLOTS][:, 1, hs], tile_bank[3][:, hs], ACT.Relu, scale=-1.0,
                                             bias=back_cum[:, c, g * HPG + h:g * HPG + h + 1])
                    ins.then_inc(s_seg_back, 1)
                    for d in range(2):
                        if d:
                            act.wait_ge(s_seg_back, u + 1)
                        else:
                            act.wait_ge(s_seg, u + 1)
                        w = decay[u % SCAN_SLOTS][:, d, :]
                        act.activation(w, w, ACT.Exp, scale=-1.0 if d else 1.0).then_inc(s_exp, 1)

            def ssd_norm():
                e, base, k = norm["ssd"]
                for m in range(k):
                    act.wait_ge(yz_ready, m + 1)
                    square(xbc[:, m, :], base + m)
                take_std("ssd")
                for m in range(k):
                    act.wait_ge(opnd_ready, opnd["ssd_y"] + m + 1)
                    act.activation(y_hi[:, m, :], xbc[:, m, :], ACT.Copy).then_inc(opnd_hi, 1)

            def conf_mix():
                s = lin["conf_in"]
                act.wait_ge(late_loaded, 16)
                act.activation(tap_hi[:, :], conf_tab[:, CONV_DVE * TAPS31:KD * TAPS31], ACT.Copy).then_inc(tap_hi_ready, 1)

                def diagonals(tile, k):
                    if tile:
                        act.wait_ge(pe_tap, (tile - 1) * TAPS31 + k + 1)
                    at = tile * TAPS31 + k
                    act.activation(diagonal[:, k, 0, :], ident[:, 0:P], ACT.Identity, scale=tap_hi[:, at:at + 1].bitcast(F32))
                    act.activation(diagonal[:, k, 1, :], ident[:, 0:P], ACT.Identity, scale=tap_lo[:, at:at + 1]
                                   ).then_inc(diag_ready, 1)

                def glu_high(k):
                    act.wait_ge(glu_ready, 1 + 2 * (CONV_DVE + k) + 2)
                    act.activation(glu_hi[:, k, :], glu[:, CONV_DVE + k, :], ACT.Copy).then_inc(glu_hi_ready, 1)

                first = iter(range(TAPS31))
                for m in range(s.chunks):
                    round_next(s.n0 + m + 1)
                    if m >= 4:
                        act.wait_ge(tap_lo_ready, 1)
                        for _ in range(3):
                            k = next(first, None)
                            if k is not None:
                                diagonals(0, k)
                    act.wait_ge(w_used, s.n0 + m + 1)
                    gated, tile = m % 2, m // 2
                    if tile >= HALF_SLOTS:
                        act.wait_ge(glu_ready, 1 + 2 * (tile - HALF_SLOTS) + 2)
                    act.activation((linear_half, gate_half)[gated][:, tile % HALF_SLOTS, :],
                                   tile_bank[(s.t0 + m) % BANKS][:, 0:COLS],
                                   ACT.Sigmoid if gated else ACT.Identity, bias=conf_tab[:, C_BIN + m:C_BIN + m + 1]
                                   ).then_inc(evac, 1)
                    if m >= 2 * CONV_DVE + 2 and m % 2 == 0:
                        glu_high(tile - CONV_DVE - 1)
                glu_high(CONV_PE - 1)
                for tile in range(1, CONV_PE + 1):
                    if tile < CONV_PE:
                        for k in range(TAPS31):
                            diagonals(tile, k)
                    m = CONV_DVE + tile - 1
                    act.wait_ge(pe_tap, tile * TAPS31)
                    act.activation(convolved[:, m, :], (mod_bank, col_bank)[(tile - 1) % 2][:, 0:CONVOLVED], ACT.Identity,
                                   bias=conf_tab[:, C_DWB + m:C_DWB + m + 1]).then_inc(pe_conv, 1)
                e, base, _ = norm["ln"]
                for m in range(KD):
                    act.wait_ge(ln_centred, m + 1)
                    square(work[:, m, :], base + m)
                take_std("ln")
                o = opnd["mid2"]
                for m in range(KD + 1):
                    if m < KD:
                        act.wait_ge(ln_scaled, m + 1)
                        act.activation(work[:, m, :], work[:, m, :], ACT.Silu, scale=conf_tab[:, C_LNG + m:C_LNG + m + 1],
                                       bias=conf_tab[:, C_LNB + m:C_LNB + m + 1]).then_inc(opnd_ready, 1)
                    if m:
                        act.wait_ge(opnd_ready, o + m)
                        act.activation(h_hi[:, m - 1, :], work[:, m - 1, :], ACT.Copy).then_inc(opnd_hi, 1)

            def attn_mix():
                s = lin["qkv"]
                for m in range(s.chunks):
                    round_next(s.n0 + m + 1)
                    act.wait_ge(w_used, s.n0 + m + 1)
                    act.activation(qkv[:, m, :], tile_bank[(s.t0 + m) % BANKS][:, 0:COLS], ACT.Copy).then_inc(evac, 1)
                e, base, _ = norm["qk"]
                act.wait_ge(evac, 4 + s.evac0 + s.chunks)
                for m in range(QK):
                    square(qkv[:, m, :], base + m)
                for kv in range(AKV):
                    act.wait_ge(v_turned, kv + 1)
                    act.activation(v_rows[:, kv, :], tile_bank[2 + kv][:, 0:3 * AD], ACT.Copy).then_inc(v_copied, 1)
                act.wait_ge(sq_used, sum_groups["qk"][1])
                act.activation(qk_std[:, :], stat_bank[:, 0:3 * QK], ACT.Sqrt, bias=eps_col[:, 0:1]).then_inc(qk_std_ready, 1)
                o = opnd["mid3"]
                for u in range(3 * AH + 3):
                    if u < 3 * AH:
                        w = P if u % 3 == 0 else PAST + LAT
                        act.wait_ge(att_max, u + 1)
                        if u >= 2:
                            act.wait_ge(att_turned, u - 1)
                            act.wait_ge(att_inv, u - 1)
                        act.activation(prob[:, u % 2, 0:w], tile_bank[u % 2][:, 0:w], ACT.Exp, scale=SCALE,
                                       bias=neg_max[:, u % 2:u % 2 + 1], accum_out=row_sum[:, u % 2:u % 2 + 1]
                                       ).then_inc(att_exp, 1)
                    if 2 <= u < 3 * AH + 2:
                        b = u - 2
                        w = P if b % 3 == 0 else PAST + LAT
                        act.wait_ge(att_turned, b + 1)
                        if b >= 2:
                            act.wait_ge(att_pv, b - 1)
                        act.activation(prob_t[:, b % 2, 0:w], tile_bank[2 + b % 2][:, 0:w], ACT.Copy).then_inc(att_pt, 1)
                    if u >= 3:
                        b = u - 3
                        h, c = b // 3, b % 3
                        act.wait_ge(att_pv, b + 1)
                        act.activation(work[:, h, CHUNKS[c][0]:CHUNKS[c][0] + P], (mod_bank, col_bank)[b % 2][:, 0:P],
                                       ACT.Copy).then_inc(opnd_ready if c == 2 else att_part, 1)
                        if c == 0 and h:
                            high_head(o, h - 1)
                high_head(o, AH - 1)

            def high_head(o, h):
                act.wait_ge(att_part, 2 * h + 2)
                act.wait_ge(opnd_ready, o + h + 1)
                act.activation(h_hi[:, h, :], work[:, h, :], ACT.Copy).then_inc(opnd_hi, 1)

            act.wait_ge(cond_loaded, 16)
            act.wait_ge(vec_init, 1)
            act.activation(cond32[:, :, 0:2], cond[:, :, :], ACT.Silu).then_inc(cond_ready, 1)
            act.wait_ge(consts, CONSTS)
            act.activation(spare[:, 5:6], eps_col[:, :], ACT.Copy).then_inc(evac, 4)
            squares_of_x("pre0.0", 0)
            take_std("pre0.0")
            round_next(0)
            for l in range(DEPTH):
                if l == 0:
                    split_high("mix0")
                    s = lin["pool"]
                    round_next(1)
                    act.wait_ge(coef_ready, 1)
                    for m in range(KD):
                        if m == 4:
                            round_next(2)
                        if m % 4 == 3:
                            act.wait_ge(w_used, m // 4 + 1)
                        else:
                            act.wait_ge(pe, m + 1 - m // 4)
                        tile_out(s, "post0.0", m, 1, scale=pool_scale)
                if l == 1:
                    modulate_high(1, "mix1", 0)
                    act.wait_ge(coef_ready, 2)
                    ssd_conv()
                    ssd_z_dt()
                    dt_prepare()
                    scan_act()
                    ssd_norm()
                    tiles_out(lin["ssd_out"], "post1.0", 1)
                if l == 2:
                    modulate_high(2, "mix2", 0)
                    act.wait_ge(coef_ready, 3)
                    conf_mix()
                    tiles_out(lin["conf_out"], "post2.0", 1, conf_tab[:, C_BOUT:C_BOUT + KD])
                if l == 3:
                    modulate_high(3, "mix3", 0)
                    act.wait_ge(coef_ready, 4)
                    attn_mix()
                    tiles_out(lin["attn_out"], "post3.0", 1)
                take_std(f"post{l}.0")
                squares_of_x(f"pre{l}.1", KD * (2 * l + 1))
                take_std(f"pre{l}.1")
                modulate_high(l, f"ffn{l}", 1)
                if l == 3:
                    act.wait_ge(cache_stored, 32)
                ffn_in(l)
                if l == 0:
                    act.wait_ge(gate2_ready, 1)
                tiles_out(lin[f"ffn_out{l}"], f"post{l}.1", 3)
                if l == 1:
                    act.dma_start(conf_tab[:, :], a["conf_tab"]).then_inc(late_loaded, 16)
                if l == 2:
                    act.dma_start(attn_tab[:, :], a["attn_tab"]).then_inc(late_loaded, 16)
                    act.dma_start(k_all[:, :, 0:PAST], a["cache_k"]).then_inc(late_loaded, 16)
                take_std(f"post{l}.1")
                if l + 1 < DEPTH:
                    squares_of_x(f"pre{l + 1}.0", KD * (2 * l + 2))
                    take_std(f"pre{l + 1}.0")

        @block.vector
        def _(vec):
            ch = Chain(vec, dve)

            def low_part(s, j, i=None, per=0):
                n = s.n0 + j
                w0, w1 = split_at(s), s.tiles * s.width
                vec.wait_ge(w_rounded, n + 1 if i is None else i * per + (n + 1))
                vec.tensor_tensor(w_lo[:, n % SPLIT_SLOTS, w0:w1], raw[:, slot(n), w0:w1],
                                  w_hi[:, n % SPLIT_SLOTS, w0:w1].bitcast(F32), ALU.subtract).then_inc(w_low_dve, 1)

            def low_next(n):
                s = owner(n)
                if s is not None and split_at(s) < s.tiles * s.width:
                    low_part(s, n - s.n0)

            def mod_column(g, i=None):
                at = (lambda v, per=1: v) if i is None else (lambda v, per=1: i * per + v)
                vec.wait_ge(mod_used, at(2 * g + 2, 2))
                vec.wait_ge(mod_done, at(g + 1))
                vec.transpose(mod_turned[:, :, :].rearrange("p t r -> p (t r)"), mod_bank[:, 0:MOD_TILES * 32]
                              ).then_inc(turned_ready, 1)
                vec.wait_ge(turned_ready, at(g + 1))
                to = bass.ds(at(g * MOD_TILES % (2 * 6 * KD), MOD_TILES), MOD_TILES)
                bias = b_mod[:, :, :].rearrange("p l t -> p (l t)")[:, bass.ds(at(g * MOD_TILES, MOD_TILES), MOD_TILES)]
                vec.tensor_tensor(modc[:, :, :, :].rearrange("p l t s -> p (l t) s")[:, to, :], mod_turned[:, :, 0:2],
                                  bias.unsqueeze(2).broadcast_to([P, MOD_TILES, 2]), ALU.add).then_inc(mod_done, 1)

            def take_rstd(name):
                e, base, k = norm[name]
                vec.wait_ge(std_ready, e + 1)
                vec.reciprocal(rstd[:, :], std[:, :]).then_inc(rstd_ready, 1)

            def coefficients(l, parts=(0, 1, 2, 3)):
                for part in parts:
                    k = part // 2
                    gain = gains[:, l, part, :].unsqueeze(2).broadcast_to([P, KD, 2])
                    if part % 2 == 0:
                        ch.did(vec.scalar_tensor_tensor(
                            out=coef[:, part, :, :], in0=modc[:, l % 2, (3 * k + 1) * KD:(3 * k + 2) * KD, :],
                            scalar=1.0, in1=gain, op0=ALU.add, op1=ALU.mult))
                    else:
                        ch.did(vec.tensor_tensor(coef[:, part, :, :], modc[:, l % 2, (3 * k + 2) * KD:(3 * k + 3) * KD, :],
                                                 gain, ALU.mult))
                ch.wait()
                if 1 in parts:
                    gate = coef[:, 1, :, :]
                    if l == 2:
                        vec.wait_ge(late_loaded, 16)
                        vec.tensor_tensor(gated_bias[:, :, :], gate, conf_tab[:, C_BOUT:C_BOUT + KD].unsqueeze(2)
                                          .broadcast_to([P, KD, 2]), ALU.mult).then_inc(coef_ready, 1)
                    elif l == 0:
                        vec.tensor_tensor(gate, gate, pool_scale[:, :].unsqueeze(2).broadcast_to([P, KD, 2]),
                                          ALU.mult).then_inc(coef_ready, 1)
                    else:
                        vec.memset(spare[:, 0:1], 0.0).then_inc(coef_ready, 1)

            def residual(name, evac_count, between=lambda m: None):
                e, _, _ = norm[name]
                vec.wait_ge(evac, evac_count)
                vec.wait_ge(rstd_spread, e + 1)
                scaled = [0] * KD
                for m in range(KD + 1):
                    if m < KD:
                        scaled[m] = ch.did(vec.tensor_tensor(work[:, m, :], work[:, m, :], rstd_bank[:, 0:COLS], ALU.mult))
                    if m:
                        ch.wait(scaled[m - 1])
                        vec.tensor_tensor(x[:, m - 1, :], x[:, m - 1, :], work[:, m - 1, :], ALU.add).then_inc(x_ready, 1)
                        between(m)

            def modulate_gapped():
                vec.wait_ge(rstd_spread, norm["pre0.0"][0] + 1)
                scaled = [0] * KD
                for m in range(KD + 1):
                    if m < KD:
                        scaled[m] = ch.did(vec.tensor_tensor(work[:, m, :], x[:, m, :], rstd_bank[:, 0:COLS], ALU.mult))
                    if m:
                        t = m - 1
                        ch.wait(scaled[t])
                        for c0, w, s in STREAMS:
                            ch.did(vec.tensor_scalar(gapped[:, t, GAP_AT[s]:GAP_AT[s] + w], work[:, t, c0:c0 + w],
                                                     coef[:, 0, t, s:s + 1], modc[:, 0, t, s:s + 1], ALU.mult, ALU.add))

            def modulate(l, name, k, xbase, opname):
                e, _, _ = norm[name]
                o, at = opnd[opname], KD * (2 * l + k - 1)
                vec.wait_ge(rstd_spread, e + 1)
                vec.wait_ge(x_ready, xbase + KD)
                for m in range(KD + 2):
                    if m < KD:
                        vec.tensor_tensor(work[:, m, :], x[:, m, :], rstd_bank[:, 0:COLS], ALU.mult).then_inc(mod_scaled, 1)
                    if 1 <= m <= KD:
                        t = m - 1
                        vec.wait_ge(mod_scaled, at + t + 1)
                        vec.tensor_scalar(work[:, t, 0:CTX], work[:, t, 0:CTX], coef[:, 2 * k, t, 0:1],
                                          modc[:, l % 2, 3 * k * KD + t, 0:1], ALU.mult, ALU.add).then_inc(opnd_ready, 1)
                    if m >= 2 and not low_at[opname][m - 2][0]:
                        low_operand(o, m - 2)

            def low_operand(o, t):
                vec.wait_ge(opnd_hi, o + t + 1)
                vec.tensor_tensor(h_lo[:, t, :], work[:, t, :], h_hi[:, t, :].bitcast(F32),
                                  ALU.subtract).then_inc(lo_dve, 1)

            def pool_mix():
                rest = iter(range(MOD_FIRST, MOD_POOL))

                def next_unit():
                    unit = next(rest, None)
                    if unit is not None:
                        mod_column(unit)

                ch.wait()
                n = GAPPED
                kg = KD // len(WINDOWS)
                ch.did(vec.tensor_tensor(sums_a[:, :, 1:n], gapped[:, :, 0:n - 1], gapped[:, :, 1:n], ALU.add))
                next_unit()
                ch.wait()
                src, dst, lo, hi, step = sums_a, sums_b, 1, n, 1
                for g in range(len(WINDOWS)):
                    k0, k1 = g * kg, (g + 1) * kg
                    if g:
                        ch.did(vec.tensor_tensor(dst[:, k0:, lo + step:hi - step], src[:, k0:, lo:hi - 2 * step],
                                                 src[:, k0:, lo + 2 * step:hi], ALU.add))
                        next_unit()
                        ch.wait()
                        src, dst, lo, hi, step = dst, src, lo + step, hi - step, 2 * step
                    for c0, w, s in STREAMS:
                        j0 = s * CTX
                        ga = slice(GAP_AT[s], GAP_AT[s] + w)
                        ch.did(vec.tensor_tensor(work[:, k0:k1, c0:c0 + w], src[:, k0:k1, ga],
                                                 inv_count[:, g, j0:j0 + w].unsqueeze(1).broadcast_to([P, kg, w]),
                                                 ALU.mult))
                    next_unit()
                    ch.wait()
                    for c0, w, s in STREAMS:
                        ga = slice(GAP_AT[s], GAP_AT[s] + w)
                        ins = vec.tensor_tensor(work[:, k0:k1, c0:c0 + w], work[:, k0:k1, c0:c0 + w],
                                                gapped[:, k0:k1, ga], ALU.subtract)
                        if s:
                            ins.then_inc(opnd_ready, kg)
                        else:
                            ch.did(ins)
                    next_unit()
                for unit in rest:
                    mod_column(unit)
                low_next(0)
                vec.wait_ge(mod_done, 1 + MOD_POOL)
                coefficients(0, (1,))
                for m in range(KD):
                    if not low_at["mix0"][m][0]:
                        low_operand(opnd["mix0"], m)

            def ffn_in(l):
                s = lin[f"ffn_in{l}"]
                more = l + 1 < DEPTH
                p0 = l * PAIRS

                def at(v, i):
                    return v if i is None else i * 4 + v

                def group(i, first=False, base=0):
                    for j in range(4):
                        c = s.conv0 + base + j
                        pair = p0 + (base + j) // 2
                        half = (lambda v: v) if i is None else (lambda v: i * 2 + v)
                        if i is not None or base + j + 1 < FFN_TILES:
                            low_part(s, base + j + 1, i, 4)
                        else:
                            low_next(s.n0 + base + j + 1)
                        b = tile_bank[(s.t0 + base + j) % BANKS]
                        k = bass.ds(at(base + j, i), 1)
                        tap = [taps[:, l, k, q:q + 1].rearrange("p a b -> p (a b)") for q in (0, 2)]
                        vec.wait_ge(acc_ready, at(c + 1, i))
                        vec.scalar_tensor_tensor(out=acc[:, c % 4, 1:COLS], in0=b[:, 0:COLS - 1], scalar=tap[0],
                                                 in1=acc[:, c % 4, 1:COLS], op0=ALU.mult, op1=ALU.add).then_inc(tap_first, 1)
                        if j % 2 == 0 and not (first and j == 0):
                            vec.wait_ge(g_hi_ready, half(pair))
                            q = bass.ds(half(pair - p0 - 1), 1)
                            vec.tensor_tensor(g_lo[:, q, :].rearrange("p a n -> p (a n)"), gate[:, (pair - 1) % 2, :],
                                              g_hi[:, q, :].bitcast(F32).rearrange("p a n -> p (a n)"),
                                              ALU.subtract).then_inc(g_lo_ready, 1)
                        vec.wait_ge(tap_first, at(c + 1, i))
                        vec.scalar_tensor_tensor(out=acc[:, c % 4, 0:COLS - 1], in0=b[:, 1:COLS], scalar=tap[1],
                                                 in1=acc[:, c % 4, 0:COLS - 1], op0=ALU.mult, op1=ALU.add
                                                 ).then_inc(conv_done, 1)
                        if j % 2:
                            vec.wait_ge(sil_ready, half(pair + 1))
                            vec.wait_ge(conv_done, at(4 + c + 1, i))
                            vec.tensor_tensor(gate[:, pair % 2, :], sil[:, pair % 2, :], acc[:, c % 4, :],
                                              ALU.mult).then_inc(gate_ready, 1)
                            if more and j == 3:
                                mod_column(MOD_DURING[l] + base // 4, i)

                group(None, first=True)
                with vec.Fori(0, FFN_TILES // 4 - 2) as i:
                    group(i, base=4)
                group(None, base=FFN_TILES - 4)
                vec.wait_ge(g_hi_ready, p0 + PAIRS)
                vec.tensor_tensor(g_lo[:, PAIRS - 1, :], gate[:, (p0 + PAIRS - 1) % 2, :],
                                  g_hi[:, PAIRS - 1, :].bitcast(F32), ALU.subtract).then_inc(g_lo_ready, 1)
            def ssd_conv():
                s = lin["ssd_conv"]

                def tile(base, j, i):
                    at = (lambda v: v) if i is None else (lambda v: i * 4 + v)
                    t, c = base + j, s.conv0 + base + j
                    if i is not None or t + 1 < s.chunks:
                        low_part(s, t + 1, i, 4)
                    else:
                        low_next(s.n0 + t + 1)
                    b = tile_bank[(s.t0 + t) % BANKS]
                    k = bass.ds(at(t), 1)
                    tap = [ssd_taps[:, k, q:q + 1].rearrange("p a b -> p (a b)") for q in (0, 2)]
                    left = xbc[:, k, 1:COLS].rearrange("p a n -> p (a n)")
                    right = xbc[:, k, 0:COLS - 1].rearrange("p a n -> p (a n)")
                    vec.wait_ge(acc_ready, at(c + 1))
                    vec.scalar_tensor_tensor(out=left, in0=b[:, 0:COLS - 1], scalar=tap[0], in1=left,
                                             op0=ALU.mult, op1=ALU.add).then_inc(tap_first, 1)
                    vec.wait_ge(tap_first, at(c + 1))
                    vec.scalar_tensor_tensor(out=right, in0=b[:, 1:COLS], scalar=tap[1], in1=right,
                                             op0=ALU.mult, op1=ALU.add).then_inc(conv_done, 1)

                for j in range(4):
                    tile(0, j, None)
                with vec.Fori(0, s.chunks // 4 - 2) as i:
                    for j in range(4):
                        tile(4, j, i)
                for j in range(4):
                    tile(s.chunks - 4, j, None)
                z, dt = lin["ssd_z"], lin["ssd_dt"]
                low_next(z.n0 + 1)
                mod_column(MOD_BEHIND[0] + 1)
                for j in range(1, z.chunks):
                    low_next(z.n0 + j + 1)
                low_next(dt.n0 + 1)
                mod_column(MOD_BEHIND[0] + 2)
                vec.wait_ge(mod_done, 1 + 2 * MOD_UNITS)
                coefficients(1, (2, 3))

            def dt_prepare():
                n = [0]

                def link(ins):
                    n[0] += 1
                    ins.then_inc(z_dt, 1)
                    vec.wait_ge(z_dt, n[0])

                v, mag, e, r = (sq[:, j, 0:192] for j in (1, 2, 3, 0))
                q = sq[:, 1, 192:384]
                v3 = v.rearrange("p (c h) -> p c h", c=3)
                vec.wait_ge(dt_pe, 1)
                link(vec.tensor_tensor(v3, stat_bank[:, 0:192].rearrange("p (c h) -> p c h", c=3),
                                       dt_rows[:, 0, :].unsqueeze(1).broadcast_to([P, 3, NDT]), ALU.add))
                link(vec.tensor_scalar(mag, v, -1.0, None, ALU.mult))
                link(vec.tensor_tensor(mag, mag, v, ALU.max))
                vec.wait_ge(dt_act, 2)
                link(vec.tensor_scalar(r, e, 2.0, None, ALU.add))
                link(vec.reciprocal(r, r))
                link(vec.tensor_tensor(r, r, e, ALU.mult))
                link(vec.tensor_tensor(mag, r, r, ALU.mult))
                link(vec.tensor_scalar(q, mag, 1.0 / 15, None, ALU.mult))
                for k in (13, 11, 9, 7, 5, 3):
                    link(vec.scalar_tensor_tensor(out=q, in0=q, scalar=1.0 / k, in1=mag, op0=ALU.add, op1=ALU.mult))
                link(vec.scalar_tensor_tensor(out=q, in0=q, scalar=1.0, in1=r, op0=ALU.add, op1=ALU.mult))
                link(vec.tensor_scalar(v, v, 0.0, None, ALU.max))
                flat_dt = dtv[:, :, :].rearrange("p c h -> p (c h)")
                link(vec.scalar_tensor_tensor(out=flat_dt, in0=q, scalar=2.0, in1=v, op0=ALU.mult, op1=ALU.add))
                link(vec.scalar_tensor_tensor(out=adt[:, :, :], in0=sq[:, 3, 192:256].unsqueeze(1).broadcast_to([P, 3, NDT]),
                                              scalar=-1.0, in1=dtv[:, :, :], op0=ALU.mult, op1=ALU.mult))
                assert n[0] == DT_DVE - 2
                vec.wait_ge(dt_pe, 2)
                cum = rstd_bank[:, 0:192].rearrange("p (c h) -> p c h", c=3)
                total = rstd_bank[:, 192:384].rearrange("p (c h) -> p c h", c=3)
                ch.did(vec.tensor_scalar(neg_cum[:, :, :], cum, -1.0, None, ALU.mult))
                ch.did(vec.tensor_copy(full_decay[:, :, :], total))
                ch.did(vec.tensor_copy(back_cum[:, :, :], cum[:, :, SSD_HEADS:]))
                ch.wait()
                link(vec.tensor_tensor(to_end[:, :, :], full_decay[:, :, :], neg_cum[:, :, :], ALU.add))
                vec.wait_ge(dt_act, 4)
                link(vec.tensor_tensor(to_end[:, :, :], to_end[:, :, :], dtv[:, :, :], ALU.mult))
                assert n[0] == DT_DVE

            def scan_dve():
                skip = ssd_cols[:, 0, :]
                ch.did(vec.tensor_tensor(skip, skip, ssd_cols[:, 1, :], ALU.add))
                ch.wait()

                def output(g, c, u):
                    vec.wait_ge(s_y, u + 1)
                    c0 = CHUNKS[c][0]
                    for t in range(2):
                        k = 2 * g + t
                        ins = vec.scalar_tensor_tensor(
                            out=xbc[:, k, c0:c0 + P], in0=xbc[:, k, c0:c0 + P], scalar=skip[:, k:k + 1],
                            in1=(mod_bank, col_bank)[u % 2][:, t * P:(t + 1) * P], op0=ALU.mult, op1=ALU.add)
                        if t:
                            ins.then_inc(s_out, 1)
                        else:
                            ch.did(ins)

                def take_state(g, c, u):
                    vec.wait_ge(s_state, u + 1)
                    if c == 0:
                        if g:
                            vec.wait_ge(state_stored, 16 * g)
                        vec.tensor_copy(state_new, stat_bank[:, :].rearrange("p (d n) -> p d n", d=2)).then_inc(s_taken, 1)
                        return
                    d = c - 1
                    h0 = d * SSD_HEADS + g * HPG
                    if c == 1:
                        vec.wait_ge(state_loaded[g % 2], 16 * (g // 2 + 1))
                    if g:
                        vec.wait_ge(s_y, 3 * g)
                    n = ch.did(vec.tensor_tensor(
                        state1[:, d, :].rearrange("p (h q) -> p h q", h=HPG),
                        state0[:, g % 2, d, :].rearrange("p (h q) -> p h q", h=HPG),
                        full_decay[:, c, h0:h0 + HPG].unsqueeze(2).broadcast_to([P, HPG, HEAD]), ALU.mult))
                    ch.wait(n)
                    vec.tensor_tensor(state1[:, d, :], state1[:, d, :], stat_bank[:, d * GW:(d + 1) * GW],
                                      ALU.add).then_inc(s_taken, 1)

                for g, c, u, v in steps():
                    if u:
                        take_state(*ALL_STEPS[u - 1][:3])
                    vec.wait_ge(s_copied, u + 1)
                    if u:
                        vec.wait_ge(s_w, 2 * u)
                    for d in range(2):
                        ch.did(vec.tensor_tensor(cb_mask[:, d, :], turned[:, u % 2, P + GW:], tri[:, d, :], ALU.mult))
                    masks = ch.n
                    if u >= SCAN_SLOTS:
                        vec.wait_ge(s_y, u - SCAN_SLOTS + 1)
                    vec.wait_ge(s_cum, 2 * u + 1)
                    if c:
                        vec.wait_ge(s_cexp, 2 * v + 1)
                    for h in range(HPG):
                        col = g * HPG + h
                        ins = vec.tensor_scalar(decay[u % SCAN_SLOTS][:, 0, h * P:(h + 1) * P],
                                                tile_bank[2][:, h * P:(h + 1) * P],
                                                neg_cum[:, c, col:col + 1], 0.0, ALU.add, ALU.min)
                        if h == HPG - 1:
                            ins.then_inc(s_seg, 1)
                        else:
                            ch.did(ins)
                    ch.wait(masks)
                    for d in range(2):
                        vec.wait_ge(s_exp, 2 * u + d + 1)
                        w = decay[u % SCAN_SLOTS][:, d, :].rearrange("p (h i) -> p h i", h=HPG)
                        vec.tensor_tensor(w, w, cb_mask[:, d, :].unsqueeze(1).broadcast_to([P, HPG, P]),
                                          ALU.mult).then_inc(s_w, 1)
                    if u >= SCAN_LAG:
                        output(*ALL_STEPS[u - SCAN_LAG][:3])
                take_state(*ALL_STEPS[-1][:3])
                for step in ALL_STEPS[-SCAN_LAG:]:
                    output(*step[:3])

            def ssd_norm():
                vec.wait_ge(s_out, 3 * GROUPS)
                for m in range(KI):
                    vec.tensor_tensor(xbc[:, m, :], xbc[:, m, :], zt[:, m, :], ALU.mult).then_inc(yz_ready, 1)
                take_rstd("ssd")
                e, base, k = norm["ssd"]
                vec.wait_ge(rstd_spread, e + 1)
                vec.wait_ge(yz_ready, KI)
                o = opnd["ssd_y"]
                for m in range(KI + 2):
                    if m < KI:
                        vec.scalar_tensor_tensor(out=xbc[:, m, :], in0=xbc[:, m, :], scalar=ssd_cols[:, 2, m:m + 1],
                                                 in1=rstd_bank[:, 0:COLS], op0=ALU.mult, op1=ALU.mult
                                                 ).then_inc(opnd_ready, 1)
                    if m >= 2 and not low_at["ssd_y"][m - 2][0]:
                        vec.wait_ge(opnd_hi, o + m - 1)
                        vec.tensor_tensor(y_lo[:, m - 2, :], xbc[:, m - 2, :], y_hi[:, m - 2, :].bitcast(F32),
                                          ALU.subtract).then_inc(lo_dve, 1)

            def conf_mix():
                vec.wait_ge(late_loaded, 16)
                for group in CONV_GROUPS:
                    size = len(group)
                    for m in group:
                        vec.wait_ge(glu_ready, 1 + 2 * m + 2)
                        vec.tensor_scalar(convolved[:, m, :], glu[:, m, 0:CONVOLVED],
                                          conf_tab[:, m * TAPS31:m * TAPS31 + 1],
                                          conf_tab[:, C_DWB + m:C_DWB + m + 1], ALU.mult, ALU.add).then_inc(conf_tap, 1)
                    with vec.Fori(0, (TAPS31 - 1) // 3) as i:
                        for r in range(3):
                            for m in group:
                                vec.wait_ge(conf_tap, i * (3 * size) + (group[0] * TAPS31 + size * r + m - group[0] + 1))
                                vec.scalar_tensor_tensor(
                                    out=convolved[:, m, :], in0=glu[:, m, bass.ds(i * 3 + (1 + r), CONVOLVED)],
                                    scalar=conf_tab[:, bass.ds(i * 3 + (m * TAPS31 + 1 + r), 1)],
                                    in1=convolved[:, m, :], op0=ALU.mult, op1=ALU.add).then_inc(conf_tap, 1)
                vec.wait_ge(ln_sums, 1)
                vec.tensor_copy(ln_mean[:, :], stat_bank[:, 0:3]).then_inc(ln_mean_ready, 1)
                vec.wait_ge(ln_spread, 1)
                vec.wait_ge(conf_tap, CONV_DVE * TAPS31)
                vec.wait_ge(pe_conv, CONV_PE)
                for m in range(KD):
                    for c0, w, k in STREAMS:
                        ins = vec.tensor_tensor(work[:, m, c0:c0 + w], convolved[:, m, CONVOLVED_AT[k]:CONVOLVED_AT[k] + w],
                                                rstd_bank[:, c0:c0 + w], ALU.subtract)
                        if k:
                            ins.then_inc(ln_centred, 1)
                        else:
                            ch.did(ins)
                take_rstd("ln")
                vec.wait_ge(rstd_spread, norm["ln"][0] + 1)
                vec.wait_ge(ln_centred, KD)
                ch.wait()
                for m in range(KD):
                    vec.tensor_tensor(work[:, m, :], work[:, m, :], rstd_bank[:, 0:COLS], ALU.mult).then_inc(ln_scaled, 1)
                for m in range(KD):
                    low_operand(opnd["mid2"], m)

            def attn_mix():
                lows_of(lin["qkv"])
                vec.wait_ge(late_loaded, 48)
                vec.wait_ge(qk_std_ready, 1)
                vec.reciprocal(qk_rstd[:, :], qk_std[:, :]).then_inc(qk_rstd_ready, 1)

                def rotate(t):
                    vec.wait_ge(qk_rot, t + 1)
                    if t >= 2:
                        vec.wait_ge(qk_turned, t - 1)
                    vec.tensor_tensor(rot_sin[:, t % 2, :], tile_bank[t % 2][:, 0:LAT], attn_tab[:, A_SIN:A_SIN + LAT],
                                      ALU.mult).then_inc(qk_sin, 1)
                    to = q_turned[:, t, :] if t < AH else k_all[:, t - AH, PAST:]
                    vec.wait_ge(qk_cos, t + 1)
                    vec.wait_ge(qk_sin, t + 1)
                    vec.tensor_tensor(to, to, rot_sin[:, t % 2, :], ALU.add).then_inc(qk_turned, 1)

                for t in range(QK + 1):
                    if t < QK:
                        g = A_G + (t >= AH)
                        vec.wait_ge(qk_spread, t + 1)
                        vec.scalar_tensor_tensor(out=qkv[:, t, :], in0=qkv[:, t, :], scalar=attn_tab[:, g:g + 1],
                                                 in1=(rstd_bank, mod_bank)[t % 2][:, 0:COLS], op0=ALU.mult,
                                                 op1=ALU.mult).then_inc(qk_normed, 1)
                    if t:
                        rotate(t - 1)
                o = opnd["mid3"]
                for u in range(3 * AH + 1):
                    if u < 3 * AH:
                        w = P if u % 3 == 0 else PAST + LAT
                        vec.wait_ge(att_score, u + 1)
                        if u >= 2:
                            vec.wait_ge(att_max, u - 1)
                        vec.tensor_reduce(row_max[:, u % 2:u % 2 + 1], tile_bank[u % 2][:, 0:w], AX.X, ALU.max
                                          ).then_inc(att_rowmax, 1)
                        vec.wait_ge(att_rowmax, u + 1)
                        if u >= 2:
                            vec.wait_ge(att_exp, u - 1)
                        vec.tensor_scalar(neg_max[:, u % 2:u % 2 + 1], row_max[:, u % 2:u % 2 + 1], -SCALE, None,
                                          ALU.mult).then_inc(att_max, 1)
                    if u:
                        b = u - 1
                        w = P if b % 3 == 0 else PAST + LAT
                        vec.wait_ge(att_exp, b + 1)
                        if b >= 2:
                            vec.wait_ge(att_prob, b - 1)
                        vec.reciprocal(inv_sum[:, b % 2:b % 2 + 1], row_sum[:, b % 2:b % 2 + 1]).then_inc(att_inv, 1)
                        vec.wait_ge(att_inv, b + 1)
                        vec.tensor_scalar(prob[:, b % 2, 0:w], prob[:, b % 2, 0:w], inv_sum[:, b % 2:b % 2 + 1], None,
                                          ALU.mult).then_inc(att_prob, 1)
                for h in range(AH):
                    low_operand(o, h)

            def lows_of(s):
                for j in range(s.chunks):
                    low_next(s.n0 + j + 1)

            vec.memset(cond32[:, :, :], 0.0).then_inc(vec_init, 1)
            vec.memset(work[:, :, :], 0.0).then_inc(vec_init, 1)
            vec.memset(gapped[:, :, :], 0.0).then_inc(vec_init, 1)
            vec.memset(spare[:, 3:4], 0.0).then_inc(w_low_dve, RAW_SLOTS)
            vec.memset(spare[:, 0:1], 0.0).then_inc(conv_done, 4)
            vec.memset(spare[:, 1:2], 0.0).then_inc(mod_done, 1)
            vec.wait_ge(loaded0, LOADS0)
            vec.wait_ge(vec_init, 3)
            vec.wait_ge(consts, CONSTS)
            vec.memset(spare[:, 2:3], 0.0).then_inc(x_ready, KD)
            with vec.Fori(0, MOD_FIRST) as i:
                mod_column(0, i)
            vec.wait_ge(mod_done, 1 + MOD_FIRST)
            coefficients(0, (0,))
            take_rstd("pre0.0")
            modulate_gapped()
            pool_mix()
            for l in range(DEPTH):
                if l:
                    vec.wait_ge(mod_done, 1 + MOD_BEHIND[l - 1] + 1)
                    vec.wait_ge(x_ready, KD * (2 * l + 1))
                    coefficients(l, (0, 1) if l == 1 else (0, 1, 2, 3))
                if l == 0:
                    low_next(1)
                    low_next(2)
                    s = lin["pool"]
                if l == 1:
                    take_rstd("pre1.0")
                    modulate(1, "pre1.0", 0, KD * 2, "mix1")
                    ssd_conv()
                    dt_prepare()
                    scan_dve()
                    ssd_norm()
                    lows_of(lin["ssd_out"])
                if l == 2:
                    vec.memset(spare[:, 7:8], 0.0).then_inc(
                        w_low_dve, sum(lin[name].chunks for name in linears(2)))
                    take_rstd("pre2.0")
                    modulate(2, "pre2.0", 0, KD * 4, "mix2")
                    conf_mix()
                    low_next(lin["conf_out"].n0 + KD)
                if l == 3:
                    take_rstd("pre3.0")
                    modulate(3, "pre3.0", 0, KD * 6, "mix3")
                    attn_mix()
                    lows_of(lin["attn_out"])
                s = lin[linears(l)[-1]]
                take_rstd(f"post{l}.0")
                if l == 0:
                    residual("post0.0", 4 + s.evac0 + KD, lambda m: mod_column(MOD_POOL) if m == 4 else None)
                    for g in range(MOD_POOL + 1, MOD_GLUE):
                        mod_column(g)
                    vec.wait_ge(mod_done, 1 + MOD_GLUE)
                    coefficients(0, (2,))
                else:
                    residual(f"post{l}.0", 4 + s.evac0 + KD)
                take_rstd(f"pre{l}.1")
                modulate(l, f"pre{l}.1", 1, KD * (2 * l + 2) - KD, f"ffn{l}")
                ffn_in(l)
                if l == 0:
                    vec.wait_ge(mod_done, 1 + MOD_UNITS)
                    coefficients(0, (3,))
                    vec.memset(spare[:, 0:1], 0.0).then_inc(gate2_ready, 1)
                s = lin[f"ffn_out{l}"]
                lows_of(s)
                take_rstd(f"post{l}.1")
                residual(f"post{l}.1", 4 + s.evac0 + KD)
                if l + 1 < DEPTH:
                    mod_column(MOD_BEHIND[l])

        @block.tensor
        def _(ten):
            ch = Chain(ten, pe)

            def products(bank_ap, hi, lo, w_tile, n, first, last):
                w = (w_hi[:, n % SPLIT_SLOTS, w_tile * P:(w_tile + 1) * P],
                     w_lo[:, n % SPLIT_SLOTS, w_tile * P:(w_tile + 1) * P])
                ten.matmul(bank_ap, w[0], hi, start=first, stop=False)
                ten.matmul(bank_ap, w[0], lo, start=False, stop=False)
                return ten.matmul(bank_ap, w[1], hi, start=False, stop=last)

            def chunk_ready(n, i=None, per=0):
                ready = RAW_SLOTS + n + 1
                ten.wait_ge(w_low_pool, ready if i is None else i * per + ready)
                ten.wait_ge(w_low_dve, ready if i is None else i * per + ready)

            def mod_rows_of(g, i=None):
                half = g % 2
                ten.wait_ge(mod_loaded[half], 16 * (g // 2 + 1) + (0 if i is None else i * 16))
                if half == 0:
                    ten.wait_ge(mod_done, (0 if i is None else i) + (g // 2 + 1))
                for k in range(HALF_K):
                    w = mod_raw[:, half, k * MOD_COLS:(k + 1) * MOD_COLS].rearrange("p (t q c) -> p t q c", q=4, c=32)
                    for q in range(4):
                        ins = ten.matmul(mod_bank[32 * q:32 * q + 32, 0:MOD_TILES * 32],
                                         cond32[:, half * HALF_K + k, :], w[:, :, q, :], start=half == 0 and k == 0,
                                         stop=half == 1 and k == HALF_K - 1, skip_group_check=True)
                ins.then_inc(mod_used, 1)

            def column_sums(name, col=0):
                _, base, _ = norm[name]
                for t, size, adds in sum_groups[name][0]:
                    if size > 1:
                        ten.wait_ge(sq_added, adds)
                    else:
                        ten.wait_ge(sq_ready, base + t + 1)
                    for c, (c0, s) in enumerate(CHUNKS):
                        ins = ten.matmul(stat_bank[:, c:c + 1], sq[:, (base + t) % 4, c0:c0 + P], mean_col[:, col:col + 1],
                                         start=t == sum_groups[name][0][0][0] and c == 0, stop=True,
                                         skip_group_check=True)
                    ins.then_inc(sq_used, 1)

            def spread_columns(b, src, at):
                for c, (c0, s) in enumerate(CHUNKS):
                    w = P if c == 1 else P + 1
                    ins = ten.matmul(b[:, c0:c0 + w], src[:, at + c:at + c + 1].broadcast_to([P, P]), ident[:, 0:w],
                                     start=c == 0, stop=True, skip_group_check=True)
                return ins

            def spread(name):
                e, base, k = norm[name]
                ten.wait_ge(rstd_ready, e + 1)
                spread_columns(rstd_bank, rstd, 0).then_inc(rstd_spread, 1)

            def norm_of(name, col=0):
                column_sums(name, col)
                spread(name)

            def ffn_in(l):
                s = lin[f"ffn_in{l}"]
                more = l + 1 < DEPTH
                with ten.Fori(0, FFN_TILES // 4) as i:
                    for j in range(4):
                        chunk_ready(s.n0 + j, i, 4)
                        ten.wait_ge(conv_done, i * 4 + (s.conv0 + j + 1))
                        b = tile_bank[(s.t0 + j) % BANKS][:, 0:COLS]
                        for k in range(KD):
                            if j == 0:
                                low_ready(ten, f"ffn{l}", k)
                            ins = products(b, h_hi[:, k, :], h_lo[:, k, :], k, s.n0 + j, k == 0, k == KD - 1)
                        ins.then_inc(w_used, 1)
                        if more and j % 2 == 0:
                            mod_rows_of(2 * MOD_DURING[l] + j // 2, i)

            def out_product(s, hi, lo, name, before, g_ready):
                with ten.Fori(0, 2) as i:
                    for m in range(4):
                        before(m)
                        ten.wait_ge(evac, i * 4 + (s.evac0 + m + 1))
                        b = tile_bank[(s.t0 + m) % BANKS][:, 0:COLS]
                        for half in range(s.per):
                            n = s.n0 + s.per * m + half
                            chunk_ready(n, i, 4 * s.per)
                            for k in range(s.tiles):
                                kk = half * s.tiles + k
                                if m == 0:
                                    g_ready(kk)
                                ins = products(b, hi[:, kk, :], lo[:, kk, :], k, n, kk == 0, kk == s.per * s.tiles - 1)
                            ins.then_inc(w_used, 1)
                norm_of(name)

            def plain_product(s, name, before):
                def tile(j, i=None):
                    chunk_ready(s.n0 + j, i, 4)
                    before(j, i)
                    b = tile_bank[(s.t0 + j) % BANKS][0:s.width, 0:COLS]
                    for k in range(KD):
                        if j == 0:
                            low_ready(ten, name, k)
                        w = s.width
                        wh = w_hi[:, (s.n0 + j) % SPLIT_SLOTS, k * w:(k + 1) * w]
                        wl = w_lo[:, (s.n0 + j) % SPLIT_SLOTS, k * w:(k + 1) * w]
                        ten.matmul(b, wh, h_hi[:, k, :], start=k == 0, stop=False)
                        ten.matmul(b, wh, h_lo[:, k, :], start=False, stop=False)
                        ins = ten.matmul(b, wl, h_hi[:, k, :], start=False, stop=k == KD - 1)
                    ins.then_inc(w_used, 1)

                if s.chunks >= 8:
                    with ten.Fori(0, s.chunks // 4) as i:
                        for j in range(4):
                            tile(j, i)
                else:
                    for j in range(s.chunks):
                        tile(j)

            def dt_prepare():
                s = lin["ssd_dt"]
                ten.wait_ge(evac, 4 + s.evac0 + 1)
                for c, (c0, _) in enumerate(CHUNKS):
                    ins = ten.transpose(stat_bank[:, c * NDT:(c + 1) * NDT], sq[0:NDT, 0, c0:c0 + P],
                                        ident[0:NDT, 0:NDT])
                ins.then_inc(dt_pe, 1)
                ten.wait_ge(z_dt, DT_DVE - 2)
                cum = rstd_bank[:, 0:192].rearrange("p (c h) -> p c h", c=3)
                for d in range(2):
                    hs = slice(d * SSD_HEADS, (d + 1) * SSD_HEADS)
                    ten.matmul(cum[:, :, hs], tri[:, d, :], adt[:, :, hs], start=True, stop=True, skip_group_check=True)
                ten.matmul(rstd_bank[:, 192:384], ones[:, :], adt[:, :, :].rearrange("p c h -> p (c h)"),
                           start=True, stop=True, skip_group_check=True).then_inc(dt_pe, 1)

            def scan_pe():
                def output(g, c, u, v):
                    if u >= 2:
                        ten.wait_ge(s_out, u - 1)
                    ten.wait_ge(s_w, 2 * u + 2)
                    ten.wait_ge(s_xdt, 2 * u + 2)
                    if c:
                        ten.wait_ge(s_cs, 2 * v + 2)
                        ten.wait_ge(s_taken, 3 * g + 3)
                        ten.wait_ge(state_loaded[g % 2], 16 * (g // 2 + 1))
                    b = (mod_bank, col_bank)[u % 2]
                    for h in range(HPG):
                        o = b[HEAD * (h % 2):HEAD * (h % 2 + 1), h // 2 * P:(h // 2 + 1) * P]
                        hs, ws = slice(h * HEAD, (h + 1) * HEAD), slice(h * P, (h + 1) * P)
                        terms = [(x_dt[u % SCAN_SLOTS][:, d, hs], decay[u % SCAN_SLOTS][:, d, ws]) for d in range(2)]
                        if c:
                            for d in range(2):
                                st = state0[:, g % 2, d, hs] if d == c - 1 else state1[:, d, hs]
                                terms.append((st, c_scaled[v % 2][:, d, ws]))
                        for n, (lhs, rhs) in enumerate(terms):
                            ins = ten.matmul(o, lhs, rhs, start=n == 0, stop=n == len(terms) - 1)
                    ins.then_inc(s_y, 1)

                def states(c, u):
                    ten.wait_ge(s_copied, u + 1)
                    ten.wait_ge(s_xend, u + 1)
                    if u:
                        ten.wait_ge(s_taken, u)
                    for d in state_dirs(c):
                        ins = ten.matmul(stat_bank[:, d * GW:(d + 1) * GW], turned[:, u % 2, 0:P], x_end[:, d, :],
                                         start=True, stop=True, skip_group_check=True)
                    ins.then_inc(s_state, 1)

                ten.wait_ge(xbc_ready, SSD_CONV_TILES)
                ten.wait_ge(z_dt, DT_DVE)
                for g, c, u, v in steps():
                    c0 = CHUNKS[c][0]
                    if u >= 2:
                        ten.wait_ge(s_copied, u - 1)
                    b = tile_bank[u % 2]
                    cols = slice(c0, c0 + P)
                    ten.transpose(b[:, 0:P], xbc[:, KI + g, cols], ident[:, 0:P])
                    for t in range(2):
                        ten.transpose(b[:, (t + 1) * P:(t + 2) * P], xbc[:, 2 * g + t, cols], ident[:, 0:P])
                    ten.matmul(b[:, 3 * P:], xbc[:, KI + g, cols], xbc[:, KI + GROUPS + g, cols],
                               start=True, stop=True).then_inc(s_turned, 1)
                    if u:
                        states((u - 1) % 3, u - 1)
                    for d in range(2):
                        if u:
                            ten.wait_ge((s_seg, s_seg_back)[d], u)
                        for h in range(HPG):
                            col = d * SSD_HEADS + g * HPG + h
                            ins = ten.matmul(tile_bank[2 + d][:, h * P:(h + 1) * P],
                                             adt[:, c, col:col + 1].broadcast_to([P, P]), tri[:, d, :],
                                             start=True, stop=True, skip_group_check=True)
                        ins.then_inc(s_cum, 1)
                    if u >= SCAN_LAG:
                        output(*ALL_STEPS[u - SCAN_LAG])
                states(2, 3 * GROUPS - 1)
                for step in ALL_STEPS[-SCAN_LAG:]:
                    output(*step)

            def conf_norm_pe():
                for tile in range(CONV_PE):
                    ten.wait_ge(glu_lo_ready, tile + 1)
                    if tile >= 2:
                        ten.wait_ge(pe_conv, tile - 1)
                    b = (mod_bank, col_bank)[tile % 2][:, 0:CONVOLVED]
                    for k in range(TAPS31):
                        ten.wait_ge(diag_ready, tile * TAPS31 + k + 1)
                        first, last = k == 0, k == TAPS31 - 1
                        hi, lo = glu_hi[:, tile, k:k + CONVOLVED], glu_lo[:, tile, k:k + CONVOLVED]
                        ten.matmul(b, diagonal[:, k, 0, :], hi, start=first, stop=False)
                        ten.matmul(b, diagonal[:, k, 0, :], lo, start=False, stop=False)
                        ten.matmul(b, diagonal[:, k, 1, :], hi, start=False, stop=last).then_inc(pe_tap, 1)
                for m in range(KD):
                    if m >= CONV_DVE:
                        ten.wait_ge(pe_conv, m - CONV_DVE + 1)
                    else:
                        ten.wait_ge(conf_tap, TAPS31 * max(g[-1] + 1 for g in CONV_GROUPS if m in g))
                    for c, (c0, s) in enumerate(CHUNKS):
                        at = c0 - (LAT0 if s else 0) + CONVOLVED_AT[s]
                        ins = ten.matmul(stat_bank[:, c:c + 1], convolved[:, m, at:at + P], mean_col[:, 0:1],
                                         start=m == 0 and c == 0, stop=True, skip_group_check=True)
                ins.then_inc(ln_sums, 1)
                ten.wait_ge(ln_mean_ready, 1)
                spread_columns(rstd_bank, ln_mean, 0).then_inc(ln_spread, 1)
                norm_of("ln")

            def attn_pe():
                s = lin["qkv"]
                ten.wait_ge(evac, 4 + s.evac0 + s.chunks)
                e, base, _ = norm["qk"]
                for kv in range(AKV):
                    for c, (c0, _) in enumerate(CHUNKS):
                        ins = ten.transpose(tile_bank[2 + kv][:, c * AD:(c + 1) * AD], qkv[:, QK + kv, c0:c0 + P],
                                            ident[:, 0:P])
                    ins.then_inc(v_turned, 1)
                for t in range(QK):
                    ten.wait_ge(sq_ready, base + t + 1)
                    for c, (c0, _) in enumerate(CHUNKS):
                        ins = ten.matmul(stat_bank[:, 3 * t + c:3 * t + c + 1], sq[:, (base + t) % 4, c0:c0 + P],
                                         mean_col[:, 2:3], start=True, stop=True, skip_group_check=True)
                    ins.then_inc(sq_used, 1)
                ten.wait_ge(qk_rstd_ready, 1)
                ten.wait_ge(late_loaded, 48)
                for t in range(QK + 1):
                    if t < QK:
                        if t >= 2:
                            ten.wait_ge(qk_normed, t - 1)
                        spread_columns((rstd_bank, mod_bank)[t % 2], qk_rstd, 3 * t).then_inc(qk_spread, 1)
                    if t:
                        r = t - 1
                        ten.wait_ge(qk_normed, r + 1)
                        if r >= 2:
                            ten.wait_ge(qk_sin, r - 1)
                        ten.matmul(tile_bank[r % 2][:, 0:LAT], attn_tab[:, A_PERM:A_PERM + AD],
                                   qkv[:, r, LAT0:LAT0 + LAT], start=True, stop=True).then_inc(qk_rot, 1)
                ten.wait_ge(qk_turned, QK)
                ten.wait_ge(v_copied, AKV)

                def scores(h, c, u):
                    if u >= 2:
                        ten.wait_ge(att_exp, u - 1)
                    kv = h // REP
                    q = q_turned[:, h, (c - 1) * P:c * P] if c else qkv[:, h, 0:CTX]
                    keys = k_all[:, kv, :] if c else qkv[:, AH + kv, 0:CTX]
                    ten.matmul(tile_bank[u % 2][:, 0:PAST + LAT if c else CTX], q, keys, start=True, stop=True
                               ).then_inc(att_score, 1)

                def turn(h, c, u):
                    ten.wait_ge(att_prob, u + 1)
                    if u >= 2:
                        ten.wait_ge(att_pt, u - 1)
                    for k in range(3 if c else 1):
                        ins = ten.transpose(tile_bank[2 + u % 2][:, k * P:(k + 1) * P], prob[:, u % 2, k * P:(k + 1) * P],
                                            ident[:, 0:P])
                    ins.then_inc(att_turned, 1)

                def values(h, c, u):
                    ten.wait_ge(att_pt, u + 1)
                    if u >= 2:
                        copied_out(ten, u - 2)
                    kv = h // REP
                    own = v_rows[:, kv, :]
                    if c:
                        v = [attn_tab[:, A_V + kv * AD:A_V + (kv + 1) * AD], own[:, AD:2 * AD], own[:, 2 * AD:]]
                    else:
                        v = [own[:, 0:AD]]
                    for k, rows in enumerate(v):
                        ins = ten.matmul((mod_bank, col_bank)[u % 2][:, 0:P], rows, prob_t[:, u % 2, k * P:(k + 1) * P],
                                         start=k == 0, stop=k == len(v) - 1)
                    ins.then_inc(att_pv, 1)

                every = list(units())
                for n in range(len(every) + 3):
                    if n < len(every):
                        scores(*every[n])
                    if 2 <= n < len(every) + 2:
                        turn(*every[n - 2])
                    if n >= 3:
                        values(*every[n - 3])

            ten.wait_ge(cond_ready, 1)
            ten.wait_ge(consts, CONSTS)
            with ten.Fori(0, MOD_FIRST) as i:
                for j in range(2):
                    mod_rows_of(j, i)
            norm_of("pre0.0")
            with ten.Fori(0, MOD_POOL - MOD_FIRST) as i:
                for j in range(2):
                    mod_rows_of(2 * MOD_FIRST + j, i)
            for l in range(DEPTH):
                if l == 0:
                    s = lin["pool"]
                    for m in range(KD):
                        n = s.n0 + m // 4
                        chunk_ready(n)
                        group = m // 2
                        if m >= 4:
                            ten.wait_ge(evac, 1 + m)
                        low_ready(ten, "mix0", 2 * group)
                        low_ready(ten, "mix0", 2 * group + 1)
                        for k in range(2):
                            ins = products(tile_bank[(s.t0 + m) % BANKS][:, 0:COLS], h_hi[:, 2 * group + k, :],
                                           h_lo[:, 2 * group + k, :], (m % 4) * 2 + k, n, k == 0, k == 1)
                        if m % 4 == 3:
                            ins.then_inc(w_used, 1)
                        if m % 4 != 3:
                            ch.did(ins)
                    norm_of("post0.0")
                    for g in range(2 * MOD_POOL, 2 * MOD_GLUE):
                        mod_rows_of(g)
                if l == 1:
                    conv, z, dt = lin["ssd_conv"], lin["ssd_z"], lin["ssd_dt"]
                    plain_product(conv, "mix1", lambda j, i: ten.wait_ge(conv_done, i * 4 + (conv.conv0 + j + 1)))

                    def z_before(j, i):
                        ten.wait_ge(conv_done, conv.conv0 + SSD_CONV_TILES + j + 1)
                        ten.wait_ge(evac, i * 4 + (z.evac0 + j + 1))

                    for j in range(2):
                        mod_rows_of(2 * (MOD_BEHIND[0] + 1) + j)
                    plain_product(z, "mix1", z_before)
                    for j in range(2):
                        mod_rows_of(2 * (MOD_BEHIND[0] + 2) + j)
                    plain_product(dt, "mix1", lambda j, i: ten.wait_ge(evac, dt.evac0 + 1))
                    dt_prepare()
                    scan_pe()
                    norm_of("ssd", 1)
                    out_product(lin["ssd_out"], y_hi, y_lo, "post1.0", lambda m: None,
                                lambda k: low_ready(ten, "ssd_y", k))
                if l == 2:
                    s = lin["conf_in"]
                    plain_product(s, "mix2", lambda j, i, s=s: ten.wait_ge(evac, i * 4 + (s.evac0 + j + 1)))
                    conf_norm_pe()
                    out_product(lin["conf_out"], h_hi, h_lo, "post2.0", lambda m: None,
                                lambda k: low_ready(ten, "mid2", k))
                if l == 3:
                    s = lin["qkv"]
                    plain_product(s, "mix3", lambda j, i, s=s: ten.wait_ge(evac, i * 4 + (s.evac0 + j + 1)))
                    attn_pe()
                    out_product(lin["attn_out"], h_hi, h_lo, "post3.0", lambda m: None,
                                lambda k: low_ready(ten, "mid3", k))
                norm_of(f"pre{l}.1")
                ffn_in(l)
                s = lin[f"ffn_in{l}"]
                out_product(lin[f"ffn_out{l}"], g_hi, g_lo, f"post{l}.1",
                            lambda m, s=s: ten.wait_ge(conv_done, s.conv0 + FFN_TILES + m + 1),
                            lambda k, l=l: ten.wait_ge(g_lo_ready, l * PAIRS + k + 1))
                if l + 1 < DEPTH:
                    for j in range(2):
                        mod_rows_of(2 * MOD_BEHIND[l] + j)
                    norm_of(f"pre{l + 1}.0")


def columns(ctx_part, lat_part):
    out = np.zeros((P, KD, COLS), ctx_part.dtype)
    out[:, :, 0:CTX] = ctx_part.T.reshape(KD, P, CTX).transpose(1, 0, 2)
    out[:, :, LAT0:LAT0 + LAT] = lat_part.T.reshape(KD, P, LAT).transpose(1, 0, 2)
    return out


def tiles_of(w):
    k, m = w.shape
    return np.ascontiguousarray(w.reshape(k // P, P, m // P, P).transpose(2, 1, 0, 3)).reshape(m // P, P, k)


def per_partition(v, axis=-1):
    t = v.reshape(*v.shape[:-1], v.shape[-1] // P, P)
    return np.ascontiguousarray(np.moveaxis(t, -1, 0))


PAIRED = [t for p in range(PAIRS) for t in (p, PAIRS + p)]


def lay_out(i):
    d = {}
    d["x"] = columns(i["x_prompt"][0], i["x_sample"][0])
    d["cond"] = np.ascontiguousarray(np.stack([per_partition(i["c_ctx"]), per_partition(i["c"][0])], -1))
    d["gains"] = per_partition(i["norm_g"])
    d["b_mod"] = per_partition(i["b_mod"])
    d["pool_scale"] = per_partition(i["pool_scale"][0])
    d["taps"] = np.ascontiguousarray(np.stack(
        [per_partition(v)[:, :, PAIRED] for v in (i["ffn_dw"][:, 0], i["ffn_dw"][:, 1], i["ffn_dw"][:, 2], i["ffn_dw_b"])], -1))
    inv = np.ones((len(WINDOWS), CTX + LAT), np.float32)
    for g, win in enumerate(WINDOWS):
        at = 0
        for n in (CTX, LAT):
            t = np.arange(n)
            inv[g, at:at + n] = 1.0 / (np.minimum(t + win - win // 2, n) - np.maximum(t - win // 2, 0))
            at += n
    d["inv_count"] = np.broadcast_to(inv, (P, len(WINDOWS), CTX + LAT)).copy()
    d["w_mod"] = np.ascontiguousarray(
        i["w_mod"].reshape(DEPTH, 2, HALF_K, P, MOD_UNITS, MOD_COLS).transpose(0, 4, 1, 3, 2, 5)
    ).reshape(DEPTH * MOD_PIECES, P, HALF_K * MOD_COLS)
    pw = i["pool_w"][0].reshape(2, 2, 2, P, 2, P)
    d["pool"] = np.ascontiguousarray(pw.transpose(0, 3, 1, 4, 2, 5)).reshape(2, P, D)
    w = i["ssd_w_in"][0]
    d["ssd_conv"] = tiles_of(w[:, INNER:INNER + SSD_CONV_TILES * P])
    d["ssd_z"] = tiles_of(w[:, 0:INNER])
    d["ssd_dt"] = np.ascontiguousarray(
        w[:, INNER + SSD_CONV_TILES * P:].reshape(KD, P, NDT).transpose(1, 0, 2)).reshape(1, P, KD * NDT)
    d["ssd_out"] = np.ascontiguousarray(
        tiles_of(i["ssd_w_out"][0]).reshape(KD, P, 2, D).transpose(0, 2, 1, 3)).reshape(2 * KD, P, D)
    d["ssd_taps"] = np.ascontiguousarray(np.stack([per_partition(v) for v in (*i["ssd_conv_w"][0], i["ssd_conv_b"][0])], -1))
    d["dt_rows"] = np.broadcast_to(np.stack([i["ssd_dt_bias"][0].reshape(-1), i["ssd_a_log"][0].reshape(-1)]), (P, 2, NDT)).copy()
    d["ssd_cols"] = np.ascontiguousarray(np.stack(
        [*(per_partition(np.repeat(v, HEAD)) for v in i["ssd_d"][0]), per_partition(i["ssd_norm_g"][0])], 1))
    d["state_in"] = np.ascontiguousarray(i["state_ssd"][0, 0].transpose(3, 0, 1, 2)).reshape(P, 2, INNER)
    halves = [t for p in range(KD) for t in (p, KD + p)]
    d["conf_in"] = tiles_of(i["conf_w_in"][0])[halves]
    d["conf_out"] = tiles_of(i["conf_w_out"][0])
    d["conf_tab"] = np.concatenate(
        [per_partition(i["conf_dw"][0]).transpose(0, 2, 1).reshape(P, C_BIN), per_partition(i["conf_b_in"][0])[:, halves],
         *(per_partition(i["conf_" + n][0]) for n in ("dw_b", "ln_g", "ln_b", "b_out"))], 1)
    d["qkv"] = tiles_of(i["attn_w_qkv"][0])
    d["attn_out"] = tiles_of(i["attn_w_o"][0])
    n_freq = AD // 4
    inv_freq = np.float32(ROPE_THETA) ** (-np.arange(n_freq, dtype=np.float32) / np.float32(n_freq))
    t = np.arange(LAT)
    place = np.stack([t // GRID_W, t % GRID_W]).astype(np.float32)
    angle = np.broadcast_to((inv_freq[None, :, None] * place[:, None, :])[:, None], (2, 2, n_freq, LAT)).reshape(AD, LAT)
    perm = np.zeros((2, 2, n_freq, 2, 2, n_freq), np.float32)
    for axis in range(2):
        for f in range(n_freq):
            perm[axis, 1, f, axis, 0, f] = -1.0
            perm[axis, 0, f, axis, 1, f] = 1.0
    d["attn_tab"] = np.concatenate(
        [np.cos(angle), np.sin(angle), perm.reshape(AD, AD), i["attn_q_g"].T, i["attn_k_g"].T,
         i["cache_v"][0, 0].reshape(PAST, AKV * AD)], 1)
    d["cache_k"] = np.ascontiguousarray(i["cache_k"][0, 0].transpose(2, 1, 0))
    for l in range(DEPTH):
        d[f"ffn_in{l}"] = tiles_of(i["ffn_w_in"][l])[PAIRED]
        w = tiles_of(i["ffn_w_out"][l]).reshape(KD, P, 2, HALF * P)
        d[f"ffn_out{l}"] = np.ascontiguousarray(w.transpose(0, 2, 1, 3)).reshape(2 * KD, P, HALF * P)
    return d


OUTS = {"y": [P, KD, COLS], "state": [P, 2, INNER], "cache_k": [P, AKV, CTX], "cache_v": [P, AKV, CTX]}


def kernel(**inputs):
    import concourse.bacc as bacc
    from concourse.bass_utils import run_bass_kernel_spmd

    d = lay_out({k: np.asarray(v) for k, v in inputs.items()})
    nc = bacc.Bacc("TRN2", target_bir_lowering=False, num_devices=1)
    a = {k: nc.dram_tensor("in_" + k, list(v.shape), F32, kind="ExternalInput").ap() for k, v in d.items()}
    o = {k: nc.dram_tensor("out_" + k, v, F32, kind="ExternalOutput").ap() for k, v in OUTS.items()}
    build_trunk(nc, a, o)
    r = run_bass_kernel_spmd(nc, [{"in_" + k: v for k, v in d.items()}], core_ids=[0]).results[0]
    y = np.asarray(r["out_y"])
    tokens = [np.ascontiguousarray(y[:, :, c0:c0 + w].transpose(2, 1, 0)).reshape(1, w, D) for c0, w, _ in STREAMS]
    state = np.ascontiguousarray(np.asarray(r["out_state"]).transpose(1, 2, 0)).reshape(1, 1, 2, SSD_HEADS, HEAD, STATE)
    caches = [np.ascontiguousarray(np.asarray(r["out_" + n]).transpose(2, 1, 0)).reshape(1, 1, CTX, AKV, AD)
              for n in ("cache_k", "cache_v")]
    return (*tokens, state, *caches)
```
